# Optimizing a Trainium2 kernel written in Bass

```python
import math
import jax
import jax.numpy as jnp
from jax import lax
import numpy as np

D_MODEL = 1024
BATCH = 1
SEQ = 256
DEPTH = 1

GRID_W = 64
CTX_LEN = 256

HEAD_DIM = 64
GLA_WIDTH = D_MODEL // 4
RWKV_WIDTH = D_MODEL // 4
SSD_WIDTH = D_MODEL - GLA_WIDTH - RWKV_WIDTH

GLA_HEADS = GLA_WIDTH // HEAD_DIM
GLA_DV = HEAD_DIM
GLA_DK = HEAD_DIM // 2
GLA_KEY_WIDTH = GLA_HEADS * GLA_DK
GLA_GATE_RANK = 16
GLA_GATE_TAU = 16.0
GLA_CHUNK = 16

RWKV_HEADS = RWKV_WIDTH // HEAD_DIM
RWKV_N = HEAD_DIM
RWKV_DECAY_RANK = 32
RWKV_A_RANK = 32
RWKV_GATE_RANK = 64
RWKV_DECAY_SCALE = 0.606531
RWKV_LN_EPS = 64e-5

SSD_HEADS = SSD_WIDTH // HEAD_DIM
SSD_P = HEAD_DIM
SSD_N = 128
SSD_GROUPS = 2
SSD_CONV = 4
SSD_CHUNK = 64

N_EXPERTS = 32
TOP_K = 4
D_FF = D_MODEL
SWIGLU_LIMIT = 7.0
SWIGLU_ALPHA = 1.702

NORM_EPS = 1e-6

GLA_COLS = 2 * GLA_KEY_WIDTH + 2 * GLA_WIDTH + 2 * GLA_GATE_RANK
RWKV_COLS = 3 * RWKV_WIDTH + 2 * RWKV_DECAY_RANK + RWKV_A_RANK + RWKV_GATE_RANK
SSD_XBC = SSD_WIDTH + 2 * SSD_GROUPS * SSD_N
SSD_COLS = SSD_WIDTH + SSD_XBC + 2 * SSD_HEADS
IN_COLS = GLA_COLS + RWKV_COLS + SSD_COLS

kernel_name = "hybrid_gla_rwkv7_ssd_moe_prefix_dit"

def _split(u, sizes):
    offsets = [int(o) for o in np.cumsum(sizes)[:-1]]
    return jnp.split(u, offsets, axis=-1)

def rmsnorm(x, g, eps=NORM_EPS):
    xf = x.astype(jnp.float32)
    y = xf * lax.rsqrt(jnp.mean(xf * xf, axis=-1, keepdims=True) + eps)
    return (y * g.astype(jnp.float32)).astype(x.dtype)

def modulate(h, shift, scale):
    return h * (1.0 + scale) + shift

def split_heads(t, n_heads):
    b, l, _ = t.shape
    return t.reshape(b, l, n_heads, -1).transpose(0, 2, 1, 3)

def merge_heads(t):
    b, h, l, d = t.shape
    return t.transpose(0, 2, 1, 3).reshape(b, l, h * d)

def _rows_view(u, grid_rows):
    if grid_rows is None:
        return u
    b, l, ch = u.shape
    return u.reshape(b * grid_rows, l // grid_rows, ch)

def centred_dwconv(u, w, bias, grid_rows):
    b, l, ch = u.shape
    rows = _rows_view(u, grid_rows)
    k = w.shape[0]
    pad_l = k // 2
    out = lax.conv_general_dilated(rows, w[:, None, :].astype(rows.dtype), window_strides=(1,),
                                   padding=[(pad_l, k - 1 - pad_l)],
                                   dimension_numbers=('NWC', 'WIO', 'NWC'), feature_group_count=ch)
    return out.reshape(b, l, ch) + bias

def centred_token_shift(u, mu, grid_rows):
    b, l, ch = u.shape
    rows = _rows_view(u, grid_rows)
    prev = jnp.pad(rows, ((0, 0), (1, 0), (0, 0)))[:, :-1]
    nxt = jnp.pad(rows, ((0, 0), (0, 1), (0, 0)))[:, 1:]
    out = rows + mu[0] * (prev - rows) + mu[1] * (nxt - rows)
    return out.reshape(b, l, ch)

def chunk_state_scan(chunk_decay, chunk_update, s0):
    def step(s, inp):
        d, upd = inp
        return d[..., None] * s + upd, s
    s_fin, starts = lax.scan(step, s0, (jnp.moveaxis(chunk_decay, 2, 0), jnp.moveaxis(chunk_update, 2, 0)))
    return jnp.moveaxis(starts, 0, 2), s_fin

def gla_chunked(q, k, v, g, s0):
    b_, h, l, dk = q.shape
    dv = v.shape[-1]
    c = GLA_CHUNK
    nc = l // c
    q = q.reshape(b_, h, nc, c, dk)
    k = k.reshape(b_, h, nc, c, dk)
    v = v.reshape(b_, h, nc, c, dv)
    cum = jnp.cumsum(g.reshape(b_, h, nc, c, dk).astype(jnp.float32), axis=3)
    causal = jnp.tril(jnp.ones((c, c), dtype=bool))[:, :, None]
    rel = jnp.exp(jnp.where(causal, cum[:, :, :, :, None, :] - cum[:, :, :, None, :, :], -jnp.inf))
    att = jnp.einsum('bhntd,bhnsd,bhntsd->bhnts', q, k, rel)
    o = jnp.einsum('bhnts,bhnsv->bhntv', att, v)
    last = cum[:, :, :, -1:, :]
    upd = jnp.einsum('bhnsd,bhnsv->bhndv', k * jnp.exp(last - cum), v)
    s_start, s_fin = chunk_state_scan(jnp.exp(last[:, :, :, 0, :]), upd, s0)
    o = o + jnp.einsum('bhntd,bhndv->bhntv', q * jnp.exp(cum), s_start)
    return o.reshape(b_, h, l, dv), s_fin

def ssd_chunked(xdt, a, bm, cm, s0):
    b_, h, l, p = xdt.shape
    c = SSD_CHUNK
    nc = l // c
    xdt = xdt.reshape(b_, h, nc, c, p)
    bm = bm.reshape(b_, h, nc, c, -1)
    cm = cm.reshape(b_, h, nc, c, -1)
    cum = jnp.cumsum(a.reshape(b_, h, nc, c).astype(jnp.float32), axis=-1)
    causal = jnp.tril(jnp.ones((c, c), dtype=bool))
    decay = jnp.exp(jnp.where(causal, cum[..., :, None] - cum[..., None, :], -jnp.inf))
    scores = jnp.einsum('bhctn,bhcsn->bhcts', cm, bm) * decay
    y = jnp.einsum('bhcts,bhcsp->bhctp', scores, xdt)
    last = cum[..., -1:]
    upd = jnp.einsum('bhcsn,bhcsp->bhcnp', bm * jnp.exp(last - cum)[..., None], xdt)
    s_start, s_fin = chunk_state_scan(jnp.exp(last), upd, s0)
    y = y + jnp.einsum('bhctn,bhcnp->bhctp', cm * jnp.exp(cum)[..., None], s_start)
    return y.reshape(b_, h, l, p), s_fin

def rwkv7_scan(r, w, k, v, kk, a, s0):
    def step(s, inp):
        r_t, w_t, k_t, v_t, kk_t, a_t = inp
        s_kk = jnp.einsum('bhvk,bhk->bhv', s, kk_t)
        s = (s * w_t[:, :, None, :] - s_kk[..., None] * (kk_t * a_t)[:, :, None, :]
             + v_t[..., None] * k_t[:, :, None, :])
        return s, jnp.einsum('bhvk,bhk->bhv', s, r_t)
    xs = tuple(jnp.moveaxis(t, 2, 0) for t in (r, w, k, v, kk, a))
    s_fin, o = lax.scan(step, s0, xs)
    return jnp.moveaxis(o, 0, 2), s_fin

def _flip_time(ts):
    return tuple(jnp.flip(t, axis=2) for t in ts)

def bidir_prefix_scan(scan_fn, s0, ctx_f, ctx_b, lat_f, lat_b):
    o_cf, s_cf = scan_fn(*ctx_f, s0)
    o_cb, s_cb = scan_fn(*_flip_time(ctx_b), s0)
    o_lf, _ = scan_fn(*lat_f, s_cf)
    o_lb, _ = scan_fn(*_flip_time(lat_b), s_cb)
    return o_cf + jnp.flip(o_cb, axis=2), o_lf + jnp.flip(o_lb, axis=2)

def mixer_inputs(h, p, grid_rows):
    b, l, _ = h.shape
    u = h @ p['w_in']
    u_gla, u_rw, u_ssd = _split(u, [GLA_COLS, RWKV_COLS, SSD_COLS])

    q, k, v, og, lg_f, lg_b = _split(u_gla, [GLA_KEY_WIDTH, GLA_KEY_WIDTH, GLA_WIDTH, GLA_WIDTH,
                                             GLA_GATE_RANK, GLA_GATE_RANK])

    def gla_log_decay(low, d):
        z = (low @ p['gla_gate_w'][d] + p['gla_gate_b'][d]).astype(jnp.float32)
        return split_heads(jax.nn.log_sigmoid(z) / GLA_GATE_TAU, GLA_HEADS)

    gla = dict(q=split_heads(q, GLA_HEADS) * (GLA_DK ** -0.5), k=split_heads(k, GLA_HEADS),
               v=split_heads(v, GLA_HEADS), g_f=gla_log_decay(lg_f, 0), g_b=gla_log_decay(lg_b, 1),
               gate=jax.nn.silu(og))

    u_rw = centred_token_shift(u_rw, p['rw_mu'], grid_rows)
    r, k, v, lw_f, lw_b, la, lgt = _split(u_rw, [RWKV_WIDTH, RWKV_WIDTH, RWKV_WIDTH, RWKV_DECAY_RANK,
                                               RWKV_DECAY_RANK, RWKV_A_RANK, RWKV_GATE_RANK])

    def rw_decay(low, d):
        z = p['rw_w0'][d] + jnp.tanh(low) @ p['rw_w2'][d]
        return split_heads(jnp.exp(-RWKV_DECAY_SCALE * jax.nn.sigmoid(z)), RWKV_HEADS)

    a = jax.nn.sigmoid(p['rw_a0'] + la @ p['rw_a2'])
    kk = split_heads(k * p['rw_kk'], RWKV_HEADS).astype(jnp.float32)
    kk = (kk * lax.rsqrt(jnp.sum(kk * kk, axis=-1, keepdims=True) + 1e-12)).astype(k.dtype)
    k = k * (1.0 + (a - 1.0) * p['rw_ka'])
    rwkv = dict(r=split_heads(r, RWKV_HEADS), k=split_heads(k, RWKV_HEADS), v=split_heads(v, RWKV_HEADS),
                kk=kk, a=split_heads(a, RWKV_HEADS), w_f=rw_decay(lw_f, 0), w_b=rw_decay(lw_b, 1),
                gate=jax.nn.sigmoid(lgt) @ p['rw_g2'])

    z, xbc, dt = _split(u_ssd, [SSD_WIDTH, SSD_XBC, 2 * SSD_HEADS])
    xbc = jax.nn.silu(centred_dwconv(xbc, p['ssd_conv_w'], p['ssd_conv_b'], grid_rows))
    xs, bm, cm = _split(xbc, [SSD_WIDTH, SSD_GROUPS * SSD_N, SSD_GROUPS * SSD_N])
    rep = SSD_HEADS // SSD_GROUPS
    bm = jnp.repeat(split_heads(bm, SSD_GROUPS), rep, axis=1)
    cm = jnp.repeat(split_heads(cm, SSD_GROUPS), rep, axis=1)
    xs = split_heads(xs, SSD_HEADS)
    dt = jax.nn.softplus((dt.reshape(b, l, 2, SSD_HEADS) + p['ssd_dt_bias']).astype(jnp.float32))
    a_neg = -jnp.exp(p['ssd_a_log'])
    dt_f = dt[:, :, 0].transpose(0, 2, 1)
    dt_b = dt[:, :, 1].transpose(0, 2, 1)
    ssd = dict(x=xs, xdt_f=xs * dt_f[..., None], a_f=dt_f * a_neg[0][:, None],
               xdt_b=xs * dt_b[..., None], a_b=dt_b * a_neg[1][:, None], b=bm, c=cm, z=z)
    return dict(gla=gla, rwkv=rwkv, ssd=ssd)

def _pick(f, names):
    return tuple(f[n] for n in names)

def token_mixers(fc, fl):
    b = fl['gla']['v'].shape[0]
    gc, gl = fc['gla'], fl['gla']
    nf, nb = ('q', 'k', 'v', 'g_f'), ('q', 'k', 'v', 'g_b')
    gla = bidir_prefix_scan(gla_chunked, jnp.zeros((b, GLA_HEADS, GLA_DK, GLA_DV), jnp.float32),
                            _pick(gc, nf), _pick(gc, nb), _pick(gl, nf), _pick(gl, nb))
    rc, rl = fc['rwkv'], fl['rwkv']
    nf, nb = ('r', 'w_f', 'k', 'v', 'kk', 'a'), ('r', 'w_b', 'k', 'v', 'kk', 'a')
    rwkv = bidir_prefix_scan(rwkv7_scan, jnp.zeros((b, RWKV_HEADS, RWKV_N, RWKV_N), jnp.float32),
                             _pick(rc, nf), _pick(rc, nb), _pick(rl, nf), _pick(rl, nb))
    sc, sl = fc['ssd'], fl['ssd']
    nf, nb = ('xdt_f', 'a_f', 'b', 'c'), ('xdt_b', 'a_b', 'b', 'c')
    ssd = bidir_prefix_scan(ssd_chunked, jnp.zeros((b, SSD_HEADS, SSD_N, SSD_P), jnp.float32),
                            _pick(sc, nf), _pick(sc, nb), _pick(sl, nf), _pick(sl, nb))
    return gla, rwkv, ssd

def mixer_output(f, o_gla, o_rw, y_ssd, p):
    g, r, s = f['gla'], f['rwkv'], f['ssd']
    o1 = merge_heads(rmsnorm(o_gla, p['gla_norm_g'][:, None, :])) * g['gate']
    of = o_rw.astype(jnp.float32)
    mean = jnp.mean(of, axis=-1, keepdims=True)
    var = jnp.mean(jnp.square(of - mean), axis=-1, keepdims=True)
    on = (of - mean) * lax.rsqrt(var + RWKV_LN_EPS) * p['rw_lnx_g'][:, None, :] + p['rw_lnx_b'][:, None, :]
    bonus = jnp.sum(r['r'] * r['k'] * p['rw_rk'][:, None, :], axis=-1, keepdims=True) * r['v']
    o2 = merge_heads(on + bonus) * r['gate']
    y = merge_heads(y_ssd + p['ssd_d'][:, None, None] * s['x']) * jax.nn.silu(s['z'])
    bb, l, _ = y.shape
    y = rmsnorm(y.reshape(bb, l, SSD_GROUPS, -1), p['ssd_norm_g'].reshape(SSD_GROUPS, -1)).reshape(bb, l, SSD_WIDTH)
    return jnp.concatenate([o1, o2, y], axis=-1) @ p['w_out']

def moe(h, p):
    shp = h.shape
    t = h.reshape(-1, shp[-1])
    logits = (t @ p['router_w'] + p['router_b']).astype(jnp.float32)
    top_v, top_i = lax.top_k(logits, TOP_K)
    probs = jax.nn.softmax(top_v, axis=-1)
    gates = jnp.einsum('nk,nke->ne', probs, jax.nn.one_hot(top_i, N_EXPERTS, dtype=probs.dtype)).astype(t.dtype)
    y = jnp.zeros_like(t)
    for e in range(N_EXPERTS):
        gu = t @ p['moe_w_gu'][e] + p['moe_b_gu'][e]
        glu, lin = jnp.split(gu, 2, axis=-1)
        glu = jnp.minimum(glu, SWIGLU_LIMIT)
        lin = jnp.clip(lin, -SWIGLU_LIMIT, SWIGLU_LIMIT)
        act = glu * jax.nn.sigmoid(SWIGLU_ALPHA * glu) * (lin + 1.0)
        y = y + gates[:, e:e + 1] * (act @ p['moe_w_down'][e] + p['moe_b_down'][e])
    return y.reshape(shp)

def setup_inputs(seed: int = 0) -> dict:
    key = jax.random.key(seed)
    keys = jax.random.split(key, 64)
    counter = [0]

    def nk():
        counter[0] += 1
        return keys[counter[0] - 1]

    def nrm(shape, scale):
        return jax.random.normal(nk(), shape, jnp.float32) * scale

    def gain(shape):
        return 1.0 + nrm(shape, 0.05)

    L = DEPTH
    D = D_MODEL
    dt = jnp.exp(jax.random.uniform(nk(), (L, 2, SSD_HEADS), jnp.float32, math.log(1e-3), math.log(1e-1)))
    return {
        'x': nrm((BATCH, SEQ, D), 1.0),
        'c': nrm((BATCH, D), 1.0),
        'ctx': nrm((BATCH, CTX_LEN, D), 1.0),
        'c_ctx': nrm((D,), 1.0),
        'w_ada': nrm((L, D, 6 * D), 0.5 * D ** -0.5),
        'b_ada': nrm((L, 6 * D), 0.02),
        'norm1_g': gain((L, D)),
        'norm2_g': gain((L, D)),
        'w_in': nrm((L, D, IN_COLS), D ** -0.5),
        'gla_gate_w': nrm((L, 2, GLA_GATE_RANK, GLA_KEY_WIDTH), GLA_GATE_RANK ** -0.5),
        'gla_gate_b': nrm((L, 2, GLA_KEY_WIDTH), 0.1),
        'gla_norm_g': gain((L, GLA_HEADS, GLA_DV)),
        'rw_mu': jax.random.uniform(nk(), (L, 2, RWKV_COLS), jnp.float32, 0.0, 0.45),
        'rw_w0': nrm((L, 2, RWKV_WIDTH), 1.0),
        'rw_w2': nrm((L, 2, RWKV_DECAY_RANK, RWKV_WIDTH), 0.1),
        'rw_a0': nrm((L, RWKV_WIDTH), 0.5),
        'rw_a2': nrm((L, RWKV_A_RANK, RWKV_WIDTH), 0.1),
        'rw_g2': nrm((L, RWKV_GATE_RANK, RWKV_WIDTH), RWKV_GATE_RANK ** -0.5),
        'rw_kk': gain((L, RWKV_WIDTH)),
        'rw_ka': gain((L, RWKV_WIDTH)),
        'rw_rk': nrm((L, RWKV_HEADS, RWKV_N), 0.5),
        'rw_lnx_g': gain((L, RWKV_HEADS, RWKV_N)),
        'rw_lnx_b': nrm((L, RWKV_HEADS, RWKV_N), 0.02),
        'ssd_conv_w': nrm((L, SSD_CONV, SSD_XBC), SSD_CONV ** -0.5),
        'ssd_conv_b': nrm((L, SSD_XBC), 0.02),
        'ssd_dt_bias': dt + jnp.log(-jnp.expm1(-dt)),
        'ssd_a_log': jnp.log(jax.random.uniform(nk(), (L, 2, SSD_HEADS), jnp.float32, 1.0, 16.0)),
        'ssd_d': gain((L, SSD_HEADS)),
        'ssd_norm_g': gain((L, SSD_WIDTH)),
        'w_out': nrm((L, D, D), D ** -0.5),
        'router_w': nrm((L, D, N_EXPERTS), D ** -0.5),
        'router_b': nrm((L, N_EXPERTS), 0.01),
        'moe_w_gu': nrm((L, N_EXPERTS, D, 2 * D_FF), D ** -0.5),
        'moe_b_gu': nrm((L, N_EXPERTS, 2 * D_FF), 0.01),
        'moe_w_down': nrm((L, N_EXPERTS, D_FF, D), D_FF ** -0.5),
        'moe_b_down': nrm((L, N_EXPERTS, D), 0.01),
        'final_norm_g': gain((D,)),
    }

def reference(x, c, ctx, c_ctx, w_ada, b_ada, norm1_g, norm2_g, w_in, gla_gate_w, gla_gate_b, gla_norm_g,
              rw_mu, rw_w0, rw_w2, rw_a0, rw_a2, rw_g2, rw_kk, rw_ka, rw_rk, rw_lnx_g, rw_lnx_b,
              ssd_conv_w, ssd_conv_b, ssd_dt_bias, ssd_a_log, ssd_d, ssd_norm_g, w_out,
              router_w, router_b, moe_w_gu, moe_b_gu, moe_w_down, moe_b_down, final_norm_g):
    grid_rows = x.shape[1] // GRID_W
    xl, xc = x, ctx
    for i in range(DEPTH):
        p = dict(w_in=w_in[i], gla_gate_w=gla_gate_w[i], gla_gate_b=gla_gate_b[i], gla_norm_g=gla_norm_g[i],
                 rw_mu=rw_mu[i], rw_w0=rw_w0[i], rw_w2=rw_w2[i], rw_a0=rw_a0[i], rw_a2=rw_a2[i],
                 rw_g2=rw_g2[i], rw_kk=rw_kk[i], rw_ka=rw_ka[i], rw_rk=rw_rk[i], rw_lnx_g=rw_lnx_g[i],
                 rw_lnx_b=rw_lnx_b[i], ssd_conv_w=ssd_conv_w[i], ssd_conv_b=ssd_conv_b[i],
                 ssd_dt_bias=ssd_dt_bias[i], ssd_a_log=ssd_a_log[i], ssd_d=ssd_d[i], ssd_norm_g=ssd_norm_g[i],
                 w_out=w_out[i], router_w=router_w[i], router_b=router_b[i], moe_w_gu=moe_w_gu[i],
                 moe_b_gu=moe_b_gu[i], moe_w_down=moe_w_down[i], moe_b_down=moe_b_down[i])
        mod_l = jnp.split((jax.nn.silu(c) @ w_ada[i] + b_ada[i])[:, None, :], 6, axis=-1)
        mod_c = jnp.split((jax.nn.silu(c_ctx) @ w_ada[i] + b_ada[i])[None, None, :], 6, axis=-1)

        hl = modulate(rmsnorm(xl, norm1_g[i]), mod_l[0], mod_l[1])
        hc = modulate(rmsnorm(xc, norm1_g[i]), mod_c[0], mod_c[1])
        fl = mixer_inputs(hl, p, grid_rows)
        fc = mixer_inputs(hc, p, None)
        (gla_c, gla_l), (rw_c, rw_l), (ssd_c, ssd_l) = token_mixers(fc, fl)
        xl = xl + mod_l[2] * mixer_output(fl, gla_l, rw_l, ssd_l, p)
        hl = modulate(rmsnorm(xl, norm2_g[i]), mod_l[3], mod_l[4])
        if i == DEPTH - 1:
            xl = xl + mod_l[5] * moe(hl, p)
        else:
            xc = xc + mod_c[2] * mixer_output(fc, gla_c, rw_c, ssd_c, p)
            hc = modulate(rmsnorm(xc, norm2_g[i]), mod_c[3], mod_c[4])
            y = moe(jnp.concatenate([hc, hl], axis=1), p)
            n_ctx = xc.shape[1]
            xc = xc + mod_c[5] * y[:, :n_ctx]
            xl = xl + mod_l[5] * y[:, n_ctx:]
    return rmsnorm(xl, final_norm_g)


_drawn_inputs = setup_inputs


def setup_inputs(seed=0):
    import zlib

    import numpy as np

    out = dict(_drawn_inputs(seed))
    spreads = {}
    factors = {'gla_gate_w': 2.69,
     'gla_gate_b': 5.567,
     'gla_norm_g': 16.043,
     'rw_w2': 4.824,
     'rw_kk': 49.98,
     'rw_ka': 4.58,
     'rw_lnx_g': 8.0,
     'rw_lnx_b': 42.03,
     'ssd_conv_b': 4.886,
     'ssd_d': 5.568,
     'ssd_norm_g': 4.041,
     'router_b': 19.933,
     'moe_b_gu': 45.163,
     'moe_b_down': 55.414,
     'norm2_g': 3.536}
    for name, (base, spread) in spreads.items():
        noise = np.random.default_rng([zlib.crc32(name.encode()), seed]).standard_normal(out[name].shape)
        drawn = base * np.exp(spread * noise) if base else spread * noise
        out[name] = jnp.asarray(drawn.astype(out[name].dtype))
    for name, factor in factors.items():
        out[name] = (out[name] * factor).astype(out[name].dtype)
    return out
```

```python
from contextlib import ExitStack

import concourse.bass as bass
import numpy as np
from concourse import mybir
from concourse.alu_op_type import AluOpType as ALU

F32 = mybir.dt.float32
I32 = mybir.dt.int32
ACT = mybir.ActivationFunctionType
P = 128

D, L, NT = 1024, 256, 512
KD = D // P
GRID_W = 64
DECAY = 0.606531
E, TOPK, FF, SLOTS = 32, 4, 1024, 64
EXTRA = L * TOPK // SLOTS
WORDS = 53152
LIMIT, ALPHA = 7.0, 1.702
EPS = 1e-6
NC_LEVELS = (64, 32, 16, 8, 4, 2, 1)

GLA0, RW0, SSD0, DT0 = 0, 800, 1728, 3264

(C_ID, C_TI, C_ONE, C_TIB, C_TX, C_TXB, C_BTI, C_BTX, C_BTIB, C_BTXB, C_HEAD) = range(11)
C_LEVEL = 11
C_DIAG2 = C_LEVEL + len(NC_LEVELS)
C_GBLK = C_DIAG2 + 1
C_IOTA = C_GBLK + 2
C_N = C_IOTA + 1


def constants():
    u, t = np.arange(P)[:, None], np.arange(P)[None, :]
    same = u // 64 == t // 64
    blocks = [u == t, u <= t, u >= 0 * t, u >= t, u < t, u > t, (u <= t) & same, (u < t) & same,
              (u >= t) & same, (u > t) & same, same]
    for b in NC_LEVELS:
        blocks.append((u // (2 * b) == t // (2 * b)) & (u // b % 2 != t // b % 2))
    blocks.append(2.0 * (u == t))
    v = np.arange(2 * P)[None, :]
    wide = (u // 32 == v // 64)
    last = np.zeros((P, P))
    last[:, :64] = np.arange(64)
    last[:, 64] = np.arange(P) % E
    last[:, 65] = (np.arange(P) // E + 1) * SLOTS
    last[:, 66] = last[:, 65]
    return np.ascontiguousarray(np.concatenate([np.broadcast_to(b, (P, P)) for b in blocks] + [wide, last], 1),
                                dtype=np.float32)


class Rounds:

    def __init__(self, table, full, free):
        self.full, self.free, self.at = full, free, {}
        fills, drains = [0] * len(full), [0] * len(full)
        for name, group, parts in table:
            fills[group] += 1
            self.at[name] = (group, fills[group], drains[group], drains[group] + parts)
            drains[group] += parts
        self.fills, self.drains = fills, drains

    def group(self, name):
        return self.at[name][0]

    def claim(self, pe, name):
        g, _, before, _ = self.at[name]
        if before > 0:
            pe.wait_ge(self.free[g], before)

    def filled(self, name, ins):
        ins.then_inc(self.full[self.at[name][0]], 1)

    def arrived(self, eng, name):
        g, value, _, _ = self.at[name]
        eng.wait_ge(self.full[g], value)

    def drained(self, name, ins):
        ins.then_inc(self.free[self.at[name][0]], 1)

    def partly(self, eng, name, parts):
        g, _, before, _ = self.at[name]
        eng.wait_ge(self.free[g], before + parts)

    def emptied(self, eng, name):
        g, _, _, after = self.at[name]
        eng.wait_ge(self.free[g], after)


PROJ = [
    ("B", ((SSD0 + 1024, 128, False), (SSD0 + 1152, 128, False))),
    ("C", ((SSD0 + 1280, 128, True), (SSD0 + 1408, 128, True))),
    ("xs0", ((SSD0 + 512, 128, False), (SSD0 + 640, 128, False))),
    ("xs1", ((SSD0 + 768, 128, False), (SSD0 + 896, 128, False))),
    ("z0", ((SSD0, 128, True), (SSD0 + 128, 128, True))),
    ("z1", ((SSD0 + 256, 128, True), (SSD0 + 384, 128, True))),
    ("gq", ((0, 128, True), (128, 128, False))),
    ("gv", ((256, 128, False), (384, 128, False))),
    ("og", ((512, 128, True), (640, 128, True))),
    ("lg", ((768, 32, False),)),
    ("rr", ((RW0, 128, True), (RW0 + 128, 128, True))),
    ("rk", ((RW0 + 256, 128, False), (RW0 + 384, 128, False))),
    ("rv", ((RW0 + 512, 128, False), (RW0 + 640, 128, False))),
    ("low", ((RW0 + 768, 96, False), (RW0 + 864, 64, True))),
]
W_GROUPS = [(SSD0 + 1024, 512, ("B", "C")), (SSD0 + 512, 512, ("xs0", "xs1")), (SSD0, 512, ("z0", "z1")),
            (0, 512, ("gq", "gv")), (512, 288, ("og", "lg")), (RW0, 512, ("rr", "rk")), (RW0 + 512, 416, ("rv", "low"))]

BWD_ORDER = [3, 2, 1, 0, 7, 6, 5, 4]


def round_table():
    t = [("prm", 0, 1), ("ada", 1, 1)]
    t += [(f"h{i}", i % 2 + 2, 2) for i in range(4)] + [("x0", 0, 1), ("x1", 1, 1)]
    t += [("dt", 0, 1)]
    t += [(n, (i + 1) % 4, 1) for i, (n, _) in enumerate(PROJ)]
    t += [("xst0", 0, 1), ("xst1", 1, 1), ("Bt", 2, 1), ("cc", 3, 1), ("st", 0, 1), ("sc", 1, 1)]
    for q in range(4):
        t += [(f"dc{2 * q}", 2, 2), (f"dc{2 * q + 1}", 3, 2), (f"yp{q}", q % 2, 1)]
    t += [("sn", 2, 1)]
    t += [("gz", 3, 1), ("gs", 0, 1), ("gk", 1, 1), ("gvt", 2, 1), ("gc", 3, 1), ("gS", 0, 1)]
    for i in range(9):
        t += [(f"l{i}a", (2 * i) % 4, 1), (f"l{i}b", (2 * i + 1) % 4, 1)]
    t += [("go", 2, 1), ("gn", 3, 1)]
    t += [("rz0", 0, 1), ("rz1", 1, 1), ("ra", 2, 1), ("rkn", 3, 1), ("rb", 0, 1), ("rg", 1, 1), ("rvt", 2, 1)]
    for tt in range(4):
        for s in ("cu", "bk", "AA", "BM") + (("MM",) if tt >= 2 else ()) + ("BV",):
            for d in (0, 1):
                t.append((f"{s}{tt}{d}", 2 * d + {"cu": 0, "bk": 1, "AA": 0, "BM": 1, "MM": 0, "BV": 1}[s], 1))
        for j in range(5):
            t += [(f"D{j}{tt}{d}", 2 * d, 2 if j < 4 else 1) for d in (0, 1)]
            t += [(f"T{j}{tt}{d}", 2 * d + 1, 1) for d in (0, 1)]
    for i in range(8):
        for d in (0, 1):
            t.append((f"R1{i}{d}", 2 * d, 1))
        for d in (0, 1):
            t.append((f"R2{i}{d}", 2 * d + 1, 1))
        if i >= 4:
            t += [(f"RO{i}{d}", 2 * d, 1) for d in (0, 1)]
        for d in (0, 1):
            t.append((f"R3{i}{d}", 2 * d + 1, 1))
    t += [("RU", 0, 1), ("rm", 1, 1), ("rv2", 2, 1)]
    t += [("w0", 0, 1), ("w1", 1, 1), ("n2", 2, 1), ("rt", 3, 1), ("hk0", 0, 1), ("hk1", 1, 1), ("xk0", 2, 1),
          ("xk1", 3, 1), ("m5", 0, 1), ("fg", 1, 1), ("pos", 2, 1), ("gt", 0, 1), ("cnd", 1, 1),
          ("idx", 2, 1), ("lst", 3, 1)]
    return t


def hybrid_block(nc, a):
    with ExitStack() as ctx:
        sem = lambda name: ctx.enter_context(nc.semaphore(name))
        arena = ctx.enter_context(nc.sbuf_tensor("arena", [P, WORDS], F32))
        ints = ctx.enter_context(nc.sbuf_tensor("ints", [P, 2 * EXTRA + 8], I32))
        PS = ctx.enter_context(nc.psum_tensor("PS", [P, 8, 512], F32))

        class Area:

            def __init__(self, start, end):
                self.at, self.end = start, end

            def take(self, *shape):
                n = int(np.prod(shape))
                ap = arena[:, self.at:self.at + n]
                self.at += n
                assert self.at <= self.end, (self.at, self.end, shape)
                if len(shape) == 2:
                    ap = ap.rearrange("p (a b) -> p a b", a=shape[0])
                if len(shape) == 3:
                    ap = ap.rearrange("p (a b c) -> p a b c", a=shape[0], b=shape[1])
                if len(shape) == 4:
                    ap = ap.rearrange("p (a b c d) -> p a b c d", a=shape[0], b=shape[1], c=shape[2])
                return ap

        keep = Area(0, WORDS)
        C = keep.take(C_N, P)
        pc = keep.take(162)
        w0b, gbb = keep.take(512), keep.take(256)
        dtb, alog, rbb = keep.take(16), keep.take(16), keep.take(E)
        W2A, gwb, g2w = keep.take(512), keep.take(256), keep.take(256)
        dtw, rtw = keep.take(KD, 16), keep.take(KD, E)
        csil = keep.take(KD, 2)
        mod = keep.take(48, 2)
        A1, A2 = keep.take(KD, 2), keep.take(KD)
        small = keep.take(64)
        muc, dall, dcol = keep.take(8), keep.take(8), keep.take(4)
        xT, cat = keep.take(KD, L), keep.take(KD, L)
        slots = [None] * 12
        for s in (2, 3, 4, 5, 0, 1):
            slots[s] = keep.take(2048)
        big0 = keep.at - 4096
        u_area = Area(keep.at, WORDS)

        rT, lowT, sgT = u_area.take(2, L), u_area.take(NT), u_area.take(L)
        kT, vT = u_area.take(2, NT), u_area.take(2, NT)
        after_rwkv_inputs = u_area.at
        KQ, gkc, gvT, gog, lgT = u_area.take(2, L), u_area.take(L), u_area.take(2, NT), u_area.take(2, L), u_area.take(NT)
        sz, xsT, BT, CT = u_area.take(4, L), u_area.take(4, NT), u_area.take(2, NT), u_area.take(2, L)
        scratch0 = u_area.at
        xtok, hT = None, None
        tail = Area(WORDS - 8192, WORDS)
        xtok, hT = tail.take(4, D), tail.take(KD, NT)

        sa = Area(scratch0, WORDS - 8192)
        prow = sa.take(2, P)
        diagR = sa.take(4, P)
        sb_ = Area(scratch0, WORDS - 8192 + 4096)
        xtk, Btok = sb_.take(4, 512), sb_.take(2, 256)
        dtk = sb_.take(4, 16)
        adt, wct, cumc = sb_.take(4, 16), sb_.take(2, 16), sb_.take(4, 16)
        dtmp = sb_.take(3, 64)
        ea = sb_.take(16)
        xw = sb_.take(2, 2, 512)
        Sst = sb_.take(2, 512)
        scF, scB = sb_.take(2, 3, P), sb_.take(2, 3, P)
        eD, EI, CI, WD = sb_.take(2, 768), sb_.take(2, 512), sb_.take(2, 512), sb_.take(2, 768)
        ssq = sb_.take(4, L)
        gs_ = Area(scratch0, WORDS - 8192 + 4096)
        gz, gzt = gs_.take(4, 256), gs_.take(4, 256)
        gE, gkt, gkw = gs_.take(2, 256), gs_.take(2, P), gs_.take(2, 256)
        gvk = gs_.take(4, 256)
        gSt = gs_.take(2, 256)
        gcum, qI = gs_.take(2, L), gs_.take(2, L)
        lv, lk = gs_.take(2, 512), gs_.take(2, 512)
        att = gs_.take(4, 2, L)
        gO, gsq = gs_.take(2, L), gs_.take(2, L)

        ra = Area(after_rwkv_inputs, WORDS)
        low = Area(big0, big0 + 4096)
        TT = [low.take(4, 4, P) for _ in range(2)]
        lw = ra.take(4, 512)
        kk, ba = ra.take(2, NT), ra.take(2, NT)
        al = [ra.take(2, NT) for _ in range(2)]
        rho = [ra.take(2, L) for _ in range(2)]
        be = [ra.take(2, P) for _ in range(2)]
        ka = [ra.take(2, P) for _ in range(2)]
        eb = [ra.take(3, 2, P) for _ in range(2)]
        Vt = ra.take(4, 256)
        BVs = [ra.take(4, 256) for _ in range(2)]
        mb = [ra.take(2, 4, P) for _ in range(2)]
        mk = [ra.take(4, P) for _ in range(2)]
        bm = [ra.take(4, P) for _ in range(2)]
        XX = [ra.take(4, 2, P) for _ in range(2)]
        bt = [ra.take(4, 512) for _ in range(2)]
        Us = [ra.take(2, 256) for _ in range(2)]
        RH = [ra.take(256) for _ in range(2)]
        ST = [ra.take(2, 64) for _ in range(2)]
        wc = [ra.take(2, 8) for _ in range(2)]
        oT, bon, rgt = ra.take(2, L), ra.take(2, L), ra.take(2, L)

        osq = kk.rearrange("p a b -> p (a b)")[:, 0:512]
        bon_tmp = eb[0].rearrange("p a b c -> p (a b c)")[:, 0:512]

        ma = Area(big0 + 4096, WORDS)
        for s in range(6, 12):
            slots[s] = ma.take(2048)
        h2T = ma.take(KD, L)
        h2k, xk = ma.take(2, D), ma.take(2, D)
        m5r, fgr = ma.take(D), ma.take(D)
        hg, actT = ma.take(KD, SLOTS), ma.take(4, 2, SLOTS)
        glu, lin, sgm, act_ = ma.take(512), ma.take(512), ma.take(512), ma.take(512)
        ye = ma.take(512)
        sel, selw = ma.take(2, SLOTS), ma.take(2, 2, SLOTS)
        SW = ma.take(L)
        bgrow = ma.take(2 * FF)
        this_e = ma.take(SLOTS)
        gates, spos = ma.take(2, E), ma.take(2, E)
        lgt = ma.take(2, E)
        rt1, rt2, rt3, rt4 = ma.take(2, E), ma.take(2, E), ma.take(2, E), ma.take(2, E)
        top8 = ma.take(2, 8)
        gT = ma.take(L)
        ibase = ma.take(E + EXTRA)
        cand, onehot = ma.take(4), ma.take(EXTRA)
        r2 = ma.take(L)
        msk3 = ma.take(2, 96)
        sq2 = slots[11]
        dg = slots[10].rearrange("p (a b) -> p a b", a=16)
        bdn = slots[8]

        full = [sem(f"pair_full{g}") for g in range(4)]
        free = [sem(f"pair_free{g}") for g in range(4)]
        R = Rounds(round_table(), full, free)
        consts_in, rows_in, x_in, mats_in = sem("consts_in"), sem("rows_in"), sem("x_in"), sem("mats_in")
        late_in = sem("late_in")
        zeroed = sem("zeroed")
        slot_full = [sem(f"slot_full{s}") for s in range(12)]
        slot_free = [sem(f"slot_free{s}") for s in range(12)]
        named = lambda names: [sem(n) for n in names.split()]
        vec_step, act_step, moe_vec = named("vec_step act_step moe_vec")
        silu_c, squares1, var1, std1, diag_ready, mod_ready = named("silu_c squares1 var1 std1 diag_ready mod_ready")
        conv_init, conv_silu = named("conv_init conv_silu")
        dt_abs, dt_exp, dt_ready, ctx_w, xw_ready = named("dt_abs dt_exp dt_ready ctx_w xw_ready")
        E_ready, w_ready, ssq_ready, sn_std = named("E_ready w_ready ssq_ready sn_std")
        gz_abs, gz_exp, g_ready, gkw_ready, qi_exp, qi_ready = named("gz_abs gz_exp g_ready gkw_ready qi_exp qi_ready")
        lv_arg, lv_exp, lk_ready, gsq_ready, gn_std, gla_done = named("lv_arg lv_exp lk_ready gsq_ready gn_std gla_done")
        rw_tanh, rz_sig, lw_ready, kk_sq, kk_std, rw_pre, gate_sig = named(
            "rw_tanh rz_sig lw_ready kk_sq kk_std rw_pre gate_sig")
        rw_in, osq_ready, o_std, cat_ready = named("rw_in osq_ready o_std cat_ready")
        st_ready = [sem(f"st_ready{d}") for d in range(2)]
        x2_sq, dg_ready, n2_std, h2_ready = named("x2_sq dg_ready n2_std h2_ready")
        rt_max, rt_exp, mask_ready, gates_ready, onehot_ready = named("rt_max rt_exp mask_ready gates_ready onehot_ready")
        sel_ready, gathered, hg_ready, glu_ready, sig_ready, act_ready = named(
            "sel_ready gathered hg_ready glu_ready sig_ready act_ready")
        ye_ready, selT_done, sw_ready, scattered, y_init = named("ye_ready selT_done sw_ready scattered y_init")
        actT_done, actT_ready, te_ready = named("actT_done actT_ready te_ready")
        y_read, f_sq, f_var, f_std, out_ready, out_done = named("y_read f_sq f_var f_std out_ready out_done")
        N_ROWS, N_MATS = 22, 18

        def pair(name, n=1024):
            g = R.group(name)
            return PS[:, 2 * g:2 * g + 2, :].rearrange("p a b -> p (a b)")[:, 0:n]

        def o_of(h):
            return h % 2 * 2 + h // 2

        def Cb(i, n=1):
            return C[:, i:i + n, :].rearrange("p a b -> p (a b)")

        loads = [(n % 6, 1, "ada", n) for n in range(24)]
        loads += [(2 * (n % 3), 2, "in", n) for n in range(len(W_GROUPS))]
        loads += [(2 + n, 1, "out", n) for n in range(4)]
        base = [0] * 12
        holder = [None] * 12
        place, before = {}, {}
        for s, width, kind, n in loads:
            before[kind, n] = sorted({h for h in holder[s:s + width] if h})
            base[s] += 1
            place[kind, n] = (s, base[s])
            for q in range(s, s + width):
                holder[q] = (s, base[s])

        def w_in_tile(n):
            s = place["in", n][0]
            i = {0: 0, 2: 1, 4: 2}[s]
            lo = {0: big0, 1: big0 - 8192, 2: big0 - 4096}[i]
            w = W_GROUPS[n][1]
            return arena[:, lo:lo + KD * w].rearrange("p (k c) -> p k c", k=KD)

        w_ada_k = a["w_ada"][0].rearrange("(k p) c -> k p c", p=P)
        w_in_k = a["w_in"][0].rearrange("(k p) c -> p k c", p=P)
        w_out_k = a["w_out"][0].rearrange("(k p) c -> p k c", p=P)
        gu_k = a["moe_w_gu"][0].rearrange("e (k p) c -> e k p c", p=P)
        dn_k = a["moe_w_down"][0].rearrange("e (k p) c -> e p k c", p=P)

        block = ctx.enter_context(nc.Block())

        @block.sync
        def _(sp):
            def slot_wait(kind, n):
                for s, count in before[kind, n]:
                    sp.wait_ge(slot_free[s], count)

            sp.dma_start(Cb(0, C_N), a["consts"]).then_inc(consts_in, 16)
            sp.dma_start(xtok[:, 0:2, :], a["ctx"][0].rearrange("(i p) d -> p i d", p=P)).then_inc(x_in, 16)
            sp.dma_start(xtok[:, 2:4, :], a["x"][0].rearrange("(i p) d -> p i d", p=P)).then_inc(x_in, 16)
            for n in range(24):
                s = place["ada", n][0]
                slot_wait("ada", n)
                sp.dma_start(slots[s], w_ada_k[n // 3, :, n % 3 * 2048:n % 3 * 2048 + 2048]).then_inc(slot_full[s], 16)
            for n, (c0, w, _) in enumerate(W_GROUPS):
                s = place["in", n][0]
                slot_wait("in", n)
                sp.dma_start(w_in_tile(n), w_in_k[:, :, c0:c0 + w]).then_inc(slot_full[s], 16)
            for n in range(4):
                s = place["out", n][0]
                slot_wait("out", n)
                sp.dma_start(slots[s].rearrange("p (k c) -> p k c", k=2), w_out_k[:, 2 * n:2 * n + 2, :])\
                    .then_inc(slot_full[s], 16)

            sp.wait_ge(cat_ready, 1)
            sp.dma_start(bgrow[0:E, :], a["moe_b_gu"][0]).then_inc(late_in, 16)
            sp.dma_start(bdn[0:E, 0:D], a["moe_b_down"][0]).then_inc(late_in, 16)

            def load_expert(n, e, first):
                for s in range(12):
                    if not first:
                        sp.wait_ge(slot_free[s], n + (base[s]))
                    if s < 8:
                        src = gu_k[bass.ds(e, 1), s, :, :].rearrange("a p c -> p (a c)")
                        dst = slots[s]
                    else:
                        src = dn_k[bass.ds(e, 1), :, 2 * (s - 8):2 * (s - 8) + 2, :].rearrange("a p k c -> p (a k) c")
                        dst = slots[s].rearrange("p (k c) -> p k c", k=2)
                    if first and 2 <= s <= 5:
                        sp.wait_ge(slot_free[s], base[s])
                    if first and s == 8:
                        sp.wait_ge(y_init, 1)
                    sp.dma_start(dst, src).then_inc(slot_full[s], 16)

            load_expert(0, 0, True)
            with sp.Fori(1, E) as n:
                load_expert(n, n, False)
            R.emptied(sp, "lst")
            extra = sp.value_load(ints[0:1, 0:1], min_val=0, max_val=EXTRA)
            with sp.If(extra > 0):
                with sp.Fori(0, extra) as j:
                    e = sp.value_load(ints[0:1, bass.ds(j + 8, 1)], min_val=0, max_val=E - 1)
                    load_expert(j + E, e, False)
            for i in range(2):
                sp.wait_ge(out_ready, i + 1)
                sp.dma_start(a["out"][0, i * P:(i + 1) * P, :], xk[:, i, :]).then_inc(out_done, 16)
            sp.wait_ge(out_done, 32)

        @block.gpsimd
        def _(pool):
            pool.memset(prow[:, :, :], 0.0)
            pool.memset(W2A[0:64, :], 0.0)
            pool.memset(gwb[0:32, :], 0.0).then_inc(zeroed, 1)
            pool.wait_ge(gla_done, 1)
            for d in range(2):
                last = pool.memset(ST[d], 0.0)
            last.then_inc(zeroed, 1)
            pool.wait_ge(cat_ready, 1)
            pool.memset(ye, 0.0).then_inc(ye_ready, 1)
            pool.memset(SW, 0.0).then_inc(sw_ready, 1)
            pool.memset(hg[:, 0, :], 0.0).then_inc(hg_ready, 1)
            pool.memset(act_, 0.0).then_inc(act_ready, 1)
            pool.memset(ibase, 0.0).then_inc(zeroed, 1)

        @block.scalar
        def _(act):
            steps = [0]

            def step(ins):
                ins.then_inc(act_step, 1)
                steps[0] += 1

            def settle():
                act.wait_ge(act_step, steps[0])

            act.wait_ge(zeroed, 1)
            ra_, rb_ = prow[:, 0, :], prow[:, 1, :]

            def rows(dst, src):
                act.dma_start(dst, src).then_inc(rows_in, 16)

            rows(ra_[0:48, :], a["b_ada"][0].rearrange("(r p) -> r p", p=P))
            rows(ra_[48:56, :], a["c"][0].rearrange("(r p) -> r p", p=P))
            rows(ra_[56:64, :], a["c_ctx"].rearrange("(r p) -> r p", p=P))
            rows(ra_[64:72, :], a["norm1_g"][0].rearrange("(r p) -> r p", p=P))
            rows(ra_[72:80, :], a["norm2_g"][0].rearrange("(r p) -> r p", p=P))
            rows(ra_[80:88, :], a["final_norm_g"].rearrange("(r p) -> r p", p=P))
            for i in range(2):
                mu = a["rw_mu"][0, i, :]
                rows(rb_[8 * i:8 * i + 6, :], mu[0:768].rearrange("(r p) -> r p", p=P))
                rows(rb_[8 * i + 6:8 * i + 7, 0:96], mu[768:864].rearrange("(r p) -> r p", r=1))
                rows(rb_[8 * i + 7:8 * i + 8, 0:64], mu[864:928].rearrange("(r p) -> r p", r=1))
            rows(rb_[16:18, :], a["rw_a0"][0].rearrange("(r p) -> r p", p=P))
            rows(rb_[18:20, :], a["rw_kk"][0].rearrange("(r p) -> r p", p=P))
            rows(rb_[20:22, :], a["rw_ka"][0].rearrange("(r p) -> r p", p=P))
            rows(rb_[22:24, :], a["rw_rk"][0].rearrange("(r b) n -> r (b n)", b=2))
            rows(rb_[24:26, :], a["rw_lnx_g"][0].rearrange("(r b) n -> r (b n)", b=2))
            rows(rb_[26:28, :], a["rw_lnx_b"][0].rearrange("(r b) n -> r (b n)", b=2))
            rows(rb_[28:60, :], a["ssd_conv_w"][0].rearrange("j (t p) -> (j t) p", p=P))
            rows(rb_[60:68, :], a["ssd_conv_b"][0].rearrange("(r p) -> r p", p=P))
            rows(rb_[68:72, :], a["ssd_norm_g"][0].rearrange("(r p) -> r p", p=P))
            rows(rb_[72:74, :], a["gla_norm_g"][0].rearrange("(r b) n -> r (b n)", b=2))

            def mats(dst, src):
                act.dma_start(dst, src).then_inc(mats_in, 16)

            def spread(dst, src):
                mats(dst, src.partition_broadcast(P))

            for d in range(2):
                spread(w0b[:, 256 * d:256 * d + 256], a["rw_w0"][0, d, :])
                spread(gbb[:, P * d:P * d + P], a["gla_gate_b"][0, d, :])
                spread(dtb[:, 8 * d:8 * d + 8], a["ssd_dt_bias"][0, d, :])
                spread(alog[:, 8 * d:8 * d + 8], a["ssd_a_log"][0, d, :])
                mats(W2A[32 * d:32 * d + 32, 256 * d:256 * d + 256], a["rw_w2"][0, d])
                mats(gwb[16 * d:16 * d + 16, P * d:P * d + P], a["gla_gate_w"][0, d])
            spread(rbb, a["router_b"][0])
            spread(dall, a["ssd_d"][0])
            mats(W2A[64:96, 0:256], a["rw_a2"][0])
            mats(g2w[0:64, :], a["rw_g2"][0])
            mats(dtw[:, :, :], a["w_in"][0].rearrange("(k p) c -> p k c", p=P)[:, :, DT0:DT0 + 16])
            mats(rtw[:, :, :], a["router_w"][0].rearrange("(k p) c -> p k c", p=P))

            act.wait_ge(x_in, 32)
            for i in range(4):
                act.activation(hT.rearrange("p k t -> p (k t)")[:, 1024 * i:1024 * i + 1024], xtok[:, i, :], ACT.Square,
                               accum_out=small[:, i:i + 1]).then_inc(squares1, 1)
            act.wait_ge(var1, 1)
            act.activation(small[:, 8:12], small[:, 4:8], ACT.Sqrt).then_inc(std1, 1)
            R.emptied(act, "prm")
            act.activation(csil.rearrange("p k s -> p s k"), pc[:, 48:64].rearrange("p (s k) -> p s k", s=2), ACT.Silu)\
               .then_inc(silu_c, 1)
            act.wait_ge(mod_ready, 1)
            act.wait_ge(squares1, 4)
            for i in range(4):
                R.arrived(act, f"h{i}")
                k = 2 * i
                step(act.activation(hT[:, k, 0:L], pair(f"h{i}")[:, 0:L], ACT.Identity,
                                    bias=mod[:, k, 1:2], scale=A1[:, k, 1:2]))
                ins = act.activation(hT[:, k, L:NT], pair(f"h{i}")[:, L:NT], ACT.Identity,
                                     bias=mod[:, k, 0:1], scale=A1[:, k, 0:1])
                R.drained(f"h{i}", ins)
            for i in range(2):
                R.arrived(act, f"x{i}")
                R.drained(f"x{i}", act.copy(xT[:, 4 * i:4 * i + 4, :].rearrange("p a b -> p (a b)"), pair(f"x{i}")))

            conv = {"B": (BT, 4, NT), "C": (CT, 6, L), "xs0": (xsT[:, 0:2, :], 0, NT), "xs1": (xsT[:, 2:4, :], 2, NT)}

            def conv_start(name):
                dst, tile, n = conv[name]
                R.arrived(act, name)
                for j in range(2):
                    act.activation(dst[:, j, :], pair(name)[:, 512 * j:512 * j + n], ACT.Identity,
                                   bias=pc[:, 88 + 60 + tile + j:88 + 61 + tile + j],
                                   scale=pc[:, 88 + 28 + 16 + tile + j:88 + 29 + 16 + tile + j]).then_inc(conv_init, 1)

            def conv_end(name):
                dst, _, n = conv[name]
                R.emptied(act, name)
                act.activation(dst, dst, ACT.Silu).then_inc(conv_silu, 1)

            conv_start("B")
            conv_start("C")
            conv_end("B")
            conv_start("xs0")
            conv_end("C")
            conv_start("xs1")
            conv_end("xs0")
            conv_end("xs1")
            for q in range(2):
                R.arrived(act, f"z{q}")
                R.drained(f"z{q}", act.activation(sz[:, 2 * q:2 * q + 2, :],
                                                  pair(f"z{q}").rearrange("p (a b) -> p a b", a=2)[:, :, 0:L], ACT.Silu))
            R.arrived(act, "gq")
            step(act.activation(KQ[:, 1, :], pair("gq")[:, 0:L], ACT.Copy, scale=float(32 ** -0.5)))
            step(act.copy(KQ[:, 0, :], pair("gq")[:, 512 + L:1024]))
            R.drained("gq", act.copy(gkc, pair("gq")[:, 512:512 + L]))
            R.arrived(act, "gv")
            R.drained("gv", act.copy(gvT.rearrange("p a b -> p (a b)"), pair("gv")))
            R.arrived(act, "og")
            R.drained("og", act.activation(gog[:, :, :], pair("og").rearrange("p (a b) -> p a b", a=2)[:, :, 0:L],
                                           ACT.Silu))

            R.arrived(act, "xst0")
            R.drained("xst0", act.copy(xtk[:, 0:2, :].rearrange("p a b -> p (a b)"), pair("xst0")))
            R.arrived(act, "xst1")
            R.drained("xst1", act.copy(xtk[:, 2:4, :].rearrange("p a b -> p (a b)"), pair("xst1")))
            R.arrived(act, "Bt")
            R.drained("Bt", act.copy(Btok[:, :, :].rearrange("p a b -> p (a b)"), pair("Bt", 512)))
            act.wait_ge(dt_abs, 1)
            step(act.activation(dtmp[:, 1, :], dtmp[:, 0, :], ACT.Exp))
            act.wait_ge(mats_in, 16 * N_MATS)
            act.activation(ea, alog, ACT.Exp).then_inc(dt_exp, 1)
            settle()
            act.activation(dtmp[:, 2, :], dtmp[:, 1, :], ACT.Ln, bias=1.0).then_inc(dt_exp, 1)
            R.arrived(act, "cc")
            act.activation(wct.rearrange("p a b -> p (a b)"), pair("cc")[:, 0:32], ACT.Exp).then_inc(ctx_w, 1)
            for h in range(8):
                name = f"dc{h}"
                R.arrived(act, name)
                if h >= 2:
                    act.wait_ge(w_ready, h - 1)
                R.drained(name, act.activation(EI[:, h % 2, :], pair(name, 512), ACT.Exp))
                R.emptied(act, name)
                act.activation(eD[:, h % 2, :], eD[:, h % 2, :], ACT.Exp).then_inc(E_ready, 1)
            R.emptied(act, "sn")
            act.activation(ssq.rearrange("p a b -> p (a b)")[:, 512:1024], ssq.rearrange("p a b -> p (a b)")[:, 0:512],
                           ACT.Sqrt).then_inc(sn_std, 1)

            act.wait_ge(gz_abs, 1)
            act.activation(gzt, gzt, ACT.Exp).then_inc(gz_exp, 1)
            act.wait_ge(gz_exp, 1)
            act.activation(gzt, gzt, ACT.Ln, bias=1.0).then_inc(gz_exp, 1)
            R.arrived(act, "gs")
            R.drained("gs", act.activation(gE.rearrange("p a b -> p (a b)"), pair("gs", 512), ACT.Exp))
            R.arrived(act, "gk")
            R.drained("gk", act.copy(gkt.rearrange("p a b -> p (a b)"), pair("gk", 256)))
            R.arrived(act, "gvt")
            R.drained("gvt", act.copy(gvk.rearrange("p a b -> p (a b)"), pair("gvt")))
            R.arrived(act, "gc")
            R.drained("gc", act.copy(gcum.rearrange("p a b -> p (a b)"), pair("gc", 512)))
            R.emptied(act, "gc")
            act.activation(qI, gcum, ACT.Exp).then_inc(qi_exp, 1)
            for i in range(8):
                act.wait_ge(lv_arg, i + 1)
                act.activation(lv[:, i % 2, :], lv[:, i % 2, :], ACT.Exp).then_inc(lv_exp, 1)
            R.emptied(act, "gn")
            act.activation(gsq, gsq, ACT.Sqrt).then_inc(gn_std, 1)

            act.wait_ge(gla_done, 1)
            act.activation(lowT[0:64, :], lowT[0:64, :], ACT.Tanh).then_inc(rw_tanh, 1)
            R.emptied(act, "rz0")
            R.emptied(act, "rz1")
            act.activation(lw, lw, ACT.Sigmoid).then_inc(rz_sig, 1)
            R.arrived(act, "ra")
            for c in range(2):
                ins = act.activation(ba[:, c, :], pair("ra")[:, 512 * c:512 * c + 512], ACT.Sigmoid,
                                     bias=pc[:, 88 + 16 + c:88 + 17 + c])
                if c == 0:
                    step(ins)
            R.drained("ra", ins)
            act.activation(sgT[0:64, :], sgT[0:64, :], ACT.Sigmoid).then_inc(gate_sig, 1)
            R.emptied(act, "rkn")
            act.activation(kk, kk, ACT.Sqrt).then_inc(kk_std, 1)
            R.arrived(act, "rvt")
            R.drained("rvt", act.copy(Vt.rearrange("p a b -> p (a b)"), pair("rvt")))
            R.arrived(act, "rg")
            R.drained("rg", act.copy(rgt.rearrange("p a b -> p (a b)"), pair("rg", 512)))
            for tt in range(4):
                for d in range(2):
                    name = f"cu{tt}{d}"
                    R.arrived(act, name)
                    if tt:
                        act.wait_ge(rw_in, 2 * (tt - 1) + d + 1)
                    cu = pair(name, 512).rearrange("p (c x t) -> p x c t", c=2, x=2)
                    step(act.activation(eb[d][:, 0, :, :], cu[:, 0, :, :], ACT.Exp))
                    step(act.activation(eb[d][:, 1, :, :], cu[:, 0, :, :], ACT.Exp, scale=-1.0))
                    R.drained(name, act.activation(eb[d][:, 2, :, :], cu[:, 1, :, :], ACT.Exp))
                for d in range(2):
                    name = f"bk{tt}{d}"
                    R.arrived(act, name)
                    R.drained(name, act.copy(bt[d][:, tt, :], pair(name, 512)))
                for j in range(4):
                    for d in range(2):
                        name = f"D{j}{tt}{d}"
                        R.arrived(act, name)
                        R.drained(name, act.copy(XX[d][:, :, 0, :], pair(name, 512).rearrange("p (o t) -> p o t", o=4)))
            for i in range(8):
                for d in range(2):
                    name = f"R2{i}{d}"
                    ch = i if d == 0 else BWD_ORDER[i]
                    tt, q = ch // 2, ch % 2
                    R.arrived(act, name)
                    R.drained(name, act.copy(Us[d][64 * q:64 * q + 64, tt % 2, :], pair(name, 256)[64 * q:64 * q + 64, :]))
            R.emptied(act, "rv2")
            act.activation(bon_tmp, bon_tmp, ACT.Sqrt).then_inc(o_std, 1)

            R.emptied(act, "n2")
            act.activation(r2, r2, ACT.Sqrt).then_inc(n2_std, 1)
            R.arrived(act, "hk0")
            R.drained("hk0", act.copy(h2k[:, 0, :], pair("hk0")))
            R.arrived(act, "hk1")
            R.drained("hk1", act.copy(h2k[:, 1, :], pair("hk1")))
            R.arrived(act, "xk0")
            R.drained("xk0", act.copy(xk[:, 0, :], pair("xk0")))
            R.arrived(act, "xk1")
            R.drained("xk1", act.copy(xk[:, 1, :], pair("xk1")))
            R.arrived(act, "m5")
            R.drained("m5", act.copy(m5r, pair("m5")))
            R.arrived(act, "fg")
            R.drained("fg", act.copy(fgr, pair("fg")))
            act.wait_ge(rt_max, 1)
            act.activation(rt1, rt1, ACT.Exp).then_inc(rt_exp, 1)

            def expert(n):
                act.wait_ge(gathered, n + 1)
                act.copy(hg.rearrange("p k t -> p (k t)"), PS[:, 2, :]).then_inc(hg_ready, 1)
                act.wait_ge(glu_ready, n + 1)
                act.activation(sgm, glu, ACT.Sigmoid, scale=ALPHA).then_inc(sig_ready, 1)
                act.wait_ge(selT_done, n + 1)
                act.copy(SW, PS[:, 3, 0:L]).then_inc(sw_ready, 1)
                act.wait_ge(actT_done, n + 1)
                act.copy(actT.rearrange("p a b c -> p (a b c)"), PS[:, 2, :]).then_inc(actT_ready, 1)
                act.wait_ge(slot_free[11], n + base[11] + 1)
                act.copy(ye, PS[:, 3, :]).then_inc(ye_ready, 1)

            with act.Fori(0, E) as n:
                expert(n)
            R.emptied(act, "lst")
            extra = act.value_load(ints[0:1, 0:1], min_val=0, max_val=EXTRA)
            with act.If(extra > 0):
                with act.Fori(0, extra) as j:
                    expert(j + E)
            for i in range(2):
                act.wait_ge(y_read, i + 1)
                act.activation(h2k[:, i, :], xk[:, i, :], ACT.Square, accum_out=small[:, 16 + i:17 + i]).then_inc(f_sq, 1)
            act.wait_ge(f_var, 1)
            act.activation(small[:, 18:20], small[:, 16:18], ACT.Sqrt).then_inc(f_std, 1)

        def level_out(dve, i, step, settle):
            for part, h0 in (("a", 0), ("b", 2)):
                R.arrived(dve, f"l{i}{part}")
                R.emptied(dve, f"l{i - 1}{part}")
                settle()
                for hh in range(2):
                    src = pair(f"l{i}{part}")[:, 512 * hh:512 * hh + 256].rearrange("p (i t) -> p i t", i=2)
                    for ti in range(2):
                        if i == 1:
                            ins = dve.tensor_copy(att[:, h0 + hh, ti, (1 - ti) * P:(2 - ti) * P], src[:, ti, :])
                        else:
                            ins = dve.copy_predicated(att[:, h0 + hh, ti, ti * P:ti * P + P], Cb(C_LEVEL + i - 2).bitcast(I32), src[:, ti, :])
                        if not (hh and ti):
                            step(ins)
                R.drained(f"l{i}{part}", ins)

        @block.vector
        def _(dve):
            steps = [0]

            def step(ins):
                ins.then_inc(vec_step, 1)
                steps[0] += 1

            def settle():
                dve.wait_ge(vec_step, steps[0])

            def run(ins):
                step(ins)
                settle()

            R.arrived(dve, "prm")
            step(dve.tensor_copy(pc[:, 0:88], pair("prm")[:, 0:88]))
            R.drained("prm", dve.tensor_copy(pc[:, 88:162], pair("prm")[:, 128:202]))
            B = lambda i, n=1: pc[:, 88 + i:88 + i + n]
            R.emptied(dve, "prm")
            run(dve.tensor_tensor(muc, B(0, 8), B(8, 8), ALU.add))
            step(dve.tensor_scalar(muc, muc, -1.0, 1.0, ALU.mult, ALU.add))
            dve.wait_ge(squares1, 4)
            dve.tensor_scalar(small[:, 4:8], small[:, 0:4], 1.0 / D, EPS, ALU.mult, ALU.add).then_inc(var1, 1)
            dve.wait_ge(std1, 1)
            run(dve.reciprocal(small[:, 12:16], small[:, 8:12]))
            dve.wait_ge(consts_in, 16)
            for i in range(4):
                dve.tensor_scalar(diagR[:, i, :], Cb(C_ID), small[:, 12 + i:13 + i], None, ALU.mult).then_inc(diag_ready, 1)
            R.arrived(dve, "ada")
            R.drained("ada", dve.tensor_tensor(mod, pair("ada", 96).rearrange("p (m s) -> p m s", s=2),
                                               pc[:, 0:48].unsqueeze(2).to_broadcast([P, 48, 2]), ALU.add))
            R.emptied(dve, "ada")
            step(dve.scalar_tensor_tensor(out=A2, in0=mod[:, 32:40, 0], scalar=1.0, in1=pc[:, 72:80], op0=ALU.add, op1=ALU.mult))
            dve.scalar_tensor_tensor(out=A1, in0=mod[:, 8:16, :], scalar=1.0,
                                     in1=pc[:, 64:72].unsqueeze(2).to_broadcast([P, 8, 2]),
                                     op0=ALU.add, op1=ALU.mult).then_inc(mod_ready, 1)
            dve.wait_ge(mod_ready, 1)
            for i in range(4):
                R.arrived(dve, f"h{i}")
                k = 2 * i + 1
                step(dve.tensor_scalar(hT[:, k, 0:L], pair(f"h{i}")[:, 512:512 + L], A1[:, k, 1:2], mod[:, k, 1:2],
                                       ALU.mult, ALU.add))
                ins = dve.tensor_scalar(hT[:, k, L:NT], pair(f"h{i}")[:, 512 + L:1024], A1[:, k, 0:1], mod[:, k, 0:1],
                                        ALU.mult, ALU.add)
                R.drained(f"h{i}", ins)
            R.arrived(dve, "dt")
            dve.wait_ge(mats_in, 16 * N_MATS)
            R.drained("dt", dve.tensor_tensor(dtk, pair("dt", 64).rearrange("p (a b) -> p a b", a=4),
                                              dtb.unsqueeze(1).to_broadcast([P, 4, 16]), ALU.add))
            R.emptied(dve, "dt")
            for b in range(2):
                step(dve.tensor_copy(dcol[64 * b:64 * b + 64, :], dall[64 * b:64 * b + 64, b:8:2]))

            def rows_of(ap, n):
                parts = [] if n == L else [ap[:, 0:L].rearrange("p (r w) -> p r w", r=1)]
                return parts + [ap[:, n - L:n].rearrange("p (r w) -> p r w", w=GRID_W)]

            def add_neighbours(dst, src, n, taps, name, last):
                work = []
                for off, wgt in taps:
                    for d_, s_ in zip(rows_of(dst, n), rows_of(src, n)):
                        w = d_.shape[2]
                        lo, hi = max(0, -off), w - max(0, off)
                        work.append((d_[:, :, lo:hi], s_[:, :, lo + off:hi + off], wgt))
                for i, (d_, s_, wgt) in enumerate(work):
                    ins = dve.scalar_tensor_tensor(out=d_, in0=s_, scalar=wgt, in1=d_, op0=ALU.mult, op1=ALU.add)
                    if last and i == len(work) - 1:
                        R.drained(name, ins)
                    else:
                        run(ins)

            conv = {"B": (BT, 4, NT), "C": (CT, 6, L), "xs0": (xsT[:, 0:2, :], 0, NT), "xs1": (xsT[:, 2:4, :], 2, NT)}
            for i, name in enumerate(("B", "C", "xs0", "xs1")):
                dst, tile, n = conv[name]
                dve.wait_ge(conv_init, 2 * i + 2)
                R.arrived(dve, name)
                for j in range(2):
                    taps = [(k - 2, B(28 + 8 * k + tile + j)) for k in (0, 1, 3)]
                    add_neighbours(dst[:, j, :], pair(name)[:, 512 * j:512 * j + n], n, taps, name, j == 1)
            R.arrived(dve, "lg")
            R.drained("lg", dve.tensor_copy(lgT[0:32, :], pair("lg", 512)[0:32, :]))
            shifted = {"rr": ((rT[:, 0, :], P, L), (rT[:, 1, :], P, L)), "rk": ((kT[:, 0, :], P, NT), (kT[:, 1, :], P, NT)),
                       "rv": ((vT[:, 0, :], P, NT), (vT[:, 1, :], P, NT)), "low": ((lowT, 96, NT), (sgT, 64, L))}
            for i, name in enumerate(("rr", "rk", "rv", "low")):
                R.arrived(dve, name)
                for j, (dst, m, n) in enumerate(shifted[name]):
                    c = 2 * i + j
                    src = pair(name)[0:m, 512 * j:512 * j + n]
                    run(dve.tensor_scalar(dst[0:m, :], src, muc[0:m, c:c + 1], None, ALU.mult))
                    add_neighbours(dst[0:m, :], src, n, [(-1, B(c)[0:m, :]), (1, B(8 + c)[0:m, :])], name, j == 1)

            x16 = dtk.rearrange("p a b -> p (a b)")
            dve.scalar_tensor_tensor(out=dtmp[:, 0, :], in0=x16, scalar=-1.0, in1=x16, op0=ALU.mult, op1=ALU.min).then_inc(dt_abs, 1)
            dve.wait_ge(dt_exp, 2)
            y = dtmp[:, 1, :]
            run(dve.tensor_scalar(dtmp[:, 0, :], y, 1.0 / 3, -0.5, ALU.mult, ALU.add))
            run(dve.tensor_tensor(dtmp[:, 0, :], dtmp[:, 0, :], y, ALU.mult))
            run(dve.scalar_tensor_tensor(out=dtmp[:, 0, :], in0=dtmp[:, 0, :], scalar=1.0, in1=y, op0=ALU.add, op1=ALU.mult))
            adt16 = adt.rearrange("p a b -> p (a b)")
            run(dve.tensor_scalar(adt16, y, 0.01, None, ALU.is_lt))
            run(dve.copy_predicated(dtmp[:, 2, :], adt16.bitcast(I32), dtmp[:, 0, :]))
            run(dve.scalar_tensor_tensor(out=x16, in0=x16, scalar=0.0, in1=dtmp[:, 2, :], op0=ALU.max, op1=ALU.add))
            dve.scalar_tensor_tensor(out=adt, in0=dtk, scalar=-1.0, in1=ea.unsqueeze(1).to_broadcast([P, 4, 16]),
                                     op0=ALU.mult, op1=ALU.mult).then_inc(dt_ready, 1)
            R.arrived(dve, "cc")
            dve.wait_ge(ctx_w, 1)
            R.drained("cc", dve.tensor_copy(cumc.rearrange("p a b -> p (a b)"), pair("cc", 64)))
            run(dve.tensor_tensor(wct, wct, dtk[:, 0:2, :], ALU.mult))
            R.emptied(dve, "xst0")
            R.emptied(dve, "xst1")
            for tt in range(2):
                for d in range(2):
                    ins = dve.tensor_tensor(xw[:, tt, d, :].rearrange("p (h c) -> p h c", h=8),
                                            xtk[:, tt, :].rearrange("p (h c) -> p h c", h=8),
                                            wct[:, tt, 8 * d:8 * d + 8].unsqueeze(2).to_broadcast([P, 8, 64]), ALU.mult)
                    ins.then_inc(xw_ready, 1)
            R.arrived(dve, "st")
            R.drained("st", dve.tensor_copy(Sst, pair("st").rearrange("p (a b) -> p a b", a=2)))
            R.arrived(dve, "sc")
            sc = pair("sc").rearrange("p (g s t) -> p g s t", g=2, s=2)
            for g in range(2):
                step(dve.tensor_tensor(scF[:, g, 0, :], sc[:, g, 0, 0:P], Cb(C_TI), ALU.mult))
                step(dve.tensor_copy(scF[:, g, 1, :], sc[:, g, 0, P:L]))
                step(dve.tensor_tensor(scF[:, g, 2, :], sc[:, g, 1, P:L], Cb(C_TI), ALU.mult))
                step(dve.tensor_tensor(scB[:, g, 0, :], sc[:, g, 0, 0:P], Cb(C_TIB), ALU.mult))
                step(dve.tensor_copy(scB[:, g, 1, :], sc[:, g, 1, 0:P]))
                ins = dve.tensor_tensor(scB[:, g, 2, :], sc[:, g, 1, P:L], Cb(C_TIB), ALU.mult)
                if g == 0:
                    step(ins)
            R.drained("sc", ins)
            R.emptied(dve, "sc")
            R.emptied(dve, "cc")

            def exponents(h):
                e, dc = eD[:, h % 2, :], pair(f"dc{h}", 512)
                R.partly(dve, f"dc{h}", 1)
                for i, (lo, hi, src, col) in enumerate(((0, 256, dc[:, 0:256], cumc[:, 2, h:h + 1]),
                                                        (256, 384, dc[:, 128:256], cumc[:, 3, h:h + 1]),
                                                        (384, 512, dc[:, 256:384], cumc[:, 2, 8 + h:9 + h]),
                                                        (512, 768, dc[:, 256:512], cumc[:, 3, 8 + h:9 + h]))):
                    ins = dve.tensor_scalar(e[:, lo:hi], src, col, 0.0, ALU.subtract, ALU.min)
                    if i < 3:
                        step(ins)
                R.drained(f"dc{h}", ins)

            def weights(h):
                g = h // 4
                e, w = eD[:, h % 2, :], WD[:, h % 2, :]
                dve.wait_ge(E_ready, h + 1)
                R.emptied(dve, f"dc{h}")
                if h >= 2:
                    R.arrived(dve, f"yp{(h - 2) // 2}")
                step(dve.tensor_tensor(CI[:, h % 2, :].rearrange("p (a b) -> p a b", a=2),
                                       EI[:, h % 2, :].rearrange("p (a b) -> p a b", a=2),
                                       CT[:, g:g + 1, :].to_broadcast([P, 2, L]), ALU.mult))
                sf, sbk = scF[:, g].rearrange("p a b -> p (a b)"), scB[:, g].rearrange("p a b -> p (a b)")
                for i, (lo, hi, src, col) in enumerate(((0, 256, sf[:, 0:256], dtk[:, 2, h:h + 1]),
                                                        (256, 384, sf[:, 256:384], dtk[:, 3, h:h + 1]),
                                                        (384, 512, sbk[:, 0:128], dtk[:, 2, 8 + h:9 + h]),
                                                        (512, 768, sbk[:, 128:384], dtk[:, 3, 8 + h:9 + h]))):
                    ins = dve.scalar_tensor_tensor(out=w[:, lo:hi], in0=e[:, lo:hi], scalar=col, in1=src, op0=ALU.mult, op1=ALU.mult)
                    if i < 3:
                        step(ins)
                ins.then_inc(w_ready, 1)

            def gather_heads(q):
                R.arrived(dve, f"yp{q}")
                R.drained(f"yp{q}", dve.scalar_tensor_tensor(out=cat[:, 4 + q, :], in0=xsT[:, q, L:NT], scalar=dcol[:, q:q + 1],
                                                            in1=pair(f"yp{q}", L), op0=ALU.mult, op1=ALU.add))

            dve.wait_ge(conv_silu, 4)
            exponents(0)
            for h in range(8):
                if h + 1 < 8:
                    if h + 1 >= 2:
                        dve.wait_ge(w_ready, h)
                    exponents(h + 1)
                weights(h)
                if h % 2:
                    gather_heads(h // 2)
            R.emptied(dve, "yp3")
            R.emptied(dve, "yp2")
            R.emptied(dve, "z0")
            R.emptied(dve, "z1")
            run(dve.tensor_tensor(cat[:, 4:8, :], cat[:, 4:8, :], sz, ALU.mult))
            dve.tensor_tensor(ssq, cat[:, 4:8, :], cat[:, 4:8, :], ALU.mult).then_inc(ssq_ready, 1)
            s2 = ssq.rearrange("p a b -> p (a b)")
            R.arrived(dve, "sn")
            R.drained("sn", dve.tensor_scalar(s2[:, 0:512], pair("sn", 512), 1.0 / 256, EPS, ALU.mult, ALU.add))
            dve.wait_ge(sn_std, 1)
            run(dve.reciprocal(s2[:, 0:512], s2[:, 512:1024]))
            for q in range(4):
                step(dve.scalar_tensor_tensor(out=cat[:, 4 + q, :], in0=cat[:, 4 + q, :], scalar=B(68 + q),
                                              in1=s2[:, q // 2 * 256:q // 2 * 256 + 256], op0=ALU.mult, op1=ALU.mult))
            settle()

            R.arrived(dve, "gz")
            z2 = gz.rearrange("p a b -> p (a b)")
            R.drained("gz", dve.tensor_tensor(gz, pair("gz").rearrange("p (a b) -> p a b", a=4),
                                              gbb.unsqueeze(1).to_broadcast([P, 4, 256]), ALU.add))
            R.emptied(dve, "gz")
            dve.scalar_tensor_tensor(out=gzt, in0=gz, scalar=-1.0, in1=gz, op0=ALU.mult, op1=ALU.min).then_inc(gz_abs, 1)
            dve.wait_ge(gz_exp, 2)
            run(dve.scalar_tensor_tensor(out=gz, in0=gz, scalar=0.0, in1=gzt, op0=ALU.min, op1=ALU.subtract))
            dve.tensor_scalar(z2, z2, 1.0 / 16, None, ALU.mult).then_inc(g_ready, 1)
            R.emptied(dve, "gs")
            R.emptied(dve, "gk")
            dve.tensor_tensor(gkw.rearrange("p a (d c) -> p a d c", d=2), gE.rearrange("p a (d c) -> p a d c", d=2),
                              gkt.unsqueeze(2).to_broadcast([P, 2, 2, P]), ALU.mult).then_inc(gkw_ready, 1)
            R.arrived(dve, "gS")
            R.drained("gS", dve.tensor_tensor(gSt, pair("gS", 512).rearrange("p (a b) -> p a b", a=2),
                                              Cb(C_GBLK, 2).unsqueeze(1).to_broadcast([P, 2, 256]), ALU.mult))
            dve.wait_ge(qi_exp, 1)
            dve.tensor_tensor(qI, qI, KQ[:, 1:2, :].to_broadcast([P, 2, L]), ALU.mult).then_inc(qi_ready, 1)
            for i, b in enumerate((P,) + NC_LEVELS):
                nb = L // (2 * b)
                F_ = gcum[:, 0, :].rearrange("p (n h w) -> p n h w", n=nb, h=2)
                B_ = gcum[:, 1, :].rearrange("p (n h w) -> p n h w", n=nb, h=2)
                arg = lv[:, i % 2, :].rearrange("p (x n h w) -> p x n h w", x=2, n=nb, h=2)
                mid_f = F_[:, :, 0, b - 1:b].to_broadcast([P, nb, b])
                mid_b = B_[:, :, 1, 0:1].to_broadcast([P, nb, b])
                if i >= 2:
                    dve.wait_ge(lk_ready, i - 1)
                step(dve.tensor_tensor(arg[:, 0, :, 0, :], mid_f, F_[:, :, 0, :], ALU.subtract))
                step(dve.tensor_tensor(arg[:, 0, :, 1, :], mid_b, B_[:, :, 1, :], ALU.subtract))
                step(dve.tensor_tensor(arg[:, 1, :, 0, :], B_[:, :, 0, :], mid_b, ALU.subtract))
                dve.tensor_tensor(arg[:, 1, :, 1, :], F_[:, :, 1, :], mid_f, ALU.subtract).then_inc(lv_arg, 1)
                if i == 0:
                    for part, (h0, h1) in (("a", (0, 1)), ("b", (2, 3))):
                        R.arrived(dve, f"l0{part}")
                        for hh, h in enumerate((h0, h1)):
                            src = pair(f"l0{part}")[:, 512 * hh:512 * hh + 256].rearrange("p (i t) -> p i t", i=2)
                            for ti in range(2):
                                ins = dve.tensor_tensor(att[:, h, ti, ti * P:ti * P + P], src[:, ti, :], Cb(C_DIAG2), ALU.mult)
                                if not (hh and ti):
                                    step(ins)
                        R.drained(f"l0{part}", ins)
                        R.emptied(dve, f"l0{part}")
                dve.wait_ge(lv_exp, i + 1)
                if i >= 2:
                    R.arrived(dve, f"l{i - 1}b")
                dve.tensor_tensor(lk[:, i % 2, :], lv[:, i % 2, :], KQ.rearrange("p a b -> p (a b)"), ALU.mult)\
                   .then_inc(lk_ready, 1)
                if i >= 1:
                    level_out(dve, i, step, settle)
            level_out(dve, 8, step, settle)
            R.arrived(dve, "go")
            R.drained("go", dve.tensor_copy(gO.rearrange("p a b -> p (a b)"), pair("go", 512)))
            R.emptied(dve, "go")
            dve.tensor_tensor(gsq, gO, gO, ALU.mult).then_inc(gsq_ready, 1)
            R.arrived(dve, "gn")
            R.drained("gn", dve.tensor_scalar(gsq.rearrange("p a b -> p (a b)"), pair("gn", 512), 1.0 / 64, EPS, ALU.mult, ALU.add))
            dve.wait_ge(gn_std, 1)
            run(dve.reciprocal(gsq, gsq))
            for q in range(2):
                step(dve.scalar_tensor_tensor(out=gO[:, q, :], in0=gO[:, q, :], scalar=B(72 + q), in1=gsq[:, q, :], op0=ALU.mult, op1=ALU.mult))
            settle()
            dve.tensor_tensor(cat[:, 0:2, :], gO, gog, ALU.mult).then_inc(gla_done, 1)
            dve.wait_ge(gla_done, 1)

            for i in range(2):
                R.arrived(dve, f"rz{i}")
                ins = dve.tensor_tensor(lw[:, 2 * i:2 * i + 2, :], pair(f"rz{i}").rearrange("p (a b) -> p a b", a=2),
                                        w0b.unsqueeze(1).to_broadcast([P, 2, 512]), ALU.add)
                R.drained(f"rz{i}", ins)
            for c in range(2):
                step(dve.tensor_scalar(kk[:, c, :], kT[:, c, :], B(18 + c), None, ALU.mult))
            settle()
            dve.tensor_tensor(al[0], kk, kk, ALU.mult).then_inc(kk_sq, 1)
            run(dve.tensor_copy(al[1], kk))
            dve.wait_ge(rz_sig, 1)
            dve.tensor_scalar(lw, lw, -DECAY, None, ALU.mult).then_inc(lw_ready, 1)
            R.arrived(dve, "rkn")
            R.drained("rkn", dve.tensor_scalar(kk.rearrange("p a b -> p (a b)"), pair("rkn"), 1e-12, None, ALU.add))
            dve.wait_ge(kk_std, 1)
            run(dve.reciprocal(kk, kk))
            run(dve.tensor_tensor(kk, kk, al[1], ALU.mult))
            R.emptied(dve, "ra")
            for c in range(2):
                step(dve.tensor_scalar(al[1][:, c, :], ba[:, c, :], -1.0, B(20 + c), ALU.add, ALU.mult))
            settle()
            step(dve.scalar_tensor_tensor(out=kT, in0=al[1], scalar=1.0, in1=kT, op0=ALU.add, op1=ALU.mult))
            run(dve.tensor_tensor(ba, ba, kk, ALU.mult))
            for c in range(2):
                ins = dve.scalar_tensor_tensor(out=bon[:, c, :], in0=rT[:, c, :], scalar=B(22 + c), in1=kT[:, c, L:NT], op0=ALU.mult, op1=ALU.mult)
                if c == 0:
                    step(ins)
            ins.then_inc(rw_pre, 1)
            R.arrived(dve, "rb")
            R.drained("rb", dve.tensor_tensor(bon, pair("rb", 512).rearrange("p (a b) -> p a b", a=2), vT[:, :, L:NT], ALU.mult))

            masks = [dict(strict_t=Cb(C_BTX), strict=Cb(C_BTXB), incl=Cb(C_BTI)), dict(strict_t=Cb(C_BTXB), strict=Cb(C_BTX), incl=Cb(C_BTIB))]
            bc4 = lambda m: m.unsqueeze(1).to_broadcast([P, 4, P])
            for tt in range(4):
                cols = slice(tt * P, tt * P + P)
                lat = tt >= 2
                lcols = slice((tt - 2) * P, (tt - 1) * P)
                for d in range(2):
                    R.emptied(dve, f"cu{tt}{d}")
                    if tt:
                        R.arrived(dve, f"BM{tt - 1}{d}")
                        if lat:
                            R.arrived(dve, f"BV{tt - 1}{d}")
                    EP, EM, EX = eb[d][:, 0], eb[d][:, 1], eb[d][:, 2]
                    step(dve.tensor_tensor(al[d][:, :, cols], kk[:, :, cols], EX, ALU.mult))
                    step(dve.scalar_tensor_tensor(out=be[d], in0=ba[:, :, cols], scalar=-1.0, in1=EM, op0=ALU.mult, op1=ALU.mult))
                    if lat:
                        step(dve.tensor_tensor(rho[d][:, :, lcols], rT[:, :, lcols], EP, ALU.mult))
                    at = 63 if d == 0 else 0
                    step(dve.tensor_copy(wc[d][:, :, 2 * tt:2 * tt + 2], EP[:, :, at:at + 65:64]))
                    dve.tensor_tensor(ka[d], kT[:, :, cols], EM, ALU.mult).then_inc(rw_in, 1)
                view = lambda name: pair(name).rearrange("p (o x t) -> p o x t", o=4, x=2)
                for d in range(2):
                    name = f"AA{tt}{d}"
                    R.arrived(dve, name)
                    step(dve.tensor_tensor(XX[d][:, :, 0, :], view(name)[:, :, 0, :], bc4(masks[d]["strict_t"]), ALU.mult))
                    R.drained(name, dve.tensor_tensor(XX[d][:, :, 1, :], view(name)[:, :, 1, :], bc4(masks[d]["strict"]), ALU.mult))
                    settle()
                    step(dve.tensor_tensor(TT[d][:, tt], XX[d][:, :, 0, :], bc4(Cb(C_ID)), ALU.add))
                for d in range(2):
                    name = f"BM{tt}{d}"
                    R.arrived(dve, name)
                    if tt:
                        R.arrived(dve, f"BV{tt - 1}{d}")
                    R.drained(name, dve.tensor_tensor(bm[d], view(name)[:, :, 0, :], bc4(masks[d]["strict_t"]), ALU.mult))
                if lat:
                    for d in range(2):
                        name = f"MM{tt}{d}"
                        R.arrived(dve, name)
                        step(dve.tensor_tensor(mb[d][:, tt - 2], view(name)[:, :, 0, :], bc4(masks[d]["incl"]), ALU.mult))
                        R.drained(name, dve.tensor_tensor(mk[d], view(name)[:, :, 1, :], bc4(masks[d]["incl"]), ALU.mult))
                for d in range(2):
                    name = f"BV{tt}{d}"
                    R.arrived(dve, name)
                    ins = dve.tensor_copy(BVs[d][:, tt, :], pair(name, 256))
                    if lat:
                        step(ins)
                        src = pair(name)[:, 512:768].rearrange("p (a b) -> p a b", a=2)
                        if d == 0:
                            ins = dve.tensor_copy(oT[:, :, lcols], src)
                        else:
                            R.emptied(dve, f"BV{tt}0")
                            ins = dve.tensor_tensor(oT[:, :, lcols], oT[:, :, lcols], src, ALU.add)
                    R.drained(name, ins)
                for j in range(5):
                    for d in range(2):
                        name = f"D{j}{tt}{d}"
                        R.arrived(dve, name)
                        R.drained(name, dve.tensor_copy(XX[d][:, :, 1, :], pair(name)[:, 512:1024].rearrange("p (o t) -> p o t", o=4)))
                    for d in range(2):
                        name = f"T{j}{tt}{d}"
                        R.arrived(dve, name)
                        settle()
                        if j:
                            R.emptied(dve, f"T{j - 1}{tt}{d}")
                        R.drained(name, dve.tensor_tensor(TT[d][:, tt], TT[d][:, tt], pair(name, 512).rearrange("p (o t) -> p o t", o=4), ALU.add))
            R.emptied(dve, "BV30")
            R.emptied(dve, "BV31")
            for i in range(8):
                for d in range(2):
                    ch = i if d == 0 else BWD_ORDER[i]
                    tt, q = ch // 2, ch % 2
                    rows = slice(64 * q, 64 * q + 64)
                    name = f"R1{i}{d}"
                    R.arrived(dve, name)
                    R.drained(name, dve.tensor_tensor(
                        RH[d][rows, :].rearrange("p (b s c) -> p b s c", b=2, s=2),
                        pair(name).rearrange("p (b s c) -> p b s c", b=2, s=8)[rows, :, 0:2, :],
                        BVs[d][rows, tt, :].rearrange("p (b s c) -> p b s c", b=2, s=2), ALU.add))
                if i >= 4:
                    for d in range(2):
                        ch = i if d == 0 else BWD_ORDER[i]
                        tcol = slice((ch - 4) * 64, (ch - 3) * 64)
                        name = f"RO{i}{d}"
                        R.arrived(dve, name)
                        if i >= 5:
                            R.emptied(dve, f"RO{i - 1}{1 - d}")
                        for p in range(2):
                            half = slice(64 * p, 64 * p + 64)
                            src = pair(name)[half, 512 * p:512 * p + 128].rearrange("p (s t) -> p s t", s=2)
                            ins = dve.tensor_tensor(oT[half, :, tcol], oT[half, :, tcol], src, ALU.add)
                            if p == 0:
                                step(ins)
                        R.drained(name, ins)
                for d in range(2):
                    ch = i if d == 0 else BWD_ORDER[i]
                    name = f"R3{i}{d}"
                    R.arrived(dve, name)
                    if i:
                        dve.wait_ge(st_ready[d], i)
                    else:
                        dve.wait_ge(zeroed, 2)
                    R.drained(name, dve.tensor_tensor(ST[d], ST[d], pair(name, 128).rearrange("p (s c) -> p s c", s=2), ALU.add))
                    R.emptied(dve, name)
                    dve.tensor_tensor(ST[d], ST[d], wc[d][:, :, ch:ch + 1].to_broadcast([P, 2, 64]), ALU.mult).then_inc(st_ready[d], 1)
            R.arrived(dve, "RU")
            R.emptied(dve, "RO70")
            R.emptied(dve, "RO71")
            R.drained("RU", dve.tensor_tensor(oT, oT, pair("RU", 512).rearrange("p (a b) -> p a b", a=2), ALU.add))
            R.emptied(dve, "RU")
            R.arrived(dve, "rm")
            flat = lambda ap: ap.rearrange("p a b -> p (a b)")
            R.drained("rm", dve.scalar_tensor_tensor(out=flat(oT), in0=pair("rm", 512), scalar=-1.0 / 64, in1=flat(oT), op0=ALU.mult, op1=ALU.add))
            R.emptied(dve, "rm")
            dve.tensor_tensor(osq, flat(oT), flat(oT), ALU.mult).then_inc(osq_ready, 1)
            R.arrived(dve, "rv2")
            R.drained("rv2", dve.tensor_scalar(bon_tmp, pair("rv2", 512), 1.0 / 64, 64e-5, ALU.mult, ALU.add))
            dve.wait_ge(o_std, 1)
            run(dve.reciprocal(bon_tmp, bon_tmp))
            run(dve.tensor_tensor(flat(oT), flat(oT), bon_tmp, ALU.mult))
            for c in range(2):
                step(dve.tensor_scalar(oT[:, c, :], oT[:, c, :], B(24 + c), B(26 + c), ALU.mult, ALU.add))
            settle()
            run(dve.tensor_tensor(oT, oT, bon, ALU.add))
            R.emptied(dve, "rg")
            dve.tensor_tensor(cat[:, 2:4, :], oT, rgt, ALU.mult).then_inc(cat_ready, 1)
            dve.wait_ge(cat_ready, 1)

            for i in range(2):
                R.arrived(dve, f"w{i}")
                for j in range(4):
                    k = 4 * i + j
                    ins = dve.scalar_tensor_tensor(out=xT[:, k, :], in0=pair(f"w{i}")[:, L * j:L * j + L], scalar=mod[:, 16 + k, 0:1],
                                                   in1=xT[:, k, :], op0=ALU.mult, op1=ALU.add)
                    if j < 3:
                        step(ins)
                R.drained(f"w{i}", ins)
            settle()
            R.emptied(dve, "w1")
            R.emptied(dve, "w0")
            dve.tensor_tensor(sq2, flat(xT), flat(xT), ALU.mult).then_inc(x2_sq, 1)
            for j in range(8):
                step(dve.tensor_scalar(dg[:, j, :], Cb(C_ID), mod[:, 40 + j, 0:1], None, ALU.mult))
                ins = dve.tensor_scalar(dg[:, 8 + j, :], Cb(C_ID), pc[:, 80 + j:81 + j], None, ALU.mult)
                if j < 7:
                    step(ins)
            ins.then_inc(dg_ready, 1)
            R.arrived(dve, "n2")
            R.drained("n2", dve.tensor_scalar(r2, pair("n2", L), 1.0 / D, EPS, ALU.mult, ALU.add))
            dve.wait_ge(n2_std, 1)
            run(dve.reciprocal(r2, r2))
            run(dve.tensor_tensor(h2T, xT, r2.unsqueeze(1).to_broadcast([P, KD, L]), ALU.mult))
            for k in range(KD):
                ins = dve.tensor_scalar(h2T[:, k, :], h2T[:, k, :], A2[:, k:k + 1], mod[:, 24 + k, 0:1], ALU.mult, ALU.add)
                if k < KD - 1:
                    step(ins)
            ins.then_inc(h2_ready, 1)

            R.arrived(dve, "rt")
            R.drained("rt", dve.tensor_tensor(lgt, pair("rt", 64).rearrange("p (a b) -> p a b", a=2), rbb.unsqueeze(1).to_broadcast([P, 2, E]), ALU.add))
            R.emptied(dve, "rt")
            for i in range(2):
                step(dve.max(top8[:, i, :], lgt[:, i, :]))
            settle()
            bce = lambda c: c.to_broadcast([P, 2, E])
            dve.tensor_tensor(rt1, lgt, bce(top8[:, :, 0:1]), ALU.subtract).then_inc(rt_max, 1)
            run(dve.tensor_tensor(rt2, lgt, bce(top8[:, :, 3:4]), ALU.is_gt))
            run(dve.tensor_tensor(rt3, lgt, bce(top8[:, :, 3:4]), ALU.is_equal))
            run(dve.tensor_reduce(small[:, 30:32], rt2, mybir.AxisListType.X, ALU.add))
            run(dve.tensor_scalar(small[:, 30:32], small[:, 30:32], -1.0, float(TOPK), ALU.mult, ALU.add))
            run(dve.tensor_copy(rt4, rt3))
            src, dst = rt4, spos
            for sh in (1, 2, 4, 8, 16):
                step(dve.tensor_tensor(dst[:, :, sh:E], src[:, :, sh:E], src[:, :, 0:E - sh], ALU.add))
                run(dve.tensor_copy(dst[:, :, 0:sh], src[:, :, 0:sh]))
                src, dst = dst, src
            run(dve.tensor_tensor(src, src, bce(small[:, 30:32].unsqueeze(2)), ALU.is_le))
            run(dve.tensor_tensor(rt3, rt3, src, ALU.mult))
            dve.tensor_tensor(rt2, rt2, rt3, ALU.add).then_inc(mask_ready, 1)
            dve.wait_ge(mask_ready, 1)
            dve.tensor_copy(msk3.rearrange("p a (r e) -> p a r e", r=3), rt2.unsqueeze(2).to_broadcast([P, 2, 3, E])).then_inc(mask_ready, 1)
            dve.wait_ge(rt_exp, 1)
            run(dve.tensor_tensor(gates, rt1, rt2, ALU.mult))
            run(dve.tensor_reduce(small[:, 34:36], gates, mybir.AxisListType.X, ALU.add))
            run(dve.reciprocal(small[:, 34:36], small[:, 34:36]))
            dve.tensor_tensor(gates, gates, bce(small[:, 34:36].unsqueeze(2)), ALU.mult).then_inc(gates_ready, 1)
            R.arrived(dve, "pos")
            R.drained("pos", dve.scalar_tensor_tensor(out=spos, in0=pair("pos", 64).rearrange("p (a b) -> p a b", a=2), scalar=1.0, in1=rt2, op0=ALU.add, op1=ALU.mult))
            R.emptied(dve, "pos")
            run(dve.tensor_scalar(spos, spos, -1.0, None, ALU.add))
            R.arrived(dve, "gt")
            R.drained("gt", dve.tensor_copy(gT[0:E, :], pair("gt", L)[0:E, :]))
            cd = cand[0:96, :]
            lastc = C[:, C_IOTA, :]
            R.arrived(dve, "cnd")
            R.drained("cnd", dve.tensor_scalar(cd[:, 0:1], pair("cnd", 1)[0:96, :], lastc[0:96, 66:67], None, ALU.is_gt))
            R.arrived(dve, "idx")
            R.drained("idx", dve.tensor_copy(cd[:, 1:2], pair("idx", 1)[0:96, :]))
            R.emptied(dve, "idx")
            dve.tensor_scalar(onehot[0:96, :], lastc[0:96, 0:EXTRA], cd[:, 1:2], cd[:, 0:1], ALU.is_equal, ALU.mult).then_inc(onehot_ready, 1)
            R.arrived(dve, "lst")
            step(dve.tensor_copy(ints[:, 0:1], pair("lst", 1)))
            step(dve.tensor_copy(ints[:, 8:8 + EXTRA], pair("lst", 64)[:, 16:16 + EXTRA]))
            dve.wait_ge(zeroed, 3)
            R.drained("lst", dve.tensor_copy(ibase[:, E:E + EXTRA], pair("lst", 64)[:, 32:32 + EXTRA]))

            def expert(n, e):
                k = 4

                def mark(i, ins, other=None):
                    ins.then_inc(other or moe_vec, 1)
                    if other:
                        dve.wait_ge(other, n + 1)
                    else:
                        dve.wait_ge(moe_vec, n * k + i)

                dve.wait_ge(sw_ready, n + 1)
                for i in range(2):
                    mark(1 + i, dve.tensor_scalar(sel[:, i, :], lastc[:, 0:SLOTS], ibase[:, bass.ds(n, 1)], spos[:, i, bass.ds(e, 1)], ALU.add, ALU.is_equal))
                for i in range(2):
                    ins = dve.tensor_scalar(selw[:, i, :, :], sel[:, i:i + 1, :].to_broadcast([P, 2, SLOTS]), gates[:, i, bass.ds(e, 1)], None, ALU.mult)
                    ins.then_inc(sel_ready, 1)
                mark(3, dve.tensor_copy(this_e[0:E, :], C[0:E, C_ID, bass.ds(e, 1)].to_broadcast([E, SLOTS])), te_ready)
                dve.wait_ge(slot_free[7], n + base[7] + 1)
                mark(4, dve.tensor_scalar(glu, PS[:, 0, :], LIMIT, None, ALU.min), glu_ready)
                mark(3, dve.tensor_scalar(lin, PS[:, 1, :], LIMIT, -LIMIT, ALU.min, ALU.max))
                mark(4, dve.scalar_tensor_tensor(out=lin, in0=lin, scalar=1.0, in1=glu, op0=ALU.add, op1=ALU.mult))
                dve.wait_ge(sig_ready, n + 1)
                dve.tensor_tensor(act_, lin, sgm, ALU.mult).then_inc(act_ready, 1)

            with dve.Fori(0, E) as n:
                expert(n, n)
            extra = dve.value_load(ints[0:1, 0:1], min_val=0, max_val=EXTRA)
            with dve.If(extra > 0):
                with dve.Fori(0, extra) as j:
                    e = dve.value_load(ints[0:1, bass.ds(j + 8, 1)], min_val=0, max_val=E - 1)
                    expert(j + E, e)
            dve.wait_ge(scattered, 1)
            for name in ("m5", "fg", "xk0", "xk1"):
                R.emptied(dve, name)
            for i in range(2):
                y = PS[:, 4 + 2 * i:6 + 2 * i, :].rearrange("p a b -> p (a b)")
                run(dve.tensor_tensor(h2T.rearrange("p a b -> p (a b)")[:, 1024 * i:1024 * i + 1024], y, m5r, ALU.mult))
                dve.tensor_tensor(xk[:, i, :], xk[:, i, :], h2T.rearrange("p a b -> p (a b)")[:, 1024 * i:1024 * i + 1024], ALU.add).then_inc(y_read, 1)
            dve.wait_ge(f_sq, 2)
            dve.tensor_scalar(small[:, 16:18], small[:, 16:18], 1.0 / D, EPS, ALU.mult, ALU.add).then_inc(f_var, 1)
            dve.wait_ge(f_std, 1)
            run(dve.reciprocal(small[:, 42:44], small[:, 18:20]))
            for i in range(2):
                dve.scalar_tensor_tensor(out=xk[:, i, :], in0=xk[:, i, :], scalar=small[:, 42 + i:43 + i], in1=fgr, op0=ALU.mult, op1=ALU.mult).then_inc(out_ready, 1)

        @block.tensor
        def _(pe):
            owed = []

            def mm(out, lhsT, rhs, start=True, stop=True, skip=False):
                ins = pe.matmul(out, lhsT, rhs, start=start, stop=stop, skip_group_check=skip)
                return ins

            def pay(ins):
                if owed:
                    ins.then_inc(owed.pop(0), 1)
                return ins

            ident = Cb(C_ID)
            pe.wait_ge(rows_in, 16 * N_ROWS)
            pe.wait_ge(consts_in, 16)
            pe.transpose(pair("prm")[:, 0:88], prow[0:88, 0, :], ident[0:88, 0:88])
            R.filled("prm", pe.transpose(pair("prm")[:, 128:202], prow[0:74, 1, :], ident[0:74, 0:74]))
            pe.wait_ge(silu_c, 1)
            for n in range(24):
                s, nth = place["ada", n]
                pe.wait_ge(slot_full[s], 16 * nth)
                for m in range(16):
                    col = 2 * (n % 3 * 16 + m)
                    ins = mm(pair("ada")[:, col:col + 2], slots[s][:, m * P:m * P + P], csil[:, n // 3, :],
                             start=n == 0 and m == 0, stop=n >= 21, skip=True)
                if n < 23:
                    ins.then_inc(slot_free[s], 1)
            R.filled("ada", ins)
            owed.append(slot_free[s])
            pe.wait_ge(diag_ready, 4)
            pe.wait_ge(x_in, 32)
            for i in range(4):
                R.claim(pe, f"h{i}")
                for j in range(2):
                    k = 2 * i + j
                    for t in range(4):
                        ins = mm(pair(f"h{i}")[:, 512 * j + t * P:512 * j + t * P + P], xtok[:, t, k * P:k * P + P], diagR[:, t, :])
                        if not (j == 1 and t == 3):
                            pay(ins)
                R.filled(f"h{i}", ins)
            for i in range(2):
                R.claim(pe, f"x{i}")
                for j in range(4):
                    k = 4 * i + j
                    for t in range(2):
                        ins = pe.transpose(pair(f"x{i}")[:, L * j + t * P:L * j + t * P + P], xtok[:, 2 + t, k * P:k * P + P], ident)
                R.filled(f"x{i}", ins)
            for i in range(4):
                R.emptied(pe, f"h{i}")
            R.claim(pe, "dt")
            pe.wait_ge(mats_in, 16 * N_MATS)
            for t in range(4):
                for k in range(KD):
                    ins = mm(pair("dt")[:, 16 * t:16 * t + 16], hT[:, k, t * P:t * P + P], dtw[:, k, :], start=k == 0, stop=k == 7)
            R.filled("dt", ins)
            tiles = dict(PROJ)
            for g, (c0, w, names) in enumerate(W_GROUPS):
                s, nth = place["in", g]
                wt = w_in_tile(g)
                pe.wait_ge(slot_full[s], 16 * nth)
                for name in names:
                    R.claim(pe, name)
                    work = tiles[name]
                    for j, (col, m, lat) in enumerate(work):
                        n = L if lat else NT
                        for k in range(KD):
                            ins = mm(pair(name)[0:m, 512 * j:512 * j + n], wt[:, k, col - c0:col - c0 + m], hT[:, k, NT - n:NT],
                                     start=k == 0, stop=k == 7)
                            if not (j == len(work) - 1 and k == 7):
                                pay(ins)
                    R.filled(name, ins)
                owed.append(slot_free[s])

            pe.wait_ge(conv_silu, 4)
            for i in range(2):
                R.claim(pe, f"xst{i}")
                for t in range(2):
                    for c in range(4):
                        ins = pe.transpose(pair(f"xst{i}")[:, 512 * t + c * P:512 * t + c * P + P],
                                           xsT[:, c, (2 * i + t) * P:(2 * i + t + 1) * P], ident)
                        if not (t and c == 3):
                            pay(ins)
                R.filled(f"xst{i}", ins)
            R.claim(pe, "Bt")
            for t in range(2):
                for g in range(2):
                    ins = pe.transpose(pair("Bt")[:, 256 * t + g * P:256 * t + g * P + P], BT[:, g, t * P:t * P + P], ident)
            R.filled("Bt", ins)
            pe.wait_ge(dt_ready, 1)
            R.claim(pe, "cc")
            F, Bw = slice(0, 8), slice(8, 16)
            sums = [(0, F, ((C_TXB, 0), (C_ONE, 1))), (0, Bw, ((C_TX, 0),)), (1, F, ((C_TXB, 1),)), (1, Bw, ((C_TX, 1), (C_ONE, 0))),
                    (2, F, ((C_TI, 2),)), (2, Bw, ((C_TIB, 2), (C_ONE, 3))), (3, F, ((C_TI, 3), (C_ONE, 2))), (3, Bw, ((C_TIB, 3),))]
            for t, cols, terms in sums:
                for i, (m, u) in enumerate(terms):
                    ins = mm(pair("cc")[:, 16 * t + cols.start:16 * t + cols.stop], Cb(m), adt[:, u, cols], start=i == 0, stop=i == len(terms) - 1)
            R.filled("cc", ins)
            pe.wait_ge(xw_ready, 4)
            R.emptied(pe, "Bt")
            R.claim(pe, "st")
            for d in range(2):
                for g in range(2):
                    for t in range(2):
                        ins = mm(pair("st")[:, 512 * d + 256 * g:512 * d + 256 * g + 256], Btok[:, t, g * P:g * P + P],
                                 xw[:, t, d, 256 * g:256 * g + 256], start=t == 0, stop=t == 1)
            R.filled("st", ins)
            R.claim(pe, "sc")
            for g in range(2):
                for t in range(2):
                    ins = mm(pair("sc")[:, 512 * g + 256 * t:512 * g + 256 * t + 256], BT[:, g, L + t * P:L + t * P + P], CT[:, g, :])
            R.filled("sc", ins)

            def running_sums(h):
                name = f"dc{h}"
                R.claim(pe, name)
                out = pair(name)
                for d, (u1, u2, m1, m2, lo) in enumerate(((2, 3, C_TI, C_TI, P), (3, 2, C_ONE, C_TIB, 0))):
                    col = 8 * d + h
                    mm(out[:, 256 * d:256 * d + 256], adt[:, u1, col:col + 1].to_broadcast([P, P]), Cb(m1, 2), stop=False)
                    ins = mm(out[:, 256 * d + lo:256 * d + lo + P], adt[:, u2, col:col + 1].to_broadcast([P, P]), Cb(m2), start=False)
                R.filled(name, ins)

            running_sums(0)
            R.emptied(pe, "st")
            for q in range(4):
                running_sums(2 * q + 1) if q == 0 else None
                for hh in range(2):
                    h = 2 * q + hh
                    if h + 2 < 8 and False:
                        pass
                    pe.wait_ge(w_ready, h + 1)
                    if hh == 0:
                        R.claim(pe, f"yp{q}")
                    out = pair(f"yp{q}")[64 * hh:64 * hh + 64, :]
                    w, ci = WD[:, h % 2, :], CI[:, h % 2, :]
                    x2_, x3_ = xtk[:, 2, 64 * h:64 * h + 64], xtk[:, 3, 64 * h:64 * h + 64]
                    mm(out[:, 0:256], x2_, w[:, 0:256], stop=False, skip=True)
                    mm(out[:, 128:256], x3_, w[:, 256:384], start=False, stop=False, skip=True)
                    mm(out[:, 0:128], x2_, w[:, 384:512], start=False, stop=False, skip=True)
                    mm(out[:, 0:256], x3_, w[:, 512:768], start=False, stop=False, skip=True)
                    mm(out[:, 0:256], Sst[:, 0, 64 * h:64 * h + 64], ci[:, 0:256], start=False, stop=False, skip=True)
                    ins = mm(out[:, 0:256], Sst[:, 1, 64 * h:64 * h + 64], ci[:, 256:512], start=False, skip=True)
                    if hh == 0 and q < 3:
                        running_sums(h + 2)
                R.filled(f"yp{q}", ins)
                if q < 3:
                    running_sums(2 * q + 3)
            pe.wait_ge(ssq_ready, 1)
            R.claim(pe, "sn")
            for g in range(2):
                for t in range(2):
                    ins = mm(pair("sn")[:, 256 * g:256 * g + 256], Cb(C_ONE), ssq[:, 2 * g + t, :], start=t == 0, stop=t == 1)
            R.filled("sn", ins)

            R.emptied(pe, "lg")
            R.claim(pe, "gz")
            for t in range(4):
                ins = mm(pair("gz")[:, 256 * t:256 * t + 256], lgT[0:32, t * P:t * P + P], gwb[0:32, :])
            R.filled("gz", ins)
            pe.wait_ge(g_ready, 1)
            R.claim(pe, "gs")
            for t, d, terms in ((0, 0, ((C_TXB, 0), (C_ONE, 1))), (0, 1, ((C_TX, 0),)), (1, 0, ((C_TXB, 1),)), (1, 1, ((C_TX, 1), (C_ONE, 0)))):
                for i, (m, u) in enumerate(terms):
                    ins = mm(pair("gs")[:, 256 * t + P * d:256 * t + P * d + P], Cb(m), gz[:, u, P * d:P * d + P], start=i == 0, stop=i == len(terms) - 1)
            R.filled("gs", ins)
            R.emptied(pe, "gq")
            R.claim(pe, "gk")
            for t in range(2):
                ins = pe.transpose(pair("gk")[:, t * P:t * P + P], gkc[:, t * P:t * P + P], ident)
            R.filled("gk", ins)
            R.emptied(pe, "gv")
            R.claim(pe, "gvt")
            for t in range(4):
                for c in range(2):
                    ins = pe.transpose(pair("gvt")[:, 256 * t + c * P:256 * t + c * P + P], gvT[:, c, t * P:t * P + P], ident)
            R.filled("gvt", ins)
            R.claim(pe, "gc")
            for d, (u1, u2, m1, m2, lo) in enumerate(((2, 3, C_TI, C_TI, P), (3, 2, C_ONE, C_TIB, 0))):
                mm(pair("gc")[:, 256 * d:256 * d + 256], gz[:, u1, P * d:P * d + P], Cb(m1, 2), stop=False)
                ins = mm(pair("gc")[:, 256 * d + lo:256 * d + lo + P], gz[:, u2, P * d:P * d + P], Cb(m2), start=False)
            R.filled("gc", ins)
            pe.wait_ge(gkw_ready, 1)
            R.emptied(pe, "gvt")
            R.claim(pe, "gS")
            for d in range(2):
                for t in range(2):
                    ins = mm(pair("gS")[:, 256 * d:256 * d + 256], gkw[:, t, P * d:P * d + P], gvk[:, t, :], start=t == 0, stop=t == 1)
            R.filled("gS", ins)
            for i in range(9):
                if i:
                    pe.wait_ge(lk_ready, i)
                src = KQ if i == 0 else lk[:, (i - 1) % 2, :].rearrange("p (x t) -> p x t", x=2)
                for part, h0 in (("a", 0), ("b", 2)):
                    R.claim(pe, f"l{i}{part}")
                    for hh in range(2):
                        rows = slice(32 * (h0 + hh), 32 * (h0 + hh) + 32)
                        for s in range(2):
                            t = 1 - s if i == 1 else s
                            ins = mm(pair(f"l{i}{part}")[:, 512 * hh + s * P:512 * hh + s * P + P], src[rows, 0, s * P:s * P + P], src[rows, 1, t * P:t * P + P])
                    R.filled(f"l{i}{part}", ins)
            pe.wait_ge(qi_ready, 1)
            R.emptied(pe, "gS")
            R.emptied(pe, "l8a")
            R.emptied(pe, "l8b")
            R.claim(pe, "go")
            for q in range(2):
                for p in range(2):
                    h = 2 * q + p
                    for t in range(2):
                        mm(pair("go")[64 * p:64 * p + 64, 256 * q:256 * q + 256], gvk[:, 2 + t, 64 * h:64 * h + 64], att[:, h, t, :],
                           start=t == 0, stop=False, skip=True)
                for d in range(2):
                    ins = mm(pair("go")[:, 256 * q:256 * q + 256], gSt[:, d, P * q:P * q + P], qI[:, d, :], start=False, stop=d == 1, skip=True)
            R.filled("go", ins)
            pe.wait_ge(gsq_ready, 1)
            R.claim(pe, "gn")
            R.filled("gn", mm(pair("gn", 512), Cb(C_HEAD), gsq.rearrange("p a b -> p (a b)")))

            pe.wait_ge(rw_tanh, 1)
            for i in range(2):
                R.claim(pe, f"rz{i}")
                for t in range(2):
                    ins = mm(pair(f"rz{i}")[:, 512 * t:512 * t + 512], lowT[0:64, (2 * i + t) * P:(2 * i + t + 1) * P], W2A[0:64, :])
                R.filled(f"rz{i}", ins)
            R.emptied(pe, "low")
            R.claim(pe, "ra")
            for c in range(2):
                ins = mm(pair("ra")[:, 512 * c:512 * c + 512], W2A[64:96, c * P:c * P + P], lowT[64:96, :])
            R.filled("ra", ins)
            pe.wait_ge(kk_sq, 1)
            R.claim(pe, "rkn")
            for c in range(2):
                ins = mm(pair("rkn")[:, 512 * c:512 * c + 512], Cb(C_HEAD), al[0][:, c, :])
            R.filled("rkn", ins)
            pe.wait_ge(rw_pre, 1)
            R.claim(pe, "rb")
            R.filled("rb", mm(pair("rb", 512), Cb(C_HEAD), bon.rearrange("p a b -> p (a b)")))
            pe.wait_ge(gate_sig, 1)
            R.claim(pe, "rg")
            for c in range(2):
                ins = mm(pair("rg")[:, 256 * c:256 * c + 256], g2w[0:64, c * P:c * P + P], sgT[0:64, :])
            R.filled("rg", ins)
            R.emptied(pe, "rv")
            R.claim(pe, "rvt")
            for t in range(4):
                for c in range(2):
                    ins = pe.transpose(pair("rvt")[:, 256 * t + c * P:256 * t + c * P + P], vT[:, c, t * P:t * P + P], ident)
            R.filled("rvt", ins)
            R.emptied(pe, "rvt")
            pe.wait_ge(lw_ready, 1)
            for tt in range(4):
                cols, lcols = slice(tt * P, tt * P + P), slice((tt - 2) * P, (tt - 1) * P)
                for d in range(2):
                    R.claim(pe, f"cu{tt}{d}")
                    for c in range(2):
                        ins = mm(pair(f"cu{tt}{d}")[:, 256 * c:256 * c + 256], lw[:, tt, 256 * d + c * P:256 * d + c * P + P],
                                 Cb(C_BTI if d == 0 else C_BTIB, 2))
                    R.filled(f"cu{tt}{d}", ins)
                for d in range(2):
                    pe.wait_ge(rw_in, 2 * tt + d + 1)
                    R.claim(pe, f"bk{tt}{d}")
                    for x, src in enumerate((be[d], ka[d])):
                        for c in range(2):
                            ins = pe.transpose(pair(f"bk{tt}{d}")[:, 256 * x + c * P:256 * x + c * P + P], src[:, c, :], ident)
                    R.filled(f"bk{tt}{d}", ins)

                def by_heads(name, pairs_):
                    R.claim(pe, name)
                    for h in range(4):
                        half, c, o = slice(64 * (h % 2), 64 * (h % 2) + 64), h // 2, o_of(h)
                        for x, (st, mv) in enumerate(pairs_):
                            ins = mm(pair(name)[:, 256 * o + P * x:256 * o + P * x + P], st[half, c, :], mv[half, c, :])
                    R.filled(name, ins)

                for d in range(2):
                    by_heads(f"AA{tt}{d}", ((be[d], al[d][:, :, cols]), (al[d][:, :, cols], be[d])))
                for d in range(2):
                    by_heads(f"BM{tt}{d}", ((ka[d], al[d][:, :, cols]),))
                if tt >= 2:
                    for d in range(2):
                        by_heads(f"MM{tt}{d}", ((be[d], rho[d][:, :, lcols]), (ka[d], rho[d][:, :, lcols])))
                for d in range(2):
                    R.emptied(pe, f"BM{tt}{d}")
                    if tt >= 2:
                        R.emptied(pe, f"MM{tt}{d}")
                    name = f"BV{tt}{d}"
                    R.claim(pe, name)
                    for h in range(4):
                        o = o_of(h)
                        ins = mm(pair(name)[:, 64 * o:64 * o + 64], bm[d][:, o, :], Vt[:, tt, 64 * h:64 * h + 64])
                    if tt >= 2:
                        for h in range(4):
                            ins = mm(pair(name)[64 * (h % 2):64 * (h % 2) + 64, 512 + P * (h // 2):512 + P * (h // 2) + P],
                                     Vt[:, tt, 64 * h:64 * h + 64], mk[d][:, o_of(h), :])
                    R.filled(name, ins)
                for j in range(5):
                    for d in range(2):
                        name = f"D{j}{tt}{d}"
                        R.emptied(pe, f"AA{tt}{d}" if j == 0 else f"D{j - 1}{tt}{d}")
                        R.claim(pe, name)
                        for o in range(4):
                            XTo, Xo = XX[d][:, o, 0, :], XX[d][:, o, 1, :]
                            ins = mm(pair(name)[:, 512 + P * o:512 + P * o + P], XTo, Xo)
                            if j < 4:
                                ins = mm(pair(name)[:, P * o:P * o + P], Xo, XTo)
                        R.filled(name, ins)
                    for d in range(2):
                        name = f"T{j}{tt}{d}"
                        R.emptied(pe, f"D{j}{tt}{d}")
                        if j:
                            R.emptied(pe, f"T{j - 1}{tt}{d}")
                        R.claim(pe, name)
                        for o in range(4):
                            ins = mm(pair(name)[:, P * o:P * o + P], XX[d][:, o, 1, :], TT[d][:, tt, o, :])
                        R.filled(name, ins)
            pe.wait_ge(zeroed, 2)
            for i in range(8):
                where = [(i // 2, i % 2), (BWD_ORDER[i] // 2, BWD_ORDER[i] % 2)]
                for d in range(2):
                    tt, q = where[d]
                    ch = 2 * tt + q
                    name = f"R1{i}{d}"
                    if i:
                        pe.wait_ge(st_ready[d], i)
                    R.claim(pe, name)
                    for h in range(4):
                        p, c = h % 2, h // 2
                        half = slice(64 * p, 64 * p + 64)
                        ins = mm(pair(name)[64 * q:64 * q + 64, 512 * p + 64 * c:512 * p + 64 * c + 64], al[d][half, c, 64 * ch:64 * ch + 64], ST[d][half, c, :])
                    R.filled(name, ins)
                for d in range(2):
                    tt, q = where[d]
                    rows = slice(64 * q, 64 * q + 64)
                    name = f"R2{i}{d}"
                    R.emptied(pe, f"R1{i}{d}")
                    if i == 0:
                        R.emptied(pe, f"T430")
                        R.emptied(pe, f"T431")
                    R.claim(pe, name)
                    for o in range(4):
                        ins = mm(pair(name)[rows, 64 * o:64 * o + 64], TT[d][rows, tt, o, 64 * q:64 * q + 64], RH[d][rows, 64 * o:64 * o + 64])
                    R.filled(name, ins)
                if i >= 4:
                    for d in range(2):
                        ch = 2 * where[d][0] + where[d][1]
                        name = f"RO{i}{d}"
                        R.claim(pe, name)
                        for h in range(4):
                            p, c = h % 2, h // 2
                            half = slice(64 * p, 64 * p + 64)
                            ins = mm(pair(name)[half, 512 * p + 64 * c:512 * p + 64 * c + 64], ST[d][half, c, :], rho[d][half, c, 64 * (ch - 4):64 * (ch - 3)])
                        R.filled(name, ins)
                for d in range(2):
                    tt, q = where[d]
                    rows = slice(64 * q, 64 * q + 64)
                    name = f"R3{i}{d}"
                    R.emptied(pe, f"R2{i}{d}")
                    R.emptied(pe, f"bk3{d}")
                    R.claim(pe, name)
                    for h in range(4):
                        p, c, o = h % 2, h // 2, o_of(h)
                        out = pair(name)[64 * p:64 * p + 64, 64 * c:64 * c + 64]
                        mm(out, bt[d][rows, tt, 64 * h:64 * h + 64], Us[d][rows, tt % 2, 64 * o:64 * o + 64], stop=False)
                        ins = mm(out, bt[d][rows, tt, 256 + 64 * h:256 + 64 * h + 64], Vt[rows, tt, 64 * h:64 * h + 64], start=False)
                    R.filled(name, ins)
            R.claim(pe, "RU")
            for h in range(4):
                p, c, o = h % 2, h // 2, o_of(h)
                for t in range(2):
                    for d in range(2):
                        ins = mm(pair("RU")[64 * p:64 * p + 64, 256 * c + P * t:256 * c + P * t + P], Us[d][:, t, 64 * o:64 * o + 64],
                                 mb[d][:, t, o, :], start=d == 0, stop=d == 1)
            R.filled("RU", ins)
            R.emptied(pe, "RU")
            R.claim(pe, "rm")
            R.filled("rm", mm(pair("rm", 512), Cb(C_HEAD), oT.rearrange("p a b -> p (a b)")))
            pe.wait_ge(osq_ready, 1)
            R.claim(pe, "rv2")
            R.filled("rv2", mm(pair("rv2", 512), Cb(C_HEAD), osq))

            pe.wait_ge(cat_ready, 1)
            for i in range(2):
                R.claim(pe, f"w{i}")
                for j in range(4):
                    m = 4 * i + j
                    for k in range(KD):
                        s, nth = place["out", k // 2]
                        if m == 0 and k % 2 == 0:
                            pe.wait_ge(slot_full[s], 16 * nth)
                        w = slots[s].rearrange("p (k c) -> p k c", k=2)[:, k % 2, :]
                        ins = mm(pair(f"w{i}")[:, L * j:L * j + L], w[:, m * P:m * P + P], cat[:, k, :], start=k == 0, stop=k == 7)
                R.filled(f"w{i}", ins)
            owed.extend(slot_free[2 + n] for n in range(4))
            pe.wait_ge(x2_sq, 1)
            R.claim(pe, "n2")
            for k in range(KD):
                ins = mm(pair("n2", L), Cb(C_ONE), sq2[:, L * k:L * k + L], start=k == 0, stop=k == 7)
                if k < 7:
                    pay(ins)
            R.filled("n2", ins)
            pe.wait_ge(h2_ready, 1)
            R.claim(pe, "rt")
            for t in range(2):
                for k in range(KD):
                    ins = mm(pair("rt")[:, E * t:E * t + E], h2T[:, k, t * P:t * P + P], rtw[:, k, :], start=k == 0, stop=k == 7)
            R.filled("rt", ins)
            for nm, src in (("hk", h2T), ("xk", xT)):
                for t in range(2):
                    R.claim(pe, f"{nm}{t}")
                    for k in range(KD):
                        ins = pe.transpose(pair(f"{nm}{t}")[:, k * P:k * P + P], src[:, k, t * P:t * P + P], ident)
                    R.filled(f"{nm}{t}", ins)
            pe.wait_ge(dg_ready, 1)
            for x, name in enumerate(("m5", "fg")):
                R.claim(pe, name)
                for k in range(KD):
                    ins = mm(pair(name)[:, k * P:k * P + P], Cb(C_ONE), dg[:, 8 * x + k, :])
                R.filled(name, ins)
            pe.wait_ge(mask_ready, 1)
            R.claim(pe, "pos")
            mm(pair("pos")[:, 0:E], Cb(C_TX), rt2[:, 0, :])
            mm(pair("pos")[:, E:2 * E], Cb(C_ONE), rt2[:, 0, :], stop=False)
            R.filled("pos", mm(pair("pos")[:, E:2 * E], Cb(C_TX), rt2[:, 1, :], start=False))
            pe.wait_ge(late_in, 32)
            pe.wait_ge(gates_ready, 1)
            R.claim(pe, "gt")
            for t in range(2):
                ins = pe.transpose(pair("gt")[0:E, t * P:t * P + P], gates[:, t, :], ident)
            R.filled("gt", ins)
            pe.wait_ge(mask_ready, 2)
            R.claim(pe, "cnd")
            for t in range(2):
                ins = mm(pair("cnd")[0:96, 0:1], msk3[:, t, :], C[:, C_ONE, 0:1], start=t == 0, stop=t == 1)
            R.filled("cnd", ins)
            R.emptied(pe, "cnd")
            R.claim(pe, "idx")
            R.filled("idx", mm(pair("idx")[0:96, 0:1], C[0:96, C_TX, 0:96], cand[0:96, 0:1]))
            pe.wait_ge(onehot_ready, 1)
            R.claim(pe, "lst")
            mm(pair("lst")[:, 0:1], C[0:96, C_ONE, :], cand[0:96, 0:1])
            mm(pair("lst")[:, 16:32], C[0:96, C_IOTA, 64:65].to_broadcast([96, P]), onehot[0:96, :])
            R.filled("lst", mm(pair("lst")[:, 32:48], C[0:96, C_IOTA, 65:66].to_broadcast([96, P]), onehot[0:96, :]))

            R.emptied(pe, "gt")
            for name in ("cnd", "idx", "lst", "fg", "m5"):
                R.emptied(pe, name)
            for t in range(2):
                for half in range(2):
                    ins = mm(PS[:, 4 + 2 * t + half, :], gT[0:E, t * P:t * P + P], bdn[0:E, 512 * half:512 * half + 512], stop=False, skip=True)
            ins.then_inc(y_init, 1)
            pe.wait_ge(zeroed, 3)
            for name in ("hk0", "hk1"):
                R.emptied(pe, name)

            def scatter(last=False):
                for half in range(2):
                    rows = slice(64 * half, 64 * half + 64)
                    for t in range(2):
                        ins = mm(PS[:, 4 + 2 * t + half, :], SW[rows, t * P:t * P + P], ye[rows, :], start=False, stop=last, skip=True)
                return ins

            def expert(n):
                pe.wait_ge(sel_ready, n * 2 + 2)
                for k in range(KD):
                    for t in range(2):
                        ins = mm(PS[:, 2, SLOTS * k:SLOTS * k + SLOTS], h2k[:, t, k * P:k * P + P], sel[:, t, :], start=t == 0, stop=t == 1)
                ins.then_inc(gathered, 1)
                pe.wait_ge(hg_ready, n + 2)
                pe.wait_ge(act_ready, n + 1)
                pe.wait_ge(te_ready, n + 1)
                for x in range(2):
                    for half in range(2):
                        mm(PS[64 * half:64 * half + 64, x, :], this_e[0:E, :], bgrow[0:E, 1024 * x + 512 * half:1024 * x + 512 * half + 512],
                           stop=False, skip=True)
                for k in range(KD):
                    pe.wait_ge(slot_full[k], (n + (base[k] + 1)) * 16)
                    for x in range(2):
                        for half in range(2):
                            ins = mm(PS[64 * half:64 * half + 64, x, :], hg[:, k, :],
                                     slots[k][:, 1024 * x + 512 * half:1024 * x + 512 * half + 512], start=False, stop=k == 7, skip=True)
                    ins.then_inc(slot_free[k], 1)
                pe.wait_ge(ye_ready, n + 1)
                pe.wait_ge(sw_ready, n + 1)
                scatter()
                for t in range(2):
                    ins = pe.transpose(PS[:, 3, t * P:t * P + P], selw[:, t, :, :].rearrange("p a b -> p (a b)"), ident)
                ins.then_inc(selT_done, 1)
                pe.wait_ge(act_ready, n + 2)
                for c in range(4):
                    ins = pe.transpose(PS[:, 2, c * P:c * P + P], act_[:, c * P:c * P + P], ident)
                ins.then_inc(actT_done, 1)
                pe.wait_ge(actT_ready, n + 1)
                pe.wait_ge(sw_ready, n + 2)
                for s in range(8, 12):
                    pe.wait_ge(slot_full[s], (n + (base[s] + 1)) * 16)
                    w = slots[s].rearrange("p (k c) -> p k c", k=2)
                    for k2 in range(2):
                        k = 2 * (s - 8) + k2
                        for half in range(2):
                            ins = mm(PS[64 * half:64 * half + 64, 3, :], actT[:, k % 4, k // 4, :], w[:, k2, 512 * half:512 * half + 512],
                                     start=k == 0, stop=k == 7)
                    ins.then_inc(slot_free[s], 1)

            with pe.Fori(0, E) as n:
                expert(n)
            extra = pe.value_load(ints[0:1, 0:1], min_val=0, max_val=EXTRA)
            with pe.If(extra > 0):
                with pe.Fori(0, extra) as j:
                    expert(j + E)
            pe.wait_ge(ye_ready, extra + (E + 1))
            pe.wait_ge(sw_ready, extra + (E + 1))
            scatter(last=True).then_inc(scattered, 1)


_INS = ["x", "c", "ctx", "c_ctx", "w_ada", "b_ada", "norm1_g", "norm2_g", "w_in", "gla_gate_w", "gla_gate_b", "gla_norm_g",
        "rw_mu", "rw_w0", "rw_w2", "rw_a0", "rw_a2", "rw_g2", "rw_kk", "rw_ka", "rw_rk", "rw_lnx_g", "rw_lnx_b",
        "ssd_conv_w", "ssd_conv_b", "ssd_dt_bias", "ssd_a_log", "ssd_d", "ssd_norm_g", "w_out", "router_w", "router_b",
        "moe_w_gu", "moe_b_gu", "moe_w_down", "moe_b_down", "final_norm_g"]


def kernel(**inputs):
    import concourse.bacc as bacc
    from concourse.bass_utils import run_bass_kernel_spmd

    nc = bacc.Bacc("TRN2", target_bir_lowering=False, num_devices=1)
    arrays, aps = {}, {}
    sent = {name: np.ascontiguousarray(inputs[name]) for name in _INS}
    sent["consts"] = constants()
    for name, value in sent.items():
        arrays[f"in_{name}"] = value
        aps[name] = nc.dram_tensor(f"in_{name}", value.shape, mybir.dt.from_np(value.dtype), kind="ExternalInput").ap()
    aps["out"] = nc.dram_tensor("out_0", (1, L, D), F32, kind="ExternalOutput").ap()
    hybrid_block(nc, aps)
    return run_bass_kernel_spmd(nc, [arrays], core_ids=[0]).results[0]["out_0"]
```

```python
from contextlib import ExitStack

import concourse.bass as bass
import numpy as np
from concourse import mybir
from concourse.alu_op_type import AluOpType as ALU

F32 = mybir.dt.float32
I32 = mybir.dt.int32
ACT = mybir.ActivationFunctionType
P = 128

D, L, NT = 1024, 256, 512
KD = D // P
GRID_W = 64
DECAY = 0.606531
E, TOPK, FF, SLOTS = 32, 4, 1024, 64
EXTRA = L * TOPK // SLOTS
WORDS = 53152
SPARE = 3
LIMIT, ALPHA = 7.0, 1.702
EPS = 1e-6
NC_LEVELS = (64, 32, 16, 8, 4, 2, 1)

GLA0, RW0, SSD0, DT0 = 0, 800, 1728, 3264

(C_ID, C_TI, C_ONE, C_TIB, C_TX, C_TXB, C_BTI, C_BTX, C_BTIB, C_BTXB, C_HEAD) = range(11)
C_LEVEL = 11
C_DIAG2 = C_LEVEL + len(NC_LEVELS)
C_GBLK = C_DIAG2 + 1
C_IOTA = C_GBLK + 2
C_N = C_IOTA + 1


def constants():
    u, t = np.arange(P)[:, None], np.arange(P)[None, :]
    same = u // 64 == t // 64
    blocks = [u == t, u <= t, u >= 0 * t, u >= t, u < t, u > t, (u <= t) & same, (u < t) & same,
              (u >= t) & same, (u > t) & same, same]
    for b in NC_LEVELS:
        blocks.append((u // (2 * b) == t // (2 * b)) & (u // b % 2 != t // b % 2))
    blocks.append(2.0 * (u == t))
    v = np.arange(2 * P)[None, :]
    wide = (u // 32 == v // 64)
    last = np.zeros((P, P))
    last[:, :64] = np.arange(64)
    last[:, 64] = np.arange(P) % E
    last[:, 65] = (np.arange(P) // E + 1) * SLOTS
    last[:, 66] = last[:, 65]
    last[:, 80:96] = u % 32 == np.arange(16)[None, :]
    return np.ascontiguousarray(np.concatenate([np.broadcast_to(b, (P, P)) for b in blocks] + [wide, last], 1),
                                dtype=np.float32)


class Rounds:

    def __init__(self, table, full, free):
        self.full, self.free, self.at = full, free, {}
        fills, drains = [0] * len(full), [0] * len(full)
        for name, group, parts in table:
            fills[group] += 1
            self.at[name] = (group, fills[group], drains[group], drains[group] + parts)
            drains[group] += parts
        self.fills, self.drains = fills, drains

    def group(self, name):
        return self.at[name][0]

    def claim(self, pe, name):
        g, _, before, _ = self.at[name]
        if before > 0:
            pe.wait_ge(self.free[g], before)

    def filled(self, name, ins):
        ins.then_inc(self.full[self.at[name][0]], 1)

    def arrived(self, eng, name):
        g, value, _, _ = self.at[name]
        eng.wait_ge(self.full[g], value)

    def drained(self, name, ins):
        ins.then_inc(self.free[self.at[name][0]], 1)

    def partly(self, eng, name, parts):
        g, _, before, _ = self.at[name]
        eng.wait_ge(self.free[g], before + parts)

    def emptied(self, eng, name):
        g, _, _, after = self.at[name]
        eng.wait_ge(self.free[g], after)


PROJ = [
    ("B", ((SSD0 + 1024, 128, False), (SSD0 + 1152, 128, False))),
    ("C", ((SSD0 + 1280, 128, True), (SSD0 + 1408, 128, True))),
    ("xs0", ((SSD0 + 512, 128, False), (SSD0 + 640, 128, False))),
    ("xs1", ((SSD0 + 768, 128, False), (SSD0 + 896, 128, False))),
    ("z0", ((SSD0, 128, True), (SSD0 + 128, 128, True))),
    ("z1", ((SSD0 + 256, 128, True), (SSD0 + 384, 128, True))),
    ("gq", ((0, 128, True), (128, 128, False))),
    ("gv", ((256, 128, False), (384, 128, False))),
    ("og", ((512, 128, True), (640, 128, True))),
    ("lg", ((768, 32, False),)),
    ("rr", ((RW0, 128, True), (RW0 + 128, 128, True))),
    ("rk", ((RW0 + 256, 128, False), (RW0 + 384, 128, False))),
    ("rv", ((RW0 + 512, 128, False), (RW0 + 640, 128, False))),
    ("low", ((RW0 + 768, 96, False), (RW0 + 864, 64, True))),
]
W_GROUPS = [(SSD0 + 1024, 512, ("B", "C")), (SSD0 + 512, 512, ("xs0", "xs1")), (SSD0, 512, ("z0", "z1")),
            (0, 512, ("gq", "gv")), (512, 288, ("og", "lg")), (RW0, 512, ("rr", "rk")), (RW0 + 512, 416, ("rv", "low"))]

ADA_AFTER = (1, 1, 1, 1, 2, 1, 1, 0, 2, 1, 2, 1, 1, 1)

RECIP_AT = 3
BUSY_ADA, BUSY_FIRST, BUSY_TILE, BUSY_STATE, BUSY_SOLVE = 5, 12, 4, 6, 4

BWD_ORDER = [3, 2, 1, 0, 7, 6, 5, 4]


def round_table():
    t = [("x0", 0, 1), ("x1", 1, 1), ("prm", 2, 1), ("ada0", 3, 1), ("mt0", 0, 1)]
    t += [(f"h{i}", i % 2 + 2, 2) for i in range(4)]
    t += [("dtp", 0, 1), ("dt", 1, 1)]
    for i, (n, _) in enumerate(PROJ):
        t += [("gz", 0, 1)] if n == "rk" else []
        t.append((n, (i + 1) % 3, 1))
    for i in (1, 2):
        t += [(f"ada{i}", 3, 1), (f"mt{i}", 3, 1)]
    t += [("xst0", 0, 1), ("xst1", 1, 1), ("gs", 0, 1), ("gk", 1, 1), ("gvt", 0, 1), ("gc", 1, 1), ("Bt", 2, 1), ("cc", 3, 1), ("st", 0, 1), ("sc", 1, 1)]
    for q in range(4):
        t += [(n, g, 1) for n, g in ((("rz0", 1), ("rz1", 1)), (("ra", 0),), (("gS", 1), ("rg", 1)), (("rkn", 0),))[q]]
        t += [(f"dc{2 * q}", 2, 2), (f"dc{2 * q + 1}", 3, 2), (f"yp{q}", q % 2, 1)]
    t += [("sn", 2, 1)]
    for i in range(9):
        t += [(f"l{i}a", (2 * i) % 4, 1), (f"l{i}b", (2 * i + 1) % 4, 1)]
    t += [("rb", 0, 1), ("go", 2, 1), ("gn", 3, 1)]
    t += [("rvt", 1, 1)]
    for tt in range(4):
        for s in ("cu", "bk", "AA", "BM") + (("MM",) if tt >= 2 else ()) + ("BV",):
            for d in (0, 1):
                t.append((f"{s}{tt}{d}", 2 * d + {"cu": 0, "bk": 1, "AA": 0, "BM": 1, "MM": 0, "BV": 1}[s], 1))
        for j in range(5):
            t += [(f"D{j}{tt}{d}", 2 * d, 2 if j < 4 else 1) for d in (0, 1)]
            t += [(f"T{j}{tt}{d}", 2 * d + 1, 1) for d in (0, 1)]
    for i in range(8):
        for d in (0, 1):
            t.append((f"R1{i}{d}", 2 * d, 1))
        for d in (0, 1):
            t.append((f"R2{i}{d}", 2 * d + 1, 1))
        if i >= 4:
            t += [(f"RO{i}{d}", 2 * d, 1) for d in (0, 1)]
        for d in (0, 1):
            t.append((f"R3{i}{d}", 2 * d + 1, 1))
    t += [("RU", 0, 1), ("rm", 1, 1), ("rv2", 2, 1)]
    t += [("w0", 3, 1), ("w1", 0, 1), ("m5", 1, 1), ("fg", 2, 1), ("n2", 3, 1), ("xk0", 0, 1), ("xk1", 1, 1), ("rt", 2, 1),
          ("hk0", 3, 1), ("hk1", 0, 1), ("pos", 1, 1), ("gt", 0, 1), ("cnd", 1, 1), ("idx", 2, 1), ("lst", 3, 1)]
    return t


def hybrid_block(nc, a):
    with ExitStack() as ctx:
        sem = lambda name: ctx.enter_context(nc.semaphore(name))
        arena = ctx.enter_context(nc.sbuf_tensor("arena", [P, WORDS], F32))
        ints = ctx.enter_context(nc.sbuf_tensor("ints", [P, 2 * EXTRA + 8], I32))
        PS = ctx.enter_context(nc.psum_tensor("PS", [P, 8, 512], F32))

        class Area:

            def __init__(self, start, end):
                self.at, self.end = start, end

            def take(self, *shape):
                n = int(np.prod(shape))
                ap = arena[:, self.at:self.at + n]
                self.at += n
                assert self.at <= self.end, (self.at, self.end, shape)
                if len(shape) == 2:
                    ap = ap.rearrange("p (a b) -> p a b", a=shape[0])
                if len(shape) == 3:
                    ap = ap.rearrange("p (a b c) -> p a b c", a=shape[0], b=shape[1])
                if len(shape) == 4:
                    ap = ap.rearrange("p (a b c d) -> p a b c d", a=shape[0], b=shape[1], c=shape[2])
                return ap

        keep = Area(0, WORDS)
        C = keep.take(C_N, P)
        pc = keep.take(162)
        w0b, gbb = keep.take(512), keep.take(256)
        dtb, alog, rbb = keep.take(16), keep.take(16), keep.take(E)
        W2A, gwb, g2w = keep.take(512), keep.take(256), keep.take(256)
        dtw_at = keep.at
        dtw, rtw = keep.take(KD, 16), keep.take(KD, E)
        dtw_and_next = arena[:, dtw_at:dtw_at + KD * 16 + 16]
        csil = keep.take(KD, 32)
        modrow = keep.take(512)
        mod = keep.take(48, 2)
        A1, A2 = keep.take(KD, 2), keep.take(KD)
        small = keep.take(64)
        muc, dall, dcol = keep.take(8), keep.take(8), keep.take(4)
        xT, cat = keep.take(KD, L), keep.take(KD, L)
        slots = [None] * 14
        for s in (2, 3, 4, 5, 0, 1):
            slots[s] = keep.take(2048)
        big0 = keep.at - 4096
        u_area = Area(keep.at, WORDS)

        rT, lowT, sgT = u_area.take(2, L), u_area.take(NT), u_area.take(L)
        kT, vT = u_area.take(2, NT), u_area.take(2, NT)
        after_rwkv_inputs = u_area.at
        KQ, gkc, gvT, gog, lgT = u_area.take(2, L), u_area.take(L), u_area.take(2, NT), u_area.take(2, L), u_area.take(NT)
        sz, xsT, BT, CT = u_area.take(4, L), u_area.take(4, NT), u_area.take(2, NT), u_area.take(2, L)
        scratch0 = u_area.at
        xtok, hT = None, None
        tail = Area(WORDS - 8192, WORDS)
        xtok, hT = tail.take(4, D), tail.take(KD, NT)
        for s in range(2):
            slots[12 + s] = hT.rearrange("p k t -> p (k t)")[:, 2048 * s:2048 * s + 2048]

        sa = Area(scratch0, WORDS - 8192)
        prow = sa.take(2, P)
        diagR = sa.take(4, P)
        sb_ = Area(scratch0, WORDS - 8192 + 4096)
        xtk, Btok = sb_.take(4, 512), sb_.take(2, 256)
        dtk = sb_.take(4, 16)
        adt, wct, cumc = sb_.take(4, 16), sb_.take(2, 16), sb_.take(4, 16)
        dtmp = sb_.take(3, 64)
        ea = sb_.take(16)
        xw = sb_.take(2, 2, 512)
        Sst = sb_.take(2, 512)
        scF, scB = sb_.take(2, 3, P), sb_.take(2, 3, P)
        eD, EI, CI, WD = sb_.take(2, 768), sb_.take(2, 512), sb_.take(2, 512), sb_.take(2, 768)
        ssq = sb_.take(4, L)
        gz = sb_.take(4, 256)
        dt_quarters = gz.rearrange("p a b -> p (a b)")[:, 0:NT]
        gzt = ssq
        gp = Area(big0 - 8192, big0 - 4096)
        gE, gkt, gkw = gp.take(2, 256), gp.take(2, P), gp.take(2, 256)
        gvk = gp.take(4, 256)
        gSt = gp.take(2, 256)
        gcum, qI = gp.take(2, L), gp.take(2, L)
        gs_ = Area(scratch0, WORDS - 8192 + 4096)
        lv, lk = gs_.take(2, 512), gs_.take(2, 512)
        att = gs_.take(4, 2, L)
        gO, gsq = gs_.take(2, L), gs_.take(2, L)

        RWKV_WORDS = 22560
        ra = Area(WORDS - RWKV_WORDS, WORDS)
        assert WORDS - RWKV_WORDS >= after_rwkv_inputs
        low = Area(big0, big0 + 4096)
        TT = [low.take(4, 4, P) for _ in range(2)]
        rp = Area(big0 - 4096, big0)
        lw = rp.take(4, 512)
        kk, ba = rp.take(2, NT), rp.take(2, NT)
        ktmp = [TT[0].rearrange("p a b c -> p (a b c)")[:, 1024 * i:1024 * i + 1024].rearrange("p (a b) -> p a b", a=2) for i in range(2)]
        BVs = [ra.take(4, 256) for _ in range(2)]
        mb = [ra.take(2, 4, P) for _ in range(2)]
        mk = [ra.take(4, P) for _ in range(2)]
        bm = [ra.take(4, P) for _ in range(2)]
        XX = [ra.take(4, 2, P) for _ in range(2)]
        bt = [ra.take(4, 512) for _ in range(2)]
        Us = [ra.take(2, 256) for _ in range(2)]
        RH = [ra.take(256) for _ in range(2)]
        assert ra.at >= gs_.at
        al = [ra.take(2, NT) for _ in range(2)]
        rho = [ra.take(2, L) for _ in range(2)]
        be = [ra.take(2, P) for _ in range(2)]
        ka = [ra.take(2, P) for _ in range(2)]
        eb = [ra.take(3, 2, P) for _ in range(2)]
        Vt = ra.take(4, 256)
        ST = [ra.take(2, P) for _ in range(2)]
        wc = [ra.take(2, 8) for _ in range(2)]
        oT, bon, rgt = ra.take(2, L), ra.take(2, L), ra.take(2, L)
        assert ra.at == WORDS

        osq = XX[0].rearrange("p a b c -> p (a b c)")[:, 0:512]
        WM = [eb[d].rearrange("p a b c -> p (a b c)")[:, 0:512].rearrange("p (i c e) -> p i c e", i=2, c=2) for d in range(2)]
        bon_tmp = eb[0].rearrange("p a b c -> p (a b c)")[:, 0:512]

        ma = Area(big0 + 4096, WORDS)
        for s in range(6, 12):
            slots[s] = ma.take(2048)
        h2T = ma.take(KD, L)
        h2k, xk = ma.take(2, D), ma.take(2, D)
        m5r, fgr = ma.take(D), ma.take(D)
        hg, actT = ma.take(KD, SLOTS), ma.take(4, 2, SLOTS)
        glu_at = ma.at
        glu, lin, sgm, act_ = ma.take(512), ma.take(512), ma.take(512), ma.take(512)
        ye = ma.take(512)
        sel, selw = ma.take(2, SLOTS), ma.take(2, 2, SLOTS)
        SW = ma.take(L)
        bgrow = ma.take(2 * FF)
        this_e = ma.take(SLOTS)
        gates, spos = ma.take(2, E), ma.take(2, E)
        lgt = ma.take(2, E)
        rt1, rt2, rt3, rt4 = ma.take(2, E), ma.take(2, E), ma.take(2, E), ma.take(2, E)
        top8 = ma.take(2, 8)
        gT = ma.take(L)
        ibase = ma.take(E + EXTRA)
        cand, onehot = ma.take(4), ma.take(EXTRA)
        r2 = ma.take(L)
        msk3 = ma.take(2, 96)
        sq2 = cat.rearrange("p k t -> p (k t)")
        dg = ma.take(16, P)
        bdn = arena[:, glu_at:glu_at + D]

        spare = [ap.rearrange("p k t -> p (k t)") for ap in (cat, xT, h2T)]

        full = [sem(f"pair_full{g}") for g in range(4)]
        free = [sem(f"pair_free{g}") for g in range(4)]
        R = Rounds(round_table(), full, free)
        ident_in = sem("ident_in")
        consts_in, rows_in, x_in, mats_in = sem("consts_in"), sem("rows_in"), sem("x_in"), sem("mats_in")
        late_in = sem("late_in")
        zeroed = sem("zeroed")
        slot_full = [sem(f"slot_full{s}") for s in range(14)]
        spare_full = [sem(f"spare_full{s}") for s in range(SPARE)]
        slot_free = [sem(f"slot_free{s}") for s in range(14)]
        named = lambda names: [sem(n) for n in names.split()]
        vec_step, act_step, moe_vec = named("vec_step act_step moe_vec")
        pool_step, kk_norm = named("pool_step kk_norm")
        silu_c, squares1, var1, std1, diag_ready, mod_ready = named("silu_c squares1 var1 std1 diag_ready mod_ready")
        conv_init, conv_silu = named("conv_init conv_silu")
        dt_abs, dt_exp, dt_ready, ctx_w, xw_ready = named("dt_abs dt_exp dt_ready ctx_w xw_ready")
        E_ready, w_ready, ssq_ready, sn_std = named("E_ready w_ready ssq_ready sn_std")
        gz_abs, gz_exp, g_ready, gkw_ready, qi_exp, qi_ready = named("gz_abs gz_exp g_ready gkw_ready qi_exp qi_ready")
        lv_arg, lv_exp, lk_ready, gsq_ready, gn_std, gla_done = named("lv_arg lv_exp lk_ready gsq_ready gn_std gla_done")
        rw_tanh, rz_sig, lw_ready, kk_sq, kk_std, rw_pre, gate_sig = named(
            "rw_tanh rz_sig lw_ready kk_sq kk_std rw_pre gate_sig")
        rw_in, osq_ready, o_std, cat_ready = named("rw_in osq_ready o_std cat_ready")
        st_ready = [sem(f"st_ready{d}") for d in range(2)]
        wm_ready = [sem(f"wm_ready{d}") for d in range(2)]
        x2_sq, dg_ready, n2_std, h2_scaled, h2_ready = named("x2_sq dg_ready n2_std h2_scaled h2_ready")
        rt_max, rt_exp, mask_ready, gates_ready, onehot_ready = named("rt_max rt_exp mask_ready gates_ready onehot_ready")
        sel_ready, gathered, hg_ready, glu_ready, sig_ready, act_ready = named(
            "sel_ready gathered hg_ready glu_ready sig_ready act_ready")
        ye_ready, selT_done, sw_ready, scattered, y_init = named("ye_ready selT_done sw_ready scattered y_init")
        actT_done, actT_ready, te_ready = named("actT_done actT_ready te_ready")
        y_read, f_sq, f_var, f_std, out_ready, out_done = named("y_read f_sq f_var f_std out_ready out_done")
        N_ROWS, N_MATS = 22, 18

        def pair(name, n=1024):
            g = R.group(name)
            return PS[:, 2 * g:2 * g + 2, :].rearrange("p a b -> p (a b)")[:, 0:n]

        def o_of(h):
            return h % 2 * 2 + h // 2

        def Cb(i, n=1):
            return C[:, i:i + n, :].rearrange("p a b -> p (a b)")

        loads = [(n if n < 6 else n + 6, 1, "ada", n) for n in range(8)]
        def streamed(kind, n):
            return (2 * ((n + 1) % 2), 2, "in", n) if kind == "in" else (4 + n % 2, 1, "ada", n)

        used, n_ada = [], 8
        for i, (name, _) in enumerate(PROJ):
            used += [("in", g) for g, (_, _, names) in enumerate(W_GROUPS) if names[-1] == name]
            used += [("ada", n_ada + j) for j in range(ADA_AFTER[i])]
            n_ada += ADA_AFTER[i]
        loads += [streamed(kind, n) for kind, n in (("in", 0), ("in", 1), ("ada", 8), ("ada", 9))]
        loads += [streamed(kind, n + 2) for kind, n in used if n + 2 < (len(W_GROUPS) if kind == "in" else 24)]
        loads += [(2 + n, 1, "out", n) for n in range(4)]
        base = [0] * 14
        holder = [None] * 14
        place, before = {}, {}
        for s, width, kind, n in loads:
            before[kind, n] = sorted({h for h in holder[s:s + width] if h})
            base[s] += 1
            place[kind, n] = (s, base[s])
            for q in range(s, s + width):
                holder[q] = (s, base[s])

        def w_in_tile(n):
            s = place["in", n][0]
            lo = {0: big0, 2: big0 - 8192}[s]
            w = W_GROUPS[n][1]
            return arena[:, lo:lo + KD * w].rearrange("p (k c) -> p k c", k=KD)

        w_ada_k = a["w_ada"][0].rearrange("(k p) c -> k p c", p=P)
        w_in_k = a["w_in"][0].rearrange("(k p) c -> p k c", p=P)
        w_out_k = a["w_out"][0].rearrange("(k p) c -> p k c", p=P)
        gu_k = a["moe_w_gu"][0].rearrange("e (k p) c -> e k p c", p=P)
        dn_k = a["moe_w_down"][0].rearrange("e (k p) c -> e p k c", p=P)

        block = ctx.enter_context(nc.Block())

        @block.sync
        def _(sp):
            def slot_wait(kind, n):
                for s, count in before[kind, n]:
                    sp.wait_ge(slot_free[s], count)

            sp.dma_start(Cb(C_ID), a["consts"][:, 0:P]).then_inc(ident_in, 16)
            sp.dma_start(xtok[:, 0:2, :], a["ctx"][0].rearrange("(i p) d -> p i d", p=P)).then_inc(x_in, 16)
            sp.dma_start(xtok[:, 2:4, :], a["x"][0].rearrange("(i p) d -> p i d", p=P)).then_inc(x_in, 16)

            def load_ada(n):
                s = place["ada", n][0]
                slot_wait("ada", n)
                sp.dma_start(slots[s], w_ada_k[n % 8, :, n // 8 * 2048:n // 8 * 2048 + 2048]).then_inc(slot_full[s], 16)

            sp.dma_start(Cb(1, C_N - 1), a["consts"][:, P:]).then_inc(consts_in, 16)
            sp.wait_ge(rows_in, 16 * N_ROWS)
            for n in range(8):
                load_ada(n)

            sp.wait_ge(zeroed, 1)

            def mats(dst, src):
                sp.dma_start(dst, src).then_inc(mats_in, 16)

            def spread(dst, src):
                mats(dst, src.partition_broadcast(P))

            for d in range(2):
                spread(w0b[:, 256 * d:256 * d + 256], a["rw_w0"][0, d, :])
                spread(gbb[:, P * d:P * d + P], a["gla_gate_b"][0, d, :])
                spread(dtb[:, 8 * d:8 * d + 8], a["ssd_dt_bias"][0, d, :])
                spread(alog[:, 8 * d:8 * d + 8], a["ssd_a_log"][0, d, :])
                mats(W2A[32 * d:32 * d + 32, 256 * d:256 * d + 256], a["rw_w2"][0, d])
                mats(gwb[16 * d:16 * d + 16, P * d:P * d + P], a["gla_gate_w"][0, d])
            spread(rbb, a["router_b"][0])
            spread(dall, a["ssd_d"][0])
            mats(W2A[64:96, 0:256], a["rw_a2"][0])
            mats(g2w[0:64, :], a["rw_g2"][0])
            mats(dtw[:, :, :], a["w_in"][0].rearrange("(k p) c -> p k c", p=P)[:, :, DT0:DT0 + 16])
            mats(rtw[:, :, :], a["router_w"][0].rearrange("(k p) c -> p k c", p=P))

            for s, _, kind, n in loads[8:]:
                if kind == "in":
                    c0, w, _ = W_GROUPS[n]
                    slot_wait("in", n)
                    sp.dma_start(w_in_tile(n), w_in_k[:, :, c0:c0 + w]).then_inc(slot_full[s], 16)
                elif kind == "ada":
                    load_ada(n)
            sp.wait_ge(gla_done, 1)
            for n in range(4):
                if n == 2:
                    sp.wait_ge(rw_in, 8)
                s = place["out", n][0]
                slot_wait("out", n)
                sp.dma_start(slots[s].rearrange("p (k c) -> p k c", k=2), w_out_k[:, 2 * n:2 * n + 2, :])\
                    .then_inc(slot_full[s], 16)

            sp.wait_ge(cat_ready, 1)
            sp.dma_start(bgrow[0:E, :], a["moe_b_gu"][0]).then_inc(late_in, 16)
            sp.dma_start(bdn[0:E, 0:D], a["moe_b_down"][0]).then_inc(late_in, 16)

            def load_expert(n, e, first, slots_from=0):
                for s in range(slots_from, 12):
                    if not first:
                        sp.wait_ge(slot_free[s], n + (base[s]))
                    if s < 8:
                        src = gu_k[bass.ds(e, 1), s, :, :].rearrange("a p c -> p (a c)")
                        dst = slots[s]
                    else:
                        src = dn_k[bass.ds(e, 1), :, 2 * (s - 8):2 * (s - 8) + 2, :].rearrange("a p k c -> p (a k) c")
                        dst = slots[s].rearrange("p (k c) -> p k c", k=2)
                    if first and 2 <= s <= 5:
                        sp.wait_ge(slot_free[s], base[s])
                    sp.dma_start(dst, src).then_inc(slot_full[s], 16)

            load_expert(0, 0, True)
            R.emptied(sp, "n2")
            sp.wait_ge(h2_ready, 1)
            for name in ("xk0", "xk1", "hk0", "hk1"):
                R.emptied(sp, name)
            for s in range(SPARE):
                sp.dma_start(spare[s], gu_k[E - 1, s, :, :]).then_inc(spare_full[s], 16)
            with sp.Fori(1, E - 1) as n:
                load_expert(n, n, False)
            load_expert(E - 1, E - 1, False, SPARE)
            R.emptied(sp, "lst")
            extra = sp.value_load(ints[0:1, 0:1], min_val=0, max_val=EXTRA)
            with sp.If(extra > 0):
                with sp.Fori(0, extra) as j:
                    e = sp.value_load(ints[0:1, bass.ds(j + 8, 1)], min_val=0, max_val=E - 1)
                    load_expert(j + E, e, False)
            for i in range(2):
                sp.wait_ge(out_ready, i + 1)
                sp.dma_start(a["out"][0, i * P:(i + 1) * P, :], xk[:, i, :]).then_inc(out_done, 16)
            sp.wait_ge(out_done, 32)

        @block.gpsimd
        def _(pool):
            pool.memset(csil, 0.0)
            pool.memset(prow[:, :, :], 0.0)
            pool.memset(W2A[0:64, :], 0.0)
            pool.memset(gwb[0:32, :], 0.0).then_inc(zeroed, 1)
            B = lambda i: pc[:, 88 + i:89 + i]
            steps = [0]

            def run(ins):
                ins.then_inc(pool_step, 1)
                steps[0] += 1
                pool.wait_ge(pool_step, steps[0])

            for name in ("yp2", "yp3", "gc"):
                R.emptied(pool, name)
            for i, b in enumerate((P,) + NC_LEVELS):
                nb = L // (2 * b)
                F_ = gcum[:, 0, :].rearrange("p (n h w) -> p n h w", n=nb, h=2)
                B_ = gcum[:, 1, :].rearrange("p (n h w) -> p n h w", n=nb, h=2)
                arg = lv[:, i % 2, :].rearrange("p (x n h w) -> p x n h w", x=2, n=nb, h=2)
                mid_f = F_[:, :, 0, b - 1:b].to_broadcast([P, nb, b])
                mid_b = B_[:, :, 1, 0:1].to_broadcast([P, nb, b])
                if i >= 2:
                    pool.wait_ge(lk_ready, i - 1)
                run(pool.tensor_tensor(arg[:, 0, :, 0, :], mid_f, F_[:, :, 0, :], ALU.subtract))
                run(pool.tensor_tensor(arg[:, 0, :, 1, :], mid_b, B_[:, :, 1, :], ALU.subtract))
                run(pool.tensor_tensor(arg[:, 1, :, 0, :], B_[:, :, 0, :], mid_b, ALU.subtract))
                pool.tensor_tensor(arg[:, 1, :, 1, :], F_[:, :, 1, :], mid_f, ALU.subtract).then_inc(lv_arg, 1)

                if i == 1:
                    R.emptied(pool, "ra")
                    for c in range(2):
                        run(pool.tensor_scalar(ktmp[0][:, c, :], ba[:, c, :], -1.0, B(20 + c), ALU.add, ALU.mult))
                if i == 2:
                    run(pool.tensor_scalar(ktmp[0], ktmp[0], 1.0, None, ALU.add))
                if i == 3:
                    run(pool.tensor_tensor(kT, kT, ktmp[0], ALU.mult))
                if i == RECIP_AT + 3:
                    pool.wait_ge(kk_norm, 2)
                    run(pool.tensor_tensor(kk, kk, ktmp[1], ALU.mult))
                if i == RECIP_AT + 4:
                    run(pool.tensor_tensor(ba, ba, kk, ALU.mult))
            for c in range(2):
                run(pool.tensor_scalar(bon[:, c, :], rT[:, c, :], B(22 + c), None, ALU.mult))
            pool.tensor_tensor(bon, bon, kT[:, :, L:NT], ALU.mult).then_inc(rw_pre, 1)
            pool.wait_ge(gla_done, 1)
            for d in range(2):
                last = pool.memset(ST[d], 0.0)
            last.then_inc(zeroed, 1)
            pool.wait_ge(cat_ready, 1)
            pool.memset(ye, 0.0).then_inc(ye_ready, 1)
            pool.memset(SW, 0.0).then_inc(sw_ready, 1)
            pool.memset(hg[:, 0, :], 0.0).then_inc(hg_ready, 1)
            pool.memset(act_, 0.0).then_inc(act_ready, 1)
            pool.memset(ibase, 0.0).then_inc(zeroed, 1)

        @block.scalar
        def _(act):
            steps = [0]

            def step(ins):
                ins.then_inc(act_step, 1)
                steps[0] += 1

            def settle():
                act.wait_ge(act_step, steps[0])

            act.wait_ge(zeroed, 1)
            ra_, rb_ = prow[:, 0, :], prow[:, 1, :]

            def rows(dst, src):
                act.dma_start(dst, src).then_inc(rows_in, 16)

            rows(ra_[0:48, :], a["b_ada"][0].rearrange("(r p) -> r p", p=P))
            rows(ra_[48:56, :], a["c"][0].rearrange("(r p) -> r p", p=P))
            rows(ra_[56:64, :], a["c_ctx"].rearrange("(r p) -> r p", p=P))
            rows(ra_[64:72, :], a["norm1_g"][0].rearrange("(r p) -> r p", p=P))
            rows(ra_[72:80, :], a["norm2_g"][0].rearrange("(r p) -> r p", p=P))
            rows(ra_[80:88, :], a["final_norm_g"].rearrange("(r p) -> r p", p=P))
            for i in range(2):
                mu = a["rw_mu"][0, i, :]
                rows(rb_[8 * i:8 * i + 6, :], mu[0:768].rearrange("(r p) -> r p", p=P))
                rows(rb_[8 * i + 6:8 * i + 7, 0:96], mu[768:864].rearrange("(r p) -> r p", r=1))
                rows(rb_[8 * i + 7:8 * i + 8, 0:64], mu[864:928].rearrange("(r p) -> r p", r=1))
            rows(rb_[16:18, :], a["rw_a0"][0].rearrange("(r p) -> r p", p=P))
            rows(rb_[18:20, :], a["rw_kk"][0].rearrange("(r p) -> r p", p=P))
            rows(rb_[20:22, :], a["rw_ka"][0].rearrange("(r p) -> r p", p=P))
            rows(rb_[22:24, :], a["rw_rk"][0].rearrange("(r b) n -> r (b n)", b=2))
            rows(rb_[24:26, :], a["rw_lnx_g"][0].rearrange("(r b) n -> r (b n)", b=2))
            rows(rb_[26:28, :], a["rw_lnx_b"][0].rearrange("(r b) n -> r (b n)", b=2))
            rows(rb_[28:60, :], a["ssd_conv_w"][0].rearrange("j (t p) -> (j t) p", p=P))
            rows(rb_[60:68, :], a["ssd_conv_b"][0].rearrange("(r p) -> r p", p=P))
            rows(rb_[68:72, :], a["ssd_norm_g"][0].rearrange("(r p) -> r p", p=P))
            rows(rb_[72:74, :], a["gla_norm_g"][0].rearrange("(r b) n -> r (b n)", b=2))

            R.emptied(act, "prm")
            act.activation(csil[:, :, 0:2].rearrange("p k s -> p s k"), pc[:, 48:64].rearrange("p (s k) -> p s k", s=2), ACT.Silu)\
               .then_inc(silu_c, 1)
            act.wait_ge(x_in, 32)
            for i in range(4):
                act.activation((cat, xsT)[i // 2].rearrange("p k t -> p (k t)")[:, 1024 * (i % 2):1024 * (i % 2) + 1024], xtok[:, i, :], ACT.Square,
                               accum_out=small[:, i:i + 1]).then_inc(squares1, 1)
            for i in range(2):
                R.arrived(act, f"x{i}")
                R.drained(f"x{i}", act.copy(xT[:, 4 * i:4 * i + 4, :].rearrange("p a b -> p (a b)"), pair(f"x{i}")))
            act.wait_ge(var1, 1)
            act.activation(small[:, 8:12], small[:, 4:8], ACT.Sqrt).then_inc(std1, 1)
            act.wait_ge(mod_ready, 1)
            act.wait_ge(squares1, 4)
            for i in range(4):
                R.arrived(act, f"h{i}")
                k = 2 * i
                step(act.activation(hT[:, k, 0:L], pair(f"h{i}")[:, 0:L], ACT.Identity,
                                    bias=mod[:, k, 1:2], scale=A1[:, k, 1:2]))
                ins = act.activation(hT[:, k, L:NT], pair(f"h{i}")[:, L:NT], ACT.Identity,
                                     bias=mod[:, k, 0:1], scale=A1[:, k, 0:1])
                R.drained(f"h{i}", ins)

            R.arrived(act, "dtp")
            R.drained("dtp", act.copy(dt_quarters, pair("dtp", 512)))

            conv = {"B": (BT, 4, NT), "C": (CT, 6, L), "xs0": (xsT[:, 0:2, :], 0, NT), "xs1": (xsT[:, 2:4, :], 2, NT)}

            def conv_start(name):
                dst, tile, n = conv[name]
                R.arrived(act, name)
                for j in range(2):
                    act.activation(dst[:, j, :], pair(name)[:, 512 * j:512 * j + n], ACT.Identity,
                                   bias=pc[:, 88 + 60 + tile + j:88 + 61 + tile + j],
                                   scale=pc[:, 88 + 28 + 16 + tile + j:88 + 29 + 16 + tile + j]).then_inc(conv_init, 1)

            def conv_end(name):
                dst, _, n = conv[name]
                R.emptied(act, name)
                act.activation(dst, dst, ACT.Silu).then_inc(conv_silu, 1)

            conv_start("B")
            conv_start("C")
            conv_end("B")
            conv_start("xs0")
            conv_end("C")
            conv_start("xs1")
            conv_end("xs0")
            conv_end("xs1")
            act.wait_ge(dt_abs, 1)
            step(act.activation(dtmp[:, 1, :], dtmp[:, 0, :], ACT.Exp))
            act.wait_ge(mats_in, 16 * N_MATS)
            act.activation(ea, alog, ACT.Exp).then_inc(dt_exp, 1)
            settle()
            act.activation(dtmp[:, 2, :], dtmp[:, 1, :], ACT.Ln, bias=1.0).then_inc(dt_exp, 1)
            for q in range(2):
                R.arrived(act, f"z{q}")
                R.drained(f"z{q}", act.activation(sz[:, 2 * q:2 * q + 2, :],
                                                  pair(f"z{q}").rearrange("p (a b) -> p a b", a=2)[:, :, 0:L], ACT.Silu))
            R.arrived(act, "gq")
            step(act.activation(KQ[:, 1, :], pair("gq")[:, 0:L], ACT.Copy, scale=float(32 ** -0.5)))
            step(act.copy(KQ[:, 0, :], pair("gq")[:, 512 + L:1024]))
            R.drained("gq", act.copy(gkc, pair("gq")[:, 512:512 + L]))
            R.arrived(act, "gv")
            R.drained("gv", act.copy(gvT.rearrange("p a b -> p (a b)"), pair("gv")))
            R.arrived(act, "og")
            R.drained("og", act.activation(gog[:, :, :], pair("og").rearrange("p (a b) -> p a b", a=2)[:, :, 0:L],
                                           ACT.Silu))

            act.wait_ge(gz_abs, 1)
            act.activation(gzt, gzt, ACT.Exp).then_inc(gz_exp, 1)
            act.wait_ge(gz_exp, 1)
            act.activation(gzt, gzt, ACT.Ln, bias=1.0).then_inc(gz_exp, 1)

            R.arrived(act, "xst0")
            R.drained("xst0", act.copy(xtk[:, 0:2, :].rearrange("p a b -> p (a b)"), pair("xst0")))
            R.arrived(act, "xst1")
            R.drained("xst1", act.copy(xtk[:, 2:4, :].rearrange("p a b -> p (a b)"), pair("xst1")))
            R.arrived(act, "gs")
            R.drained("gs", act.activation(gE.rearrange("p a b -> p (a b)"), pair("gs", 512), ACT.Exp))
            R.arrived(act, "gk")
            R.drained("gk", act.copy(gkt.rearrange("p a b -> p (a b)"), pair("gk", 256)))
            R.arrived(act, "gvt")
            R.drained("gvt", act.copy(gvk.rearrange("p a b -> p (a b)"), pair("gvt")))
            R.arrived(act, "gc")
            R.drained("gc", act.copy(gcum.rearrange("p a b -> p (a b)"), pair("gc", 512)))
            R.emptied(act, "gc")
            act.activation(qI, gcum, ACT.Exp).then_inc(qi_exp, 1)
            R.arrived(act, "Bt")
            R.drained("Bt", act.copy(Btok[:, :, :].rearrange("p a b -> p (a b)"), pair("Bt", 512)))
            R.arrived(act, "cc")
            act.activation(wct.rearrange("p a b -> p (a b)"), pair("cc")[:, 0:32], ACT.Exp).then_inc(ctx_w, 1)
            R.emptied(act, "low")
            act.activation(lowT[0:64, :], lowT[0:64, :], ACT.Tanh).then_inc(rw_tanh, 1)
            for h in range(8):
                name = f"dc{h}"
                R.arrived(act, name)
                if h >= 2:
                    act.wait_ge(w_ready, h - 1)
                R.drained(name, act.activation(EI[:, h % 2, :], pair(name, 512), ACT.Exp))
                R.emptied(act, name)
                act.activation(eD[:, h % 2, :], eD[:, h % 2, :], ACT.Exp).then_inc(E_ready, 1)
                if h == 2:
                    R.arrived(act, "ra")
                    for c in range(2):
                        ins = act.activation(ba[:, c, :], pair("ra")[:, 512 * c:512 * c + 512], ACT.Sigmoid,
                                             bias=pc[:, 88 + 16 + c:88 + 17 + c])
                        if c == 0:
                            step(ins)
                    R.drained("ra", ins)
                if h == 3:
                    R.emptied(act, "rz0")
                    R.emptied(act, "rz1")
                    act.activation(lw, lw, ACT.Sigmoid).then_inc(rz_sig, 1)
                    act.activation(sgT[0:64, :], sgT[0:64, :], ACT.Sigmoid).then_inc(gate_sig, 1)
                if h == 7:
                    R.arrived(act, "rg")
                    R.drained("rg", act.copy(rgt.rearrange("p a b -> p (a b)"), pair("rg", 512)))
                    R.emptied(act, "rkn")
                    act.activation(kk, kk, ACT.Sqrt).then_inc(kk_std, 1)

            for i in range(8):
                act.wait_ge(lv_arg, i + 1)
                act.activation(lv[:, i % 2, :], lv[:, i % 2, :], ACT.Exp).then_inc(lv_exp, 1)
                if i == 0:
                    R.emptied(act, "sn")
                    act.activation(ssq.rearrange("p a b -> p (a b)")[:, 512:1024], ssq.rearrange("p a b -> p (a b)")[:, 0:512],
                                   ACT.Sqrt).then_inc(sn_std, 1)
            R.arrived(act, "rvt")
            R.drained("rvt", act.copy(Vt.rearrange("p a b -> p (a b)"), pair("rvt")))
            R.emptied(act, "gn")
            act.activation(gsq, gsq, ACT.Sqrt).then_inc(gn_std, 1)

            for tt in range(4):
                for d in range(2):
                    name = f"cu{tt}{d}"
                    R.arrived(act, name)
                    if tt:
                        act.wait_ge(rw_in, 2 * (tt - 1) + d + 1)
                    cu = pair(name, 512).rearrange("p (c x t) -> p x c t", c=2, x=2)
                    step(act.activation(eb[d][:, 0, :, :], cu[:, 0, :, :], ACT.Exp))
                    step(act.activation(eb[d][:, 1, :, :], cu[:, 0, :, :], ACT.Exp, scale=-1.0))
                    R.drained(name, act.activation(eb[d][:, 2, :, :], cu[:, 1, :, :], ACT.Exp))
                if tt == 0:
                    act.wait_ge(gla_done, 1)
                for d in range(2):
                    name = f"bk{tt}{d}"
                    R.arrived(act, name)
                    R.drained(name, act.copy(bt[d][:, tt, :], pair(name, 512)))
                for j in range(4):
                    for d in range(2):
                        name = f"D{j}{tt}{d}"
                        R.arrived(act, name)
                        R.drained(name, act.copy(XX[d][:, :, 0, :], pair(name, 512).rearrange("p (o t) -> p o t", o=4)))
            def chunk_decays(i):
                for d in range(2):
                    ch = i if d == 0 else BWD_ORDER[i]
                    if i >= 2:
                        act.wait_ge(st_ready[d], i - 1)
                    for c in range(2):
                        ins = act.activation(WM[d][:, i % 2, c, :], Cb(C_HEAD), ACT.Copy, scale=wc[d][:, c, ch:ch + 1])
                        if c == 0:
                            step(ins)
                    ins.then_inc(wm_ready[d], 1)

            act.wait_ge(rw_in, 8)
            chunk_decays(0)
            chunk_decays(1)
            for i in range(8):
                for d in range(2):
                    name = f"R2{i}{d}"
                    ch = i if d == 0 else BWD_ORDER[i]
                    tt, q = ch // 2, ch % 2
                    R.arrived(act, name)
                    R.drained(name, act.copy(Us[d][64 * q:64 * q + 64, tt % 2, :], pair(name, 256)[64 * q:64 * q + 64, :]))
                if i < 6:
                    chunk_decays(i + 2)
            R.emptied(act, "rv2")
            act.activation(bon_tmp, bon_tmp, ACT.Sqrt).then_inc(o_std, 1)

            R.arrived(act, "m5")
            R.drained("m5", act.copy(m5r, pair("m5")))
            R.arrived(act, "fg")
            R.drained("fg", act.copy(fgr, pair("fg")))
            R.emptied(act, "n2")
            act.activation(r2, r2, ACT.Sqrt).then_inc(n2_std, 1)
            R.arrived(act, "xk0")
            R.drained("xk0", act.copy(xk[:, 0, :], pair("xk0")))
            R.arrived(act, "xk1")
            R.drained("xk1", act.copy(xk[:, 1, :], pair("xk1")))
            for k in range(KD):
                act.wait_ge(h2_scaled, k + 1)
                ins = act.activation(h2T[:, k, :], h2T[:, k, :], ACT.Identity, bias=mod[:, 24 + k, 0:1])
            ins.then_inc(h2_ready, 1)
            R.arrived(act, "hk0")
            R.drained("hk0", act.copy(h2k[:, 0, :], pair("hk0")))
            R.arrived(act, "hk1")
            R.drained("hk1", act.copy(h2k[:, 1, :], pair("hk1")))
            act.wait_ge(rt_max, 1)
            act.activation(rt1, rt1, ACT.Exp).then_inc(rt_exp, 1)

            def expert(n):
                act.wait_ge(gathered, n + 1)
                act.copy(hg.rearrange("p k t -> p (k t)"), PS[:, 2, :]).then_inc(hg_ready, 1)
                act.wait_ge(glu_ready, n + 1)
                act.activation(sgm, glu, ACT.Sigmoid, scale=ALPHA).then_inc(sig_ready, 1)
                act.wait_ge(selT_done, n + 1)
                act.copy(SW, PS[:, 3, 0:L]).then_inc(sw_ready, 1)
                act.wait_ge(actT_done, n + 1)
                act.copy(actT.rearrange("p a b c -> p (a b c)"), PS[:, 2, :]).then_inc(actT_ready, 1)
                act.wait_ge(slot_free[11], n + base[11] + 1)
                act.copy(ye, PS[:, 3, :]).then_inc(ye_ready, 1)

            with act.Fori(0, E) as n:
                expert(n)
            R.emptied(act, "lst")
            extra = act.value_load(ints[0:1, 0:1], min_val=0, max_val=EXTRA)
            with act.If(extra > 0):
                with act.Fori(0, extra) as j:
                    expert(j + E)
            for i in range(2):
                act.wait_ge(y_read, i + 1)
                act.activation(h2k[:, i, :], xk[:, i, :], ACT.Square, accum_out=small[:, 16 + i:17 + i]).then_inc(f_sq, 1)
            act.wait_ge(f_var, 1)
            act.activation(small[:, 18:20], small[:, 16:18], ACT.Sqrt).then_inc(f_std, 1)

        def level_blocks(i, part):
            return pair(f"l{i}{part}").rearrange("p (h r) -> p h r", h=2)[:, :, 0:256].rearrange("p h (i t) -> p h i t", t=P)

        def level_out(dve, i, step, settle):
            for part, h0 in (("a", 0), ("b", 2)):
                R.arrived(dve, f"l{i}{part}")
                R.emptied(dve, f"l{i - 1}{part}")
                settle()
                blocks = att[:, h0:h0 + 2].rearrange("p h a b -> p h (a b)").rearrange("p h (i t) -> p h i t", t=P)
                src = level_blocks(i, part)
                if i == 1:
                    ins = dve.tensor_copy(blocks[:, :, 1:3, :], src)
                else:
                    mask = Cb(C_LEVEL + i - 2).bitcast(I32).unsqueeze(1).unsqueeze(1).to_broadcast([P, 2, 2, P])
                    ins = dve.copy_predicated(blocks[:, :, 0:4:3, :], mask, src)
                R.drained(f"l{i}{part}", ins)

        @block.vector
        def _(dve):
            steps = [0]

            def step(ins):
                ins.then_inc(vec_step, 1)
                steps[0] += 1

            def settle():
                dve.wait_ge(vec_step, steps[0])

            def run(ins):
                step(ins)
                settle()

            R.arrived(dve, "prm")
            step(dve.tensor_copy(pc[:, 0:88], pair("prm")[:, 0:88]))
            R.drained("prm", dve.tensor_copy(pc[:, 88:162], pair("prm")[:, 128:202]))
            B = lambda i, n=1: pc[:, 88 + i:88 + i + n]
            R.emptied(dve, "prm")
            run(dve.tensor_tensor(muc, B(0, 8), B(8, 8), ALU.add))
            step(dve.tensor_scalar(muc, muc, -1.0, 1.0, ALU.mult, ALU.add))
            dve.wait_ge(squares1, 4)
            dve.tensor_scalar(small[:, 4:8], small[:, 0:4], 1.0 / D, EPS, ALU.mult, ALU.add).then_inc(var1, 1)
            dve.wait_ge(std1, 1)
            run(dve.reciprocal(small[:, 12:16], small[:, 8:12]))
            dve.wait_ge(ident_in, 16)
            for i in range(4):
                dve.tensor_scalar(diagR[:, i, :], Cb(C_ID), small[:, 12 + i:13 + i], None, ALU.mult).then_inc(diag_ready, 1)
            def modulation(i):
                R.arrived(dve, f"ada{i}")
                if i:
                    R.arrived(dve, f"mt{i - 1}")
                R.drained(f"ada{i}", dve.tensor_copy(modrow, pair(f"ada{i}", 512)))
                R.arrived(dve, f"mt{i}")
                R.drained(f"mt{i}", dve.tensor_tensor(
                    mod[:, 16 * i:16 * i + 16, :].rearrange("p (j c) s -> p j c s", j=4),
                    pair(f"mt{i}", 512).rearrange("p (c j r) -> p j c r", c=4, j=4)[:, :, :, 0:2],
                    pc[:, 16 * i:16 * i + 16].rearrange("p (j c) -> p j c", j=4).unsqueeze(3).to_broadcast([P, 4, 4, 2]), ALU.add))
                R.emptied(dve, f"mt{i}")

            modulation(0)
            dve.scalar_tensor_tensor(out=A1, in0=mod[:, 8:16, :], scalar=1.0,
                                     in1=pc[:, 64:72].unsqueeze(2).to_broadcast([P, 8, 2]),
                                     op0=ALU.add, op1=ALU.mult).then_inc(mod_ready, 1)
            dve.wait_ge(mod_ready, 1)
            for i in range(4):
                R.arrived(dve, f"h{i}")
                k = 2 * i + 1
                step(dve.tensor_scalar(hT[:, k, 0:L], pair(f"h{i}")[:, 512:512 + L], A1[:, k, 1:2], mod[:, k, 1:2],
                                       ALU.mult, ALU.add))
                ins = dve.tensor_scalar(hT[:, k, L:NT], pair(f"h{i}")[:, 512 + L:1024], A1[:, k, 0:1], mod[:, k, 0:1],
                                        ALU.mult, ALU.add)
                R.drained(f"h{i}", ins)
            R.arrived(dve, "dt")
            dve.wait_ge(mats_in, 16 * N_MATS)
            R.drained("dt", dve.tensor_tensor(dtk, pair("dt", 64).rearrange("p (a b) -> p a b", a=4),
                                              dtb.unsqueeze(1).to_broadcast([P, 4, 16]), ALU.add))
            R.emptied(dve, "dt")
            for b in range(2):
                step(dve.tensor_copy(dcol[64 * b:64 * b + 64, :], dall[64 * b:64 * b + 64, b:8:2]))

            def rows_of(ap, n):
                parts = [] if n == L else [ap[:, 0:L].rearrange("p (r w) -> p r w", r=1)]
                return parts + [ap[:, n - L:n].rearrange("p (r w) -> p r w", w=GRID_W)]

            def add_neighbours(dst, src, n, taps, name, last):
                work = []
                for off, wgt in taps:
                    for d_, s_ in zip(rows_of(dst, n), rows_of(src, n)):
                        w = d_.shape[2]
                        lo, hi = max(0, -off), w - max(0, off)
                        work.append((d_[:, :, lo:hi], s_[:, :, lo + off:hi + off], wgt))
                for i, (d_, s_, wgt) in enumerate(work):
                    ins = dve.scalar_tensor_tensor(out=d_, in0=s_, scalar=wgt, in1=d_, op0=ALU.mult, op1=ALU.add)
                    if last and i == len(work) - 1:
                        R.drained(name, ins)
                    else:
                        run(ins)

            conv = {"B": (BT, 4, NT), "C": (CT, 6, L), "xs0": (xsT[:, 0:2, :], 0, NT), "xs1": (xsT[:, 2:4, :], 2, NT)}
            for i, name in enumerate(("B", "C", "xs0", "xs1")):
                dst, tile, n = conv[name]
                dve.wait_ge(conv_init, 2 * i + 2)
                R.arrived(dve, name)
                for j in range(2):
                    taps = [(k - 2, B(28 + 8 * k + tile + j)) for k in (0, 1, 3)]
                    add_neighbours(dst[:, j, :], pair(name)[:, 512 * j:512 * j + n], n, taps, name, j == 1)
            x16 = dtk.rearrange("p a b -> p (a b)")
            dve.scalar_tensor_tensor(out=dtmp[:, 0, :], in0=x16, scalar=-1.0, in1=x16, op0=ALU.mult, op1=ALU.min).then_inc(dt_abs, 1)
            dve.wait_ge(dt_exp, 2)
            y = dtmp[:, 1, :]
            run(dve.tensor_scalar(dtmp[:, 0, :], y, 1.0 / 3, -0.5, ALU.mult, ALU.add))
            run(dve.tensor_tensor(dtmp[:, 0, :], dtmp[:, 0, :], y, ALU.mult))
            run(dve.scalar_tensor_tensor(out=dtmp[:, 0, :], in0=dtmp[:, 0, :], scalar=1.0, in1=y, op0=ALU.add, op1=ALU.mult))
            adt16 = adt.rearrange("p a b -> p (a b)")
            run(dve.tensor_scalar(adt16, y, 0.01, None, ALU.is_lt))
            run(dve.copy_predicated(dtmp[:, 2, :], adt16.bitcast(I32), dtmp[:, 0, :]))
            run(dve.scalar_tensor_tensor(out=x16, in0=x16, scalar=0.0, in1=dtmp[:, 2, :], op0=ALU.max, op1=ALU.add))
            dve.scalar_tensor_tensor(out=adt, in0=dtk, scalar=-1.0, in1=ea.unsqueeze(1).to_broadcast([P, 4, 16]),
                                     op0=ALU.mult, op1=ALU.mult).then_inc(dt_ready, 1)
            modulation(1)
            R.arrived(dve, "lg")
            R.drained("lg", dve.tensor_copy(lgT[0:32, :], pair("lg", 512)[0:32, :]))
            R.arrived(dve, "gz")
            z2 = gz.rearrange("p a b -> p (a b)")
            R.drained("gz", dve.tensor_tensor(gz, pair("gz").rearrange("p (a b) -> p a b", a=4),
                                              gbb.unsqueeze(1).to_broadcast([P, 4, 256]), ALU.add))
            R.emptied(dve, "gz")
            dve.scalar_tensor_tensor(out=gzt, in0=gz, scalar=-1.0, in1=gz, op0=ALU.mult, op1=ALU.min).then_inc(gz_abs, 1)
            shifted = {"rr": ((rT[:, 0, :], P, L), (rT[:, 1, :], P, L)), "rk": ((kT[:, 0, :], P, NT), (kT[:, 1, :], P, NT)),
                       "rv": ((vT[:, 0, :], P, NT), (vT[:, 1, :], P, NT)), "low": ((lowT, 96, NT), (sgT, 64, L))}
            for i, name in enumerate(("rr", "rk", "rv", "low")):
                R.arrived(dve, name)
                for j, (dst, m, n) in enumerate(shifted[name]):
                    c = 2 * i + j
                    src = pair(name)[0:m, 512 * j:512 * j + n]
                    run(dve.tensor_scalar(dst[0:m, :], src, muc[0:m, c:c + 1], None, ALU.mult))
                    add_neighbours(dst[0:m, :], src, n, [(-1, B(c)[0:m, :]), (1, B(8 + c)[0:m, :])], name, j == 1)
                if name == "rr":
                    dve.wait_ge(gz_exp, 2)
                    run(dve.scalar_tensor_tensor(out=gz, in0=gz, scalar=0.0, in1=gzt, op0=ALU.min, op1=ALU.subtract))
                    dve.tensor_scalar(z2, z2, 1.0 / 16, None, ALU.mult).then_inc(g_ready, 1)

            modulation(2)
            step(dve.scalar_tensor_tensor(out=A2, in0=mod[:, 32:40, 0], scalar=1.0, in1=pc[:, 72:80], op0=ALU.add, op1=ALU.mult))

            R.arrived(dve, "cc")
            dve.wait_ge(ctx_w, 1)
            R.drained("cc", dve.tensor_copy(cumc.rearrange("p a b -> p (a b)"), pair("cc", 64)))
            run(dve.tensor_tensor(wct, wct, dtk[:, 0:2, :], ALU.mult))
            R.emptied(dve, "xst0")
            R.emptied(dve, "xst1")
            for tt in range(2):
                for d in range(2):
                    ins = dve.tensor_tensor(xw[:, tt, d, :].rearrange("p (h c) -> p h c", h=8),
                                            xtk[:, tt, :].rearrange("p (h c) -> p h c", h=8),
                                            wct[:, tt, 8 * d:8 * d + 8].unsqueeze(2).to_broadcast([P, 8, 64]), ALU.mult)
                    ins.then_inc(xw_ready, 1)
            R.arrived(dve, "st")
            R.drained("st", dve.tensor_copy(Sst, pair("st").rearrange("p (a b) -> p a b", a=2)))
            R.arrived(dve, "sc")
            sc = pair("sc").rearrange("p (g s t) -> p g s t", g=2, s=2)
            for g in range(2):
                step(dve.tensor_tensor(scF[:, g, 0, :], sc[:, g, 0, 0:P], Cb(C_TI), ALU.mult))
                step(dve.tensor_copy(scF[:, g, 1, :], sc[:, g, 0, P:L]))
                step(dve.tensor_tensor(scF[:, g, 2, :], sc[:, g, 1, P:L], Cb(C_TI), ALU.mult))
                step(dve.tensor_tensor(scB[:, g, 0, :], sc[:, g, 0, 0:P], Cb(C_TIB), ALU.mult))
                step(dve.tensor_copy(scB[:, g, 1, :], sc[:, g, 1, 0:P]))
                ins = dve.tensor_tensor(scB[:, g, 2, :], sc[:, g, 1, P:L], Cb(C_TIB), ALU.mult)
                if g == 0:
                    step(ins)
            R.drained("sc", ins)
            R.emptied(dve, "sc")
            R.emptied(dve, "cc")

            def exponents(h):
                e, dc = eD[:, h % 2, :], pair(f"dc{h}", 512)
                R.partly(dve, f"dc{h}", 1)
                for i, (lo, hi, src, col) in enumerate(((0, 256, dc[:, 0:256], cumc[:, 2, h:h + 1]),
                                                        (256, 384, dc[:, 128:256], cumc[:, 3, h:h + 1]),
                                                        (384, 512, dc[:, 256:384], cumc[:, 2, 8 + h:9 + h]),
                                                        (512, 768, dc[:, 256:512], cumc[:, 3, 8 + h:9 + h]))):
                    ins = dve.tensor_scalar(e[:, lo:hi], src, col, 0.0, ALU.subtract, ALU.min)
                    if i < 3:
                        step(ins)
                R.drained(f"dc{h}", ins)

            def weights(h):
                g = h // 4
                e, w = eD[:, h % 2, :], WD[:, h % 2, :]
                dve.wait_ge(E_ready, h + 1)
                R.emptied(dve, f"dc{h}")
                if h >= 2:
                    R.arrived(dve, f"yp{(h - 2) // 2}")
                step(dve.tensor_tensor(CI[:, h % 2, :].rearrange("p (a b) -> p a b", a=2),
                                       EI[:, h % 2, :].rearrange("p (a b) -> p a b", a=2),
                                       CT[:, g:g + 1, :].to_broadcast([P, 2, L]), ALU.mult))
                sf, sbk = scF[:, g].rearrange("p a b -> p (a b)"), scB[:, g].rearrange("p a b -> p (a b)")
                for i, (lo, hi, src, col) in enumerate(((0, 256, sf[:, 0:256], dtk[:, 2, h:h + 1]),
                                                        (256, 384, sf[:, 256:384], dtk[:, 3, h:h + 1]),
                                                        (384, 512, sbk[:, 0:128], dtk[:, 2, 8 + h:9 + h]),
                                                        (512, 768, sbk[:, 128:384], dtk[:, 3, 8 + h:9 + h]))):
                    ins = dve.scalar_tensor_tensor(out=w[:, lo:hi], in0=e[:, lo:hi], scalar=col, in1=src, op0=ALU.mult, op1=ALU.mult)
                    if i < 3:
                        step(ins)
                ins.then_inc(w_ready, 1)

            def gather_heads(q):
                R.arrived(dve, f"yp{q}")
                R.drained(f"yp{q}", dve.scalar_tensor_tensor(out=cat[:, 4 + q, :], in0=xsT[:, q, L:NT], scalar=dcol[:, q:q + 1],
                                                            in1=pair(f"yp{q}", L), op0=ALU.mult, op1=ALU.add))

            dve.wait_ge(conv_silu, 4)
            exponents(0)
            for h in range(8):
                if h + 1 < 8:
                    if h + 1 >= 2:
                        dve.wait_ge(w_ready, h)
                    exponents(h + 1)
                weights(h)
                if h % 2:
                    gather_heads(h // 2)
                if h < 2:
                    R.arrived(dve, f"rz{h}")
                    ins = dve.tensor_tensor(lw[:, 2 * h:2 * h + 2, :], pair(f"rz{h}").rearrange("p (a b) -> p a b", a=2),
                                            w0b.unsqueeze(1).to_broadcast([P, 2, 512]), ALU.add)
                    R.drained(f"rz{h}", ins)
                if h == 3:
                    for c in range(2):
                        step(dve.tensor_scalar(kk[:, c, :], kT[:, c, :], B(18 + c), None, ALU.mult))
                    settle()
                    dve.tensor_tensor(ktmp[0], kk, kk, ALU.mult).then_inc(kk_sq, 1)
                    run(dve.tensor_copy(ktmp[1], kk))
                if h == 5:
                    dve.wait_ge(rz_sig, 1)
                    dve.tensor_scalar(lw, lw, -DECAY, None, ALU.mult).then_inc(lw_ready, 1)
                if h == 7:
                    R.arrived(dve, "rkn")
                    R.drained("rkn", dve.tensor_scalar(kk.rearrange("p a b -> p (a b)"), pair("rkn"), 1e-12, None, ALU.add))
                if h == 2:
                    R.emptied(dve, "gs")
                    R.emptied(dve, "gk")
                    dve.tensor_tensor(gkw.rearrange("p a (d c) -> p a d c", d=2), gE.rearrange("p a (d c) -> p a d c", d=2),
                                      gkt.unsqueeze(2).to_broadcast([P, 2, 2, P]), ALU.mult).then_inc(gkw_ready, 1)
                if h == 5:
                    R.arrived(dve, "gS")
                    R.drained("gS", dve.tensor_tensor(gSt, pair("gS", 512).rearrange("p (a b) -> p a b", a=2),
                                                      Cb(C_GBLK, 2).unsqueeze(1).to_broadcast([P, 2, 256]), ALU.mult))
                    dve.wait_ge(qi_exp, 1)
                    dve.tensor_tensor(qI, qI, KQ[:, 1:2, :].to_broadcast([P, 2, L]), ALU.mult).then_inc(qi_ready, 1)
            R.emptied(dve, "yp3")
            R.emptied(dve, "yp2")
            R.emptied(dve, "z0")
            R.emptied(dve, "z1")
            run(dve.tensor_tensor(cat[:, 4:8, :], cat[:, 4:8, :], sz, ALU.mult))
            dve.tensor_tensor(ssq, cat[:, 4:8, :], cat[:, 4:8, :], ALU.mult).then_inc(ssq_ready, 1)
            for i in range(8):
                if i == 0:
                    s2 = ssq.rearrange("p a b -> p (a b)")
                    R.arrived(dve, "sn")
                    R.drained("sn", dve.tensor_scalar(s2[:, 0:512], pair("sn", 512), 1.0 / 256, EPS, ALU.mult, ALU.add))
                if i == 1:
                    dve.wait_ge(sn_std, 1)
                    run(dve.reciprocal(s2[:, 0:512], s2[:, 512:1024]))
                if i == 2:
                    for q in range(4):
                        step(dve.scalar_tensor_tensor(out=cat[:, 4 + q, :], in0=cat[:, 4 + q, :], scalar=B(68 + q),
                                                      in1=s2[:, q // 2 * 256:q // 2 * 256 + 256], op0=ALU.mult, op1=ALU.mult))
                    settle()
                if i in (RECIP_AT, RECIP_AT + 1):
                    dve.wait_ge(kk_std, 1)
                    dve.reciprocal(kk[:, i - RECIP_AT, :], kk[:, i - RECIP_AT, :]).then_inc(kk_norm, 1)
                if i == 0:
                    for part, (h0, h1) in (("a", (0, 1)), ("b", (2, 3))):
                        R.arrived(dve, f"l0{part}")
                        blocks = att[:, h0:h0 + 2].rearrange("p h a b -> p h (a b)").rearrange("p h (i t) -> p h i t", t=P)
                        ins = dve.tensor_tensor(blocks[:, :, 0:4:3, :], level_blocks(0, part),
                                                Cb(C_DIAG2).unsqueeze(1).unsqueeze(1).to_broadcast([P, 2, 2, P]), ALU.mult)
                        R.drained(f"l0{part}", ins)
                        R.emptied(dve, f"l0{part}")
                dve.wait_ge(lv_exp, i + 1)
                if i >= 2:
                    R.arrived(dve, f"l{i - 1}b")
                dve.tensor_tensor(lk[:, i % 2, :], lv[:, i % 2, :], KQ.rearrange("p a b -> p (a b)"), ALU.mult)\
                   .then_inc(lk_ready, 1)
                if i >= 1:
                    level_out(dve, i, step, settle)
            level_out(dve, 8, step, settle)
            R.arrived(dve, "go")
            R.drained("go", dve.tensor_copy(gO.rearrange("p a b -> p (a b)"), pair("go", 512)))
            R.emptied(dve, "go")
            dve.tensor_tensor(gsq, gO, gO, ALU.mult).then_inc(gsq_ready, 1)
            R.arrived(dve, "rb")
            R.drained("rb", dve.tensor_tensor(bon, pair("rb", 512).rearrange("p (a b) -> p a b", a=2), vT[:, :, L:NT], ALU.mult))
            R.arrived(dve, "gn")
            R.drained("gn", dve.tensor_scalar(gsq.rearrange("p a b -> p (a b)"), pair("gn", 512), 1.0 / 64, EPS, ALU.mult, ALU.add))
            dve.wait_ge(gn_std, 1)
            run(dve.reciprocal(gsq, gsq))
            for q in range(2):
                step(dve.scalar_tensor_tensor(out=gO[:, q, :], in0=gO[:, q, :], scalar=B(72 + q), in1=gsq[:, q, :], op0=ALU.mult, op1=ALU.mult))
            settle()
            dve.tensor_tensor(cat[:, 0:2, :], gO, gog, ALU.mult).then_inc(gla_done, 1)
            dve.wait_ge(gla_done, 1)

            dve.wait_ge(rw_pre, 1)

            masks = [dict(strict_t=Cb(C_BTX), strict=Cb(C_BTXB), incl=Cb(C_BTI)), dict(strict_t=Cb(C_BTXB), strict=Cb(C_BTX), incl=Cb(C_BTIB))]
            bc4 = lambda m: m.unsqueeze(1).to_broadcast([P, 4, P])
            for tt in range(4):
                cols = slice(tt * P, tt * P + P)
                lat = tt >= 2
                lcols = slice((tt - 2) * P, (tt - 1) * P)
                for d in range(2):
                    R.emptied(dve, f"cu{tt}{d}")
                    if tt:
                        R.arrived(dve, f"BM{tt - 1}{d}")
                        if lat:
                            R.arrived(dve, f"BV{tt - 1}{d}")
                    EP, EM, EX = eb[d][:, 0], eb[d][:, 1], eb[d][:, 2]
                    step(dve.tensor_tensor(al[d][:, :, cols], kk[:, :, cols], EX, ALU.mult))
                    step(dve.scalar_tensor_tensor(out=be[d], in0=ba[:, :, cols], scalar=-1.0, in1=EM, op0=ALU.mult, op1=ALU.mult))
                    if lat:
                        step(dve.tensor_tensor(rho[d][:, :, lcols], rT[:, :, lcols], EP, ALU.mult))
                    at = 63 if d == 0 else 0
                    step(dve.tensor_copy(wc[d][:, :, 2 * tt:2 * tt + 2], EP[:, :, at:at + 65:64]))
                    dve.tensor_tensor(ka[d], kT[:, :, cols], EM, ALU.mult).then_inc(rw_in, 1)
                view = lambda name: pair(name).rearrange("p (o x t) -> p o x t", o=4, x=2)
                for d in range(2):
                    name = f"AA{tt}{d}"
                    R.arrived(dve, name)
                    step(dve.tensor_tensor(XX[d][:, :, 0, :], view(name)[:, :, 0, :], bc4(masks[d]["strict_t"]), ALU.mult))
                    R.drained(name, dve.tensor_tensor(XX[d][:, :, 1, :], view(name)[:, :, 1, :], bc4(masks[d]["strict"]), ALU.mult))
                    settle()
                    step(dve.tensor_tensor(TT[d][:, tt], XX[d][:, :, 0, :], bc4(Cb(C_ID)), ALU.add))
                for d in range(2):
                    name = f"BM{tt}{d}"
                    R.arrived(dve, name)
                    if tt:
                        R.arrived(dve, f"BV{tt - 1}{d}")
                    R.drained(name, dve.tensor_tensor(bm[d], view(name)[:, :, 0, :], bc4(masks[d]["strict_t"]), ALU.mult))
                if lat:
                    for d in range(2):
                        name = f"MM{tt}{d}"
                        R.arrived(dve, name)
                        step(dve.tensor_tensor(mb[d][:, tt - 2], view(name)[:, :, 0, :], bc4(masks[d]["incl"]), ALU.mult))
                        R.drained(name, dve.tensor_tensor(mk[d], view(name)[:, :, 1, :], bc4(masks[d]["incl"]), ALU.mult))
                for d in range(2):
                    name = f"BV{tt}{d}"
                    R.arrived(dve, name)
                    ins = dve.tensor_copy(BVs[d][:, tt, :], pair(name, 256))
                    if lat:
                        step(ins)
                        src = pair(name)[:, 512:768].rearrange("p (a b) -> p a b", a=2)
                        if d == 0:
                            ins = dve.tensor_copy(oT[:, :, lcols], src)
                        else:
                            R.emptied(dve, f"BV{tt}0")
                            ins = dve.tensor_tensor(oT[:, :, lcols], oT[:, :, lcols], src, ALU.add)
                    R.drained(name, ins)
                for j in range(5):
                    for d in range(2):
                        name = f"D{j}{tt}{d}"
                        R.arrived(dve, name)
                        R.drained(name, dve.tensor_copy(XX[d][:, :, 1, :], pair(name)[:, 512:1024].rearrange("p (o t) -> p o t", o=4)))
                    for d in range(2):
                        name = f"T{j}{tt}{d}"
                        R.arrived(dve, name)
                        settle()
                        if j:
                            R.emptied(dve, f"T{j - 1}{tt}{d}")
                        R.drained(name, dve.tensor_tensor(TT[d][:, tt], TT[d][:, tt], pair(name, 512).rearrange("p (o t) -> p o t", o=4), ALU.add))
            R.emptied(dve, "BV30")
            R.emptied(dve, "BV31")
            for i in range(8):
                for d in range(2):
                    ch = i if d == 0 else BWD_ORDER[i]
                    tt, q = ch // 2, ch % 2
                    rows = slice(64 * q, 64 * q + 64)
                    name = f"R1{i}{d}"
                    R.arrived(dve, name)
                    R.drained(name, dve.tensor_tensor(RH[d][rows, :], pair(name, 256)[rows, :], BVs[d][rows, tt, :], ALU.add))
                if i >= 4:
                    for d in range(2):
                        ch = i if d == 0 else BWD_ORDER[i]
                        tcol = slice((ch - 4) * 64, (ch - 3) * 64)
                        name = f"RO{i}{d}"
                        R.arrived(dve, name)
                        if i >= 5:
                            R.emptied(dve, f"RO{i - 1}{1 - d}")
                        src = pair(name, 128).rearrange("p (s t) -> p s t", s=2)
                        R.drained(name, dve.tensor_tensor(oT[:, :, tcol], oT[:, :, tcol], src, ALU.add))
                for d in range(2):
                    ch = i if d == 0 else BWD_ORDER[i]
                    name = f"R3{i}{d}"
                    R.arrived(dve, name)
                    if i:
                        dve.wait_ge(st_ready[d], i)
                    else:
                        dve.wait_ge(zeroed, 2)
                    R.drained(name, dve.tensor_tensor(ST[d], ST[d], pair(name, 256).rearrange("p (s c) -> p s c", s=2), ALU.add))
                    R.emptied(dve, name)
                    dve.wait_ge(wm_ready[d], i + 1)
                    dve.tensor_tensor(ST[d], ST[d], WM[d][:, i % 2], ALU.mult).then_inc(st_ready[d], 1)
            R.arrived(dve, "RU")
            R.emptied(dve, "RO70")
            R.emptied(dve, "RO71")
            R.drained("RU", dve.tensor_tensor(oT, oT, pair("RU", 512).rearrange("p (a b) -> p a b", a=2), ALU.add))
            R.emptied(dve, "RU")
            R.arrived(dve, "rm")
            flat = lambda ap: ap.rearrange("p a b -> p (a b)")
            R.drained("rm", dve.scalar_tensor_tensor(out=flat(oT), in0=pair("rm", 512), scalar=-1.0 / 64, in1=flat(oT), op0=ALU.mult, op1=ALU.add))
            R.emptied(dve, "rm")
            dve.tensor_tensor(osq, flat(oT), flat(oT), ALU.mult).then_inc(osq_ready, 1)
            R.arrived(dve, "rv2")
            R.drained("rv2", dve.tensor_scalar(bon_tmp, pair("rv2", 512), 1.0 / 64, 64e-5, ALU.mult, ALU.add))
            dve.wait_ge(o_std, 1)
            run(dve.reciprocal(bon_tmp, bon_tmp))
            run(dve.tensor_tensor(flat(oT), flat(oT), bon_tmp, ALU.mult))
            for c in range(2):
                step(dve.tensor_scalar(oT[:, c, :], oT[:, c, :], B(24 + c), B(26 + c), ALU.mult, ALU.add))
            settle()
            run(dve.tensor_tensor(oT, oT, bon, ALU.add))
            R.emptied(dve, "rg")
            dve.tensor_tensor(cat[:, 2:4, :], oT, rgt, ALU.mult).then_inc(cat_ready, 1)
            dve.wait_ge(cat_ready, 1)

            for j in range(8):
                step(dve.tensor_scalar(dg[:, j, :], Cb(C_ID), mod[:, 40 + j, 0:1], None, ALU.mult))
                ins = dve.tensor_scalar(dg[:, 8 + j, :], Cb(C_ID), pc[:, 80 + j:81 + j], None, ALU.mult)
                if j < 7:
                    step(ins)
            ins.then_inc(dg_ready, 1)
            for i in range(2):
                R.arrived(dve, f"w{i}")
                for j in range(4):
                    k = 4 * i + j
                    ins = dve.scalar_tensor_tensor(out=xT[:, k, :], in0=pair(f"w{i}")[:, L * j:L * j + L], scalar=mod[:, 16 + k, 0:1],
                                                   in1=xT[:, k, :], op0=ALU.mult, op1=ALU.add)
                    if j < 3:
                        step(ins)
                R.drained(f"w{i}", ins)
            settle()
            R.emptied(dve, "w1")
            R.emptied(dve, "w0")
            dve.tensor_tensor(sq2, flat(xT), flat(xT), ALU.mult).then_inc(x2_sq, 1)
            R.arrived(dve, "n2")
            R.drained("n2", dve.tensor_scalar(r2, pair("n2", L), 1.0 / D, EPS, ALU.mult, ALU.add))
            dve.wait_ge(n2_std, 1)
            run(dve.reciprocal(r2, r2))
            for k in range(KD):
                dve.scalar_tensor_tensor(out=h2T[:, k, :], in0=xT[:, k, :], scalar=A2[:, k:k + 1], in1=r2,
                                         op0=ALU.mult, op1=ALU.mult).then_inc(h2_scaled, 1)

            R.arrived(dve, "rt")
            R.drained("rt", dve.tensor_tensor(lgt, pair("rt", 64).rearrange("p (a b) -> p a b", a=2), rbb.unsqueeze(1).to_broadcast([P, 2, E]), ALU.add))
            R.emptied(dve, "rt")
            for i in range(2):
                step(dve.max(top8[:, i, :], lgt[:, i, :]))
            settle()
            bce = lambda c: c.to_broadcast([P, 2, E])
            dve.tensor_tensor(rt1, lgt, bce(top8[:, :, 0:1]), ALU.subtract).then_inc(rt_max, 1)
            run(dve.tensor_tensor(rt2, lgt, bce(top8[:, :, 3:4]), ALU.is_gt))
            run(dve.tensor_tensor(rt3, lgt, bce(top8[:, :, 3:4]), ALU.is_equal))
            run(dve.tensor_reduce(small[:, 30:32], rt2, mybir.AxisListType.X, ALU.add))
            run(dve.tensor_scalar(small[:, 30:32], small[:, 30:32], -1.0, float(TOPK), ALU.mult, ALU.add))
            run(dve.tensor_copy(rt4, rt3))
            src, dst = rt4, spos
            for sh in (1, 2, 4, 8, 16):
                step(dve.tensor_tensor(dst[:, :, sh:E], src[:, :, sh:E], src[:, :, 0:E - sh], ALU.add))
                run(dve.tensor_copy(dst[:, :, 0:sh], src[:, :, 0:sh]))
                src, dst = dst, src
            run(dve.tensor_tensor(src, src, bce(small[:, 30:32].unsqueeze(2)), ALU.is_le))
            run(dve.tensor_tensor(rt3, rt3, src, ALU.mult))
            dve.tensor_tensor(rt2, rt2, rt3, ALU.add).then_inc(mask_ready, 1)
            dve.wait_ge(mask_ready, 1)
            dve.tensor_copy(msk3.rearrange("p a (r e) -> p a r e", r=3), rt2.unsqueeze(2).to_broadcast([P, 2, 3, E])).then_inc(mask_ready, 1)
            dve.wait_ge(rt_exp, 1)
            run(dve.tensor_tensor(gates, rt1, rt2, ALU.mult))
            run(dve.tensor_reduce(small[:, 34:36], gates, mybir.AxisListType.X, ALU.add))
            run(dve.reciprocal(small[:, 34:36], small[:, 34:36]))
            dve.tensor_tensor(gates, gates, bce(small[:, 34:36].unsqueeze(2)), ALU.mult).then_inc(gates_ready, 1)
            R.arrived(dve, "pos")
            R.drained("pos", dve.scalar_tensor_tensor(out=spos, in0=pair("pos", 64).rearrange("p (a b) -> p a b", a=2), scalar=1.0, in1=rt2, op0=ALU.add, op1=ALU.mult))
            R.emptied(dve, "pos")
            run(dve.tensor_scalar(spos, spos, -1.0, None, ALU.add))
            R.arrived(dve, "gt")
            R.drained("gt", dve.tensor_copy(gT[0:E, :], pair("gt", L)[0:E, :]))
            cd = cand[0:96, :]
            lastc = C[:, C_IOTA, :]
            R.arrived(dve, "cnd")
            R.drained("cnd", dve.tensor_scalar(cd[:, 0:1], pair("cnd", 1)[0:96, :], lastc[0:96, 66:67], None, ALU.is_gt))
            R.arrived(dve, "idx")
            R.drained("idx", dve.tensor_copy(cd[:, 1:2], pair("idx", 1)[0:96, :]))
            R.emptied(dve, "idx")
            dve.tensor_scalar(onehot[0:96, :], lastc[0:96, 0:EXTRA], cd[:, 1:2], cd[:, 0:1], ALU.is_equal, ALU.mult).then_inc(onehot_ready, 1)
            R.arrived(dve, "lst")
            step(dve.tensor_copy(ints[:, 0:1], pair("lst", 1)))
            step(dve.tensor_copy(ints[:, 8:8 + EXTRA], pair("lst", 64)[:, 16:16 + EXTRA]))
            dve.wait_ge(zeroed, 3)
            R.drained("lst", dve.tensor_copy(ibase[:, E:E + EXTRA], pair("lst", 64)[:, 32:32 + EXTRA]))

            def expert(n, e):
                k = 4

                def mark(i, ins, other=None):
                    ins.then_inc(other or moe_vec, 1)
                    if other:
                        dve.wait_ge(other, n + 1)
                    else:
                        dve.wait_ge(moe_vec, n * k + i)

                dve.wait_ge(sw_ready, n + 1)
                for i in range(2):
                    mark(1 + i, dve.tensor_scalar(sel[:, i, :], lastc[:, 0:SLOTS], ibase[:, bass.ds(n, 1)], spos[:, i, bass.ds(e, 1)], ALU.add, ALU.is_equal))
                for i in range(2):
                    ins = dve.tensor_scalar(selw[:, i, :, :], sel[:, i:i + 1, :].to_broadcast([P, 2, SLOTS]), gates[:, i, bass.ds(e, 1)], None, ALU.mult)
                    ins.then_inc(sel_ready, 1)
                mark(3, dve.tensor_copy(this_e[0:E, :], C[0:E, C_ID, bass.ds(e, 1)].to_broadcast([E, SLOTS])), te_ready)
                dve.wait_ge(slot_free[7], n + base[7] + 1)
                mark(4, dve.tensor_scalar(glu, PS[:, 0, :], LIMIT, None, ALU.min), glu_ready)
                mark(3, dve.tensor_scalar(lin, PS[:, 1, :], LIMIT, -LIMIT, ALU.min, ALU.max))
                mark(4, dve.scalar_tensor_tensor(out=lin, in0=lin, scalar=1.0, in1=glu, op0=ALU.add, op1=ALU.mult))
                dve.wait_ge(sig_ready, n + 1)
                dve.tensor_tensor(act_, lin, sgm, ALU.mult).then_inc(act_ready, 1)

            with dve.Fori(0, E) as n:
                expert(n, n)
            extra = dve.value_load(ints[0:1, 0:1], min_val=0, max_val=EXTRA)
            with dve.If(extra > 0):
                with dve.Fori(0, extra) as j:
                    e = dve.value_load(ints[0:1, bass.ds(j + 8, 1)], min_val=0, max_val=E - 1)
                    expert(j + E, e)
            for name in ("m5", "fg", "xk0", "xk1"):
                R.emptied(dve, name)
            for i in range(2):
                dve.wait_ge(scattered, i + 1)
                y = PS[:, 4 + 2 * i:6 + 2 * i, :].rearrange("p a b -> p (a b)")
                run(dve.tensor_tensor(h2T.rearrange("p a b -> p (a b)")[:, 1024 * i:1024 * i + 1024], y, m5r, ALU.mult))
                dve.tensor_tensor(xk[:, i, :], xk[:, i, :], h2T.rearrange("p a b -> p (a b)")[:, 1024 * i:1024 * i + 1024], ALU.add).then_inc(y_read, 1)
            dve.wait_ge(f_sq, 2)
            dve.tensor_scalar(small[:, 16:18], small[:, 16:18], 1.0 / D, EPS, ALU.mult, ALU.add).then_inc(f_var, 1)
            dve.wait_ge(f_std, 1)
            run(dve.reciprocal(small[:, 42:44], small[:, 18:20]))
            for i in range(2):
                dve.scalar_tensor_tensor(out=xk[:, i, :], in0=xk[:, i, :], scalar=small[:, 42 + i:43 + i], in1=fgr, op0=ALU.mult, op1=ALU.mult).then_inc(out_ready, 1)

        @block.tensor
        def _(pe):
            owed = []

            def mm(out, lhsT, rhs, start=True, stop=True, skip=False):
                ins = pe.matmul(out, lhsT, rhs, start=start, stop=stop, skip_group_check=skip)
                return ins

            def pay(ins):
                if owed:
                    ins.then_inc(owed.pop(0), 1)
                return ins

            def stay_busy(name, n):
                for _ in range(n):
                    pe.matmul(pair(name)[:, 0:P], Cb(C_ID), Cb(C_ONE), start=True, stop=True)

            ident = Cb(C_ID)
            pe.wait_ge(ident_in, 16)
            pe.wait_ge(x_in, 32)
            for i in range(2):
                R.claim(pe, f"x{i}")
                for j in range(4):
                    k = 4 * i + j
                    for t in range(2):
                        ins = pe.transpose(pair(f"x{i}")[:, L * j + t * P:L * j + t * P + P], xtok[:, 2 + t, k * P:k * P + P], ident)
                R.filled(f"x{i}", ins)
            pe.wait_ge(rows_in, 16 * N_ROWS)
            pe.transpose(pair("prm")[:, 0:88], prow[0:88, 0, :], ident[0:88, 0:88])
            R.filled("prm", pe.transpose(pair("prm")[:, 128:202], prow[0:74, 1, :], ident[0:74, 0:74]))
            pe.wait_ge(silu_c, 1)

            def modulation(n):
                i = n // 8
                if n % 8 == 0:
                    R.claim(pe, f"ada{i}")
                s, nth = place["ada", n]
                pe.wait_ge(slot_full[s], 16 * nth)
                for j in range(4):
                    ins = mm(pair(f"ada{i}")[32 * j:32 * j + 32, 0:512], csil[:, n % 8, :], slots[s][:, 512 * j:512 * j + 512],
                             start=n % 8 == 0, stop=n % 8 == 7, skip=True)
                    if j < 3:
                        pay(ins)
                if n % 8 < 7:
                    ins.then_inc(slot_free[s], 1)
                else:
                    R.filled(f"ada{i}", ins)
                    owed.append(slot_free[s])

            def modulation_columns(i):
                R.emptied(pe, f"ada{i}")
                R.claim(pe, f"mt{i}")
                for c in range(4):
                    ins = pe.transpose(pair(f"mt{i}")[:, c * P:c * P + P], modrow[:, c * P:c * P + P], ident)
                    if c < 3:
                        pay(ins)
                R.filled(f"mt{i}", ins)

            R.claim(pe, "h0")
            for n in range(8):
                modulation(n)
                if n >= 4:
                    stay_busy("h0", BUSY_ADA)
            modulation_columns(0)
            stay_busy("h0", 2 * BUSY_ADA)
            pe.wait_ge(diag_ready, 4)
            pe.wait_ge(x_in, 32)
            for i in range(4):
                R.claim(pe, f"h{i}")
                for j in range(2):
                    k = 2 * i + j
                    for t in range(4):
                        ins = mm(pair(f"h{i}")[:, 512 * j + t * P:512 * j + t * P + P], xtok[:, t, k * P:k * P + P], diagR[:, t, :])
                        if not (j == 1 and t == 3):
                            pay(ins)
                R.filled(f"h{i}", ins)
            for i in range(4):
                R.emptied(pe, f"h{i}")
            R.claim(pe, "dtp")
            pe.wait_ge(mats_in, 16 * N_MATS)
            for k in range(KD):
                j = k % 4
                w = dtw_and_next[:, 16 * k:16 * k + 32]
                ins = mm(pair("dtp")[32 * j:32 * j + 32, 0:512], w, hT[:, k, :], start=k < 4, stop=k >= 4, skip=True)
            R.filled("dtp", ins)
            pe.wait_ge(consts_in, 16)
            R.emptied(pe, "dtp")
            R.claim(pe, "dt")
            for t in range(4):
                ins = mm(pair("dt")[:, 16 * t:16 * t + 16], dt_quarters[:, t * P:t * P + P], C[:, C_IOTA, 80:96])
            R.filled("dt", ins)
            tiles, n_ada, n_name = dict(PROJ), 8, 0
            for g, (c0, w, names) in enumerate(W_GROUPS):
                s, nth = place["in", g]
                wt = w_in_tile(g)
                pe.wait_ge(slot_full[s], 16 * nth)
                for name in names:
                    R.claim(pe, name)
                    work = tiles[name]
                    for j, (col, m, lat) in enumerate(work):
                        n = L if lat else NT
                        for k in range(KD):
                            ins = mm(pair(name)[0:m, 512 * j:512 * j + n], wt[:, k, col - c0:col - c0 + m], hT[:, k, NT - n:NT],
                                     start=k == 0, stop=k == 7)
                            if not (j == len(work) - 1 and k == 7):
                                pay(ins)
                    R.filled(name, ins)
                    if name == names[-1]:
                        owed.append(slot_free[s])
                    if n_ada == 16 and ADA_AFTER[n_name] == 0:
                        modulation_columns(1)
                    if name == "rr":
                        R.emptied(pe, "lg")
                        R.claim(pe, "gz")
                        for t in range(4):
                            ins = mm(pair("gz")[:, 256 * t:256 * t + 256], lgT[0:32, t * P:t * P + P], gwb[0:32, :])
                        R.filled("gz", ins)
                    for _ in range(ADA_AFTER[n_name]):
                        modulation(n_ada)
                        n_ada += 1
                    n_name += 1

            pe.wait_ge(consts_in, 16)
            pe.wait_ge(conv_silu, 4)
            for i in range(2):
                R.claim(pe, f"xst{i}")
                for t in range(2):
                    for c in range(4):
                        ins = pe.transpose(pair(f"xst{i}")[:, 512 * t + c * P:512 * t + c * P + P],
                                           xsT[:, c, (2 * i + t) * P:(2 * i + t + 1) * P], ident)
                        if not (t and c == 3):
                            pay(ins)
                R.filled(f"xst{i}", ins)
            pe.wait_ge(g_ready, 1)
            R.claim(pe, "gs")
            for t, d, terms in ((0, 0, ((C_TXB, 0), (C_ONE, 1))), (0, 1, ((C_TX, 0),)), (1, 0, ((C_TXB, 1),)), (1, 1, ((C_TX, 1), (C_ONE, 0)))):
                for i, (m, u) in enumerate(terms):
                    ins = mm(pair("gs")[:, 256 * t + P * d:256 * t + P * d + P], Cb(m), gz[:, u, P * d:P * d + P], start=i == 0, stop=i == len(terms) - 1)
            R.filled("gs", ins)
            R.emptied(pe, "gq")
            R.claim(pe, "gk")
            for t in range(2):
                ins = pe.transpose(pair("gk")[:, t * P:t * P + P], gkc[:, t * P:t * P + P], ident)
            R.filled("gk", ins)
            R.emptied(pe, "gv")
            R.claim(pe, "gvt")
            for t in range(4):
                for c in range(2):
                    ins = pe.transpose(pair("gvt")[:, 256 * t + c * P:256 * t + c * P + P], gvT[:, c, t * P:t * P + P], ident)
            R.filled("gvt", ins)
            R.claim(pe, "gc")
            for d, (u1, u2, m1, m2, lo) in enumerate(((2, 3, C_TI, C_TI, P), (3, 2, C_ONE, C_TIB, 0))):
                mm(pair("gc")[:, 256 * d:256 * d + 256], gz[:, u1, P * d:P * d + P], Cb(m1, 2), stop=False)
                ins = mm(pair("gc")[:, 256 * d + lo:256 * d + lo + P], gz[:, u2, P * d:P * d + P], Cb(m2), start=False)
            R.filled("gc", ins)
            modulation_columns(2)
            R.claim(pe, "Bt")
            for t in range(2):
                for g in range(2):
                    ins = pe.transpose(pair("Bt")[:, 256 * t + g * P:256 * t + g * P + P], BT[:, g, t * P:t * P + P], ident)
            R.filled("Bt", ins)
            pe.wait_ge(dt_ready, 1)
            R.claim(pe, "cc")
            F, Bw = slice(0, 8), slice(8, 16)
            sums = [(0, F, ((C_TXB, 0), (C_ONE, 1))), (0, Bw, ((C_TX, 0),)), (1, F, ((C_TXB, 1),)), (1, Bw, ((C_TX, 1), (C_ONE, 0))),
                    (2, F, ((C_TI, 2),)), (2, Bw, ((C_TIB, 2), (C_ONE, 3))), (3, F, ((C_TI, 3), (C_ONE, 2))), (3, Bw, ((C_TIB, 3),))]
            for t, cols, terms in sums:
                for i, (m, u) in enumerate(terms):
                    ins = mm(pair("cc")[:, 16 * t + cols.start:16 * t + cols.stop], Cb(m), adt[:, u, cols], start=i == 0, stop=i == len(terms) - 1)
            R.filled("cc", ins)
            pe.wait_ge(xw_ready, 4)
            R.emptied(pe, "Bt")
            R.claim(pe, "st")
            for d in range(2):
                for g in range(2):
                    for t in range(2):
                        ins = mm(pair("st")[:, 512 * d + 256 * g:512 * d + 256 * g + 256], Btok[:, t, g * P:g * P + P],
                                 xw[:, t, d, 256 * g:256 * g + 256], start=t == 0, stop=t == 1)
            R.filled("st", ins)
            R.claim(pe, "sc")
            for g in range(2):
                for t in range(2):
                    ins = mm(pair("sc")[:, 512 * g + 256 * t:512 * g + 256 * t + 256], BT[:, g, L + t * P:L + t * P + P], CT[:, g, :])
            R.filled("sc", ins)

            def gla_state():
                pe.wait_ge(gkw_ready, 1)
                R.emptied(pe, "gvt")
                R.claim(pe, "gS")
                for d in range(2):
                    for t in range(2):
                        ins = mm(pair("gS")[:, 256 * d:256 * d + 256], gkw[:, t, P * d:P * d + P], gvk[:, t, :], start=t == 0, stop=t == 1)
                R.filled("gS", ins)

            def running_sums(h):
                name = f"dc{h}"
                R.claim(pe, name)
                out = pair(name)
                for d, (u1, u2, m1, m2, lo) in enumerate(((2, 3, C_TI, C_TI, P), (3, 2, C_ONE, C_TIB, 0))):
                    col = 8 * d + h
                    mm(out[:, 256 * d:256 * d + 256], adt[:, u1, col:col + 1].to_broadcast([P, P]), Cb(m1, 2), stop=False)
                    ins = mm(out[:, 256 * d + lo:256 * d + lo + P], adt[:, u2, col:col + 1].to_broadcast([P, P]), Cb(m2), start=False)
                R.filled(name, ins)

            running_sums(0)
            R.emptied(pe, "st")
            running_sums(1)
            for q in range(4):
                for hh in range(2):
                    h = 2 * q + hh
                    if h + 2 < 8:
                        running_sums(h + 2)
                    if h < 2:
                        pe.wait_ge(rw_tanh, 1)
                        R.claim(pe, f"rz{h}")
                        for t in range(2):
                            ins = mm(pair(f"rz{h}")[:, 512 * t:512 * t + 512], lowT[0:64, (2 * h + t) * P:(2 * h + t + 1) * P], W2A[0:64, :])
                        R.filled(f"rz{h}", ins)
                    if h == 2:
                        R.emptied(pe, "low")
                        R.claim(pe, "ra")
                        for c in range(2):
                            ins = mm(pair("ra")[:, 512 * c:512 * c + 512], W2A[64:96, c * P:c * P + P], lowT[64:96, :])
                        R.filled("ra", ins)
                    if h == 4:
                        gla_state()
                    if h == 6:
                        pe.wait_ge(gate_sig, 1)
                        R.claim(pe, "rg")
                        for c in range(2):
                            ins = mm(pair("rg")[:, 256 * c:256 * c + 256], g2w[0:64, c * P:c * P + P], sgT[0:64, :])
                        R.filled("rg", ins)
                        pe.wait_ge(kk_sq, 1)
                        R.claim(pe, "rkn")
                        for c in range(2):
                            ins = mm(pair("rkn")[:, 512 * c:512 * c + 512], Cb(C_HEAD), ktmp[0][:, c, :])
                        R.filled("rkn", ins)
                    pe.wait_ge(w_ready, h + 1)
                    if hh == 0:
                        R.claim(pe, f"yp{q}")
                    out = pair(f"yp{q}")[64 * hh:64 * hh + 64, :]
                    w, ci = WD[:, h % 2, :], CI[:, h % 2, :]
                    x2_, x3_ = xtk[:, 2, 64 * h:64 * h + 64], xtk[:, 3, 64 * h:64 * h + 64]
                    mm(out[:, 0:256], x2_, w[:, 0:256], stop=False, skip=True)
                    mm(out[:, 128:256], x3_, w[:, 256:384], start=False, stop=False, skip=True)
                    mm(out[:, 0:128], x2_, w[:, 384:512], start=False, stop=False, skip=True)
                    mm(out[:, 0:256], x3_, w[:, 512:768], start=False, stop=False, skip=True)
                    mm(out[:, 0:256], Sst[:, 0, 64 * h:64 * h + 64], ci[:, 0:256], start=False, stop=False, skip=True)
                    ins = mm(out[:, 0:256], Sst[:, 1, 64 * h:64 * h + 64], ci[:, 256:512], start=False, skip=True)
                R.filled(f"yp{q}", ins)
            pe.wait_ge(ssq_ready, 1)
            R.claim(pe, "sn")
            for g in range(2):
                for t in range(2):
                    ins = mm(pair("sn")[:, 256 * g:256 * g + 256], Cb(C_ONE), ssq[:, 2 * g + t, :], start=t == 0, stop=t == 1)
            R.filled("sn", ins)

            for i in range(9):
                if i:
                    pe.wait_ge(lk_ready, i)
                src = KQ if i == 0 else lk[:, (i - 1) % 2, :].rearrange("p (x t) -> p x t", x=2)
                for part, h0 in (("a", 0), ("b", 2)):
                    R.claim(pe, f"l{i}{part}")
                    for s in range(2):
                        t = 1 - s if i == 1 else s
                        for hh in range(2):
                            rows = slice(32 * (h0 + hh), 32 * (h0 + hh) + 32)
                            ins = mm(pair(f"l{i}{part}")[:, 512 * hh + s * P:512 * hh + s * P + P], src[rows, 0, s * P:s * P + P], src[rows, 1, t * P:t * P + P])
                    R.filled(f"l{i}{part}", ins)
            pe.wait_ge(rw_pre, 1)
            R.claim(pe, "rb")
            R.filled("rb", mm(pair("rb", 512), Cb(C_HEAD), bon.rearrange("p a b -> p (a b)")))
            R.emptied(pe, "rv")
            R.claim(pe, "rvt")
            for t in range(4):
                for c in range(2):
                    ins = pe.transpose(pair("rvt")[:, 256 * t + c * P:256 * t + c * P + P], vT[:, c, t * P:t * P + P], ident)
            R.filled("rvt", ins)
            pe.wait_ge(qi_ready, 1)
            R.emptied(pe, "gS")
            R.emptied(pe, "l8a")
            R.emptied(pe, "l8b")
            R.claim(pe, "go")
            for q in range(2):
                for p in range(2):
                    h = 2 * q + p
                    for t in range(2):
                        mm(pair("go")[64 * p:64 * p + 64, 256 * q:256 * q + 256], gvk[:, 2 + t, 64 * h:64 * h + 64], att[:, h, t, :],
                           start=t == 0, stop=False, skip=True)
                for d in range(2):
                    ins = mm(pair("go")[:, 256 * q:256 * q + 256], gSt[:, d, P * q:P * q + P], qI[:, d, :], start=False, stop=d == 1, skip=True)
            R.filled("go", ins)
            pe.wait_ge(gsq_ready, 1)
            R.claim(pe, "gn")
            R.filled("gn", mm(pair("gn", 512), Cb(C_HEAD), gsq.rearrange("p a b -> p (a b)")))

            pe.wait_ge(lw_ready, 1)
            for tt in range(4):
                cols, lcols = slice(tt * P, tt * P + P), slice((tt - 2) * P, (tt - 1) * P)
                for d in range(2):
                    R.claim(pe, f"cu{tt}{d}")
                    for c in range(2):
                        ins = mm(pair(f"cu{tt}{d}")[:, 256 * c:256 * c + 256], lw[:, tt, 256 * d + c * P:256 * d + c * P + P],
                                 Cb(C_BTI if d == 0 else C_BTIB, 2))
                    R.filled(f"cu{tt}{d}", ins)
                for d in range(2):
                    R.claim(pe, f"bk{tt}{d}")
                    stay_busy(f"bk{tt}{d}", BUSY_TILE if tt else BUSY_FIRST)
                    pe.wait_ge(rw_in, 2 * tt + d + 1)
                    for x, src in enumerate((be[d], ka[d])):
                        for c in range(2):
                            ins = pe.transpose(pair(f"bk{tt}{d}")[:, 256 * x + c * P:256 * x + c * P + P], src[:, c, :], ident)
                    R.filled(f"bk{tt}{d}", ins)

                def by_heads(name, pairs_):
                    R.claim(pe, name)
                    for x, (st, mv) in enumerate(pairs_):
                        for h in range(4):
                            half, c, o = slice(64 * (h % 2), 64 * (h % 2) + 64), h // 2, o_of(h)
                            ins = mm(pair(name)[:, 256 * o + P * x:256 * o + P * x + P], st[half, c, :], mv[half, c, :])
                    R.filled(name, ins)

                for d in range(2):
                    by_heads(f"AA{tt}{d}", ((be[d], al[d][:, :, cols]), (al[d][:, :, cols], be[d])))
                for d in range(2):
                    by_heads(f"BM{tt}{d}", ((ka[d], al[d][:, :, cols]),))
                if tt >= 2:
                    for d in range(2):
                        by_heads(f"MM{tt}{d}", ((be[d], rho[d][:, :, lcols]), (ka[d], rho[d][:, :, lcols])))
                R.emptied(pe, "rvt")
                for d in range(2):
                    R.emptied(pe, f"BM{tt}{d}")
                    if tt >= 2:
                        R.emptied(pe, f"MM{tt}{d}")
                    name = f"BV{tt}{d}"
                    R.claim(pe, name)
                    for h in range(4):
                        o = o_of(h)
                        ins = mm(pair(name)[:, 64 * o:64 * o + 64], bm[d][:, o, :], Vt[:, tt, 64 * h:64 * h + 64])
                    if tt >= 2:
                        for h in range(4):
                            ins = mm(pair(name)[64 * (h % 2):64 * (h % 2) + 64, 512 + P * (h // 2):512 + P * (h // 2) + P],
                                     Vt[:, tt, 64 * h:64 * h + 64], mk[d][:, o_of(h), :])
                    R.filled(name, ins)
                for j in range(5):
                    for d in range(2):
                        name = f"D{j}{tt}{d}"
                        R.emptied(pe, f"AA{tt}{d}" if j == 0 else f"D{j - 1}{tt}{d}")
                        R.claim(pe, name)
                        for o in range(4):
                            XTo, Xo = XX[d][:, o, 0, :], XX[d][:, o, 1, :]
                            ins = mm(pair(name)[:, 512 + P * o:512 + P * o + P], XTo, Xo)
                            if j < 4:
                                ins = mm(pair(name)[:, P * o:P * o + P], Xo, XTo)
                        R.filled(name, ins)
                    for d in range(2):
                        name = f"T{j}{tt}{d}"
                        R.emptied(pe, f"D{j}{tt}{d}")
                        if j:
                            R.emptied(pe, f"T{j - 1}{tt}{d}")
                        R.claim(pe, name)
                        for o in range(4):
                            ins = mm(pair(name)[:, P * o:P * o + P], XX[d][:, o, 1, :], TT[d][:, tt, o, :])
                        R.filled(name, ins)
            pe.wait_ge(zeroed, 2)
            for i in range(8):
                where = [(i // 2, i % 2), (BWD_ORDER[i] // 2, BWD_ORDER[i] % 2)]
                chunk = [2 * tt + q for tt, q in where]
                rows = [slice(64 * q, 64 * q + 64) for _, q in where]

                def by_pair(ap, c):
                    return ap.rearrange("p (b s e) -> p b s e", b=2, s=2)[:, :, c, :]

                for d in range(2):
                    R.claim(pe, f"R1{i}{d}")
                stay_busy(f"R1{i}0", BUSY_STATE)
                for d in range(2):
                    if i:
                        pe.wait_ge(st_ready[d], i)
                for c in range(2):
                    for d in range(2):
                        name = f"R1{i}{d}"
                        ins = mm(by_pair(pair(name, 256)[rows[d], :], c), al[d][:, c, 64 * chunk[d]:64 * chunk[d] + 64], ST[d][:, c, :])
                        if c:
                            R.filled(name, ins)
                for d in range(2):
                    R.claim(pe, f"R2{i}{d}")
                stay_busy(f"R2{i}0", BUSY_SOLVE)
                for d in range(2):
                    R.emptied(pe, f"R1{i}{d}")
                    if i == 0:
                        R.emptied(pe, f"T43{d}")
                for o in range(4):
                    for d in range(2):
                        tt, q = where[d]
                        name = f"R2{i}{d}"
                        ins = mm(pair(name)[rows[d], 64 * o:64 * o + 64], TT[d][rows[d], tt, o, 64 * q:64 * q + 64], RH[d][rows[d], 64 * o:64 * o + 64])
                        if o == 3:
                            R.filled(name, ins)
                if i >= 4:
                    for d in range(2):
                        name = f"RO{i}{d}"
                        R.claim(pe, name)
                        for c in range(2):
                            ins = mm(pair(name)[:, 64 * c:64 * c + 64], ST[d][:, c, :], rho[d][:, c, 64 * (chunk[d] - 4):64 * (chunk[d] - 3)])
                        R.filled(name, ins)
                for d in range(2):
                    R.claim(pe, f"R3{i}{d}")
                    R.emptied(pe, f"R2{i}{d}")
                    if i == 0:
                        R.emptied(pe, f"bk3{d}")
                for c in range(2):
                    for x in range(2):
                        for d in range(2):
                            tt = where[d][0]
                            name = f"R3{i}{d}"
                            mv = by_pair(Us[d][rows[d], tt % 2, :], c) if x else Vt[rows[d], tt, P * c:P * c + P]
                            st = bt[d][rows[d], tt, 256 * (1 - x) + P * c:256 * (1 - x) + P * c + P]
                            ins = mm(pair(name)[:, P * c:P * c + P], st, mv, start=x == 0, stop=x == 1)
                            if c and x:
                                R.filled(name, ins)
            R.claim(pe, "RU")
            for h in range(4):
                p, c, o = h % 2, h // 2, o_of(h)
                for t in range(2):
                    for d in range(2):
                        ins = mm(pair("RU")[64 * p:64 * p + 64, 256 * c + P * t:256 * c + P * t + P], Us[d][:, t, 64 * o:64 * o + 64],
                                 mb[d][:, t, o, :], start=d == 0, stop=d == 1)
            R.filled("RU", ins)
            def project(i, tiles_k):
                for k in tiles_k:
                    s, nth = place["out", k // 2]
                    if i == 0 and k % 2 == 0:
                        pe.wait_ge(slot_full[s], 16 * nth)
                    w = slots[s].rearrange("p (k c) -> p k c", k=2)[:, k % 2, :]
                    for j in range(4):
                        m = 4 * i + j
                        ins = mm(pair(f"w{i}")[:, L * j:L * j + L], w[:, m * P:m * P + P], cat[:, k, :],
                                 start=k == 4 and j % 2 == 0, stop=k == 3, skip=True)
                return ins

            R.claim(pe, "w0")
            project(0, (4, 5, 6))
            R.emptied(pe, "RU")
            R.claim(pe, "rm")
            R.filled("rm", mm(pair("rm", 512), Cb(C_HEAD), oT.rearrange("p a b -> p (a b)")))
            project(0, (7,))
            pe.wait_ge(osq_ready, 1)
            R.claim(pe, "rv2")
            R.filled("rv2", mm(pair("rv2", 512), Cb(C_HEAD), osq))
            project(0, (0, 1))
            R.claim(pe, "w1")
            project(1, (4, 5, 6, 7, 0, 1))
            pe.wait_ge(cat_ready, 1)
            R.filled("w0", project(0, (2, 3)))
            R.filled("w1", project(1, (2, 3)))
            owed.extend(slot_free[2 + n] for n in range(4))
            pe.wait_ge(dg_ready, 1)
            for x, name in enumerate(("m5", "fg")):
                R.claim(pe, name)
                for k in range(KD):
                    ins = mm(pair(name)[:, k * P:k * P + P], Cb(C_ONE), dg[:, 8 * x + k, :])
                    if k < 7:
                        pay(ins)
                R.filled(name, ins)
            pe.wait_ge(x2_sq, 1)
            R.claim(pe, "n2")
            for k in range(KD):
                ins = mm(pair("n2", L), Cb(C_ONE), sq2[:, L * k:L * k + L], start=k == 0, stop=k == 7)
            R.filled("n2", ins)

            def by_token(nm, src):
                for t in range(2):
                    R.claim(pe, f"{nm}{t}")
                    for k in range(KD):
                        ins = pe.transpose(pair(f"{nm}{t}")[:, k * P:k * P + P], src[:, k, t * P:t * P + P], ident)
                    R.filled(f"{nm}{t}", ins)

            by_token("xk", xT)
            R.claim(pe, "rt")
            pe.wait_ge(h2_ready, 1)
            for t in range(2):
                for k in range(KD):
                    ins = mm(pair("rt")[:, E * t:E * t + E], h2T[:, k, t * P:t * P + P], rtw[:, k, :], start=k == 0, stop=k == 7)
            R.filled("rt", ins)
            by_token("hk", h2T)
            R.claim(pe, "pos")
            pe.wait_ge(mask_ready, 1)
            mm(pair("pos")[:, 0:E], Cb(C_TX), rt2[:, 0, :])
            mm(pair("pos")[:, E:2 * E], Cb(C_ONE), rt2[:, 0, :], stop=False)
            R.filled("pos", mm(pair("pos")[:, E:2 * E], Cb(C_TX), rt2[:, 1, :], start=False))
            R.claim(pe, "gt")
            pe.wait_ge(late_in, 32)
            pe.wait_ge(gates_ready, 1)
            for t in range(2):
                ins = pe.transpose(pair("gt")[0:E, t * P:t * P + P], gates[:, t, :], ident)
            R.filled("gt", ins)
            pe.wait_ge(mask_ready, 2)
            R.claim(pe, "cnd")
            for t in range(2):
                ins = mm(pair("cnd")[0:96, 0:1], msk3[:, t, :], C[:, C_ONE, 0:1], start=t == 0, stop=t == 1)
            R.filled("cnd", ins)
            R.claim(pe, "idx")
            R.emptied(pe, "cnd")
            R.filled("idx", mm(pair("idx")[0:96, 0:1], C[0:96, C_TX, 0:96], cand[0:96, 0:1]))
            R.claim(pe, "lst")
            pe.wait_ge(onehot_ready, 1)
            mm(pair("lst")[:, 0:1], C[0:96, C_ONE, :], cand[0:96, 0:1])
            mm(pair("lst")[:, 16:32], C[0:96, C_IOTA, 64:65].to_broadcast([96, P]), onehot[0:96, :])
            R.filled("lst", mm(pair("lst")[:, 32:48], C[0:96, C_IOTA, 65:66].to_broadcast([96, P]), onehot[0:96, :]))

            R.emptied(pe, "gt")
            for name in ("cnd", "idx", "lst", "fg", "m5"):
                R.emptied(pe, name)
            for t in range(2):
                for half in range(2):
                    ins = mm(PS[:, 4 + 2 * t + half, :], gT[0:E, t * P:t * P + P], bdn[0:E, 512 * half:512 * half + 512], stop=False, skip=True)
            ins.then_inc(y_init, 1)
            pe.wait_ge(zeroed, 3)
            for name in ("hk0", "hk1"):
                R.emptied(pe, name)

            def scatter(ts, last=False):
                for t in ts:
                    for half in range(2):
                        rows = slice(64 * half, 64 * half + 64)
                        ins = mm(PS[:, 4 + 2 * t + half, :], SW[rows, t * P:t * P + P], ye[rows, :], start=False, stop=last, skip=True)
                return ins

            def expert(n, last=False, extra_pass=False):
                pe.wait_ge(sel_ready, n * 2 + 2)
                for k in range(KD):
                    for t in range(2):
                        ins = mm(PS[:, 2, SLOTS * k:SLOTS * k + SLOTS], h2k[:, t, k * P:k * P + P], sel[:, t, :], start=t == 0, stop=t == 1)
                ins.then_inc(gathered, 1)
                pe.wait_ge(ye_ready, n + 1)
                pe.wait_ge(sw_ready, n + 1)
                scatter((0,))
                pe.wait_ge(hg_ready, n + 2)
                pe.wait_ge(act_ready, n + 1)
                for k in range(KD):
                    ahead = last and k < SPARE
                    if ahead:
                        pe.wait_ge(spare_full[k], 16)
                    else:
                        pe.wait_ge(slot_full[k], (n + (base[k] + 1 - (extra_pass and k < SPARE))) * 16)
                    w = spare[k] if ahead else slots[k]
                    for x in range(2):
                        for half in range(2):
                            ins = mm(PS[64 * half:64 * half + 64, x, :], hg[:, k, :],
                                     w[:, 1024 * x + 512 * half:1024 * x + 512 * half + 512], start=k == 0, stop=k == 7, skip=True)
                    ins.then_inc(slot_free[k], 1)
                    if k == 3:
                        pe.wait_ge(te_ready, n + 1)
                        for x in range(2):
                            for half in range(2):
                                mm(PS[64 * half:64 * half + 64, x, :], this_e[0:E, :],
                                   bgrow[0:E, 1024 * x + 512 * half:1024 * x + 512 * half + 512], start=False, stop=False, skip=True)
                scatter((1,))
                for t in range(2):
                    ins = pe.transpose(PS[:, 3, t * P:t * P + P], selw[:, t, :, :].rearrange("p a b -> p (a b)"), ident)
                ins.then_inc(selT_done, 1)
                for _ in range(3):
                    pe.matmul(PS[:, 2, 0:P], Cb(C_ID), Cb(C_ONE), start=True, stop=True)
                pe.wait_ge(act_ready, n + 2)
                for c in range(4):
                    ins = pe.transpose(PS[:, 2, c * P:c * P + P], act_[:, c * P:c * P + P], ident)
                ins.then_inc(actT_done, 1)
                pe.wait_ge(actT_ready, n + 1)
                pe.wait_ge(sw_ready, n + 2)
                for s in range(8, 12):
                    pe.wait_ge(slot_full[s], (n + (base[s] + 1)) * 16)
                    w = slots[s].rearrange("p (k c) -> p k c", k=2)
                    for k2 in range(2):
                        k = 2 * (s - 8) + k2
                        for half in range(2):
                            ins = mm(PS[64 * half:64 * half + 64, 3, :], actT[:, k % 4, k // 4, :], w[:, k2, 512 * half:512 * half + 512],
                                     start=k == 0, stop=k == 7)
                    ins.then_inc(slot_free[s], 1)

            with pe.Fori(0, E - 1) as n:
                expert(n)
            expert(E - 1, last=True)
            extra = pe.value_load(ints[0:1, 0:1], min_val=0, max_val=EXTRA)
            with pe.If(extra > 0):
                with pe.Fori(0, extra) as j:
                    expert(j + E, extra_pass=True)
            pe.wait_ge(ye_ready, extra + (E + 1))
            pe.wait_ge(sw_ready, extra + (E + 1))
            for t in range(2):
                scatter((t,), last=True).then_inc(scattered, 1)


_INS = ["x", "c", "ctx", "c_ctx", "w_ada", "b_ada", "norm1_g", "norm2_g", "w_in", "gla_gate_w", "gla_gate_b", "gla_norm_g",
        "rw_mu", "rw_w0", "rw_w2", "rw_a0", "rw_a2", "rw_g2", "rw_kk", "rw_ka", "rw_rk", "rw_lnx_g", "rw_lnx_b",
        "ssd_conv_w", "ssd_conv_b", "ssd_dt_bias", "ssd_a_log", "ssd_d", "ssd_norm_g", "w_out", "router_w", "router_b",
        "moe_w_gu", "moe_b_gu", "moe_w_down", "moe_b_down", "final_norm_g"]


def kernel(**inputs):
    import concourse.bacc as bacc
    from concourse.bass_utils import run_bass_kernel_spmd

    nc = bacc.Bacc("TRN2", target_bir_lowering=False, num_devices=1)
    arrays, aps = {}, {}
    sent = {name: np.ascontiguousarray(inputs[name]) for name in _INS}
    sent["consts"] = constants()
    for name, value in sent.items():
        arrays[f"in_{name}"] = value
        aps[name] = nc.dram_tensor(f"in_{name}", value.shape, mybir.dt.from_np(value.dtype), kind="ExternalInput").ap()
    aps["out"] = nc.dram_tensor("out_0", (1, L, D), F32, kind="ExternalOutput").ap()
    hybrid_block(nc, aps)
    return run_bass_kernel_spmd(nc, [arrays], core_ids=[0]).results[0]["out_0"]
```
